# Optimizing a Trainium2 kernel written in Bass

```python
import jax
import jax.numpy as jnp
from jax import lax
import numpy as np

D_MODEL = 1024
BATCH = 1
SEQ = 2048
DEPTH = 1

CTX_LEN = 256
GRID_W = 64
MIX_WIDTH = D_MODEL
CONV_WIDTH = MIX_WIDTH // 2
RG_WIDTH = MIX_WIDTH - CONV_WIDTH
CONV_K = 31
CONV_PAD = (CONV_K - 1) // 2
RG_CONV_K = 4
RG_PAD_L = RG_CONV_K // 2
RG_PAD_R = RG_CONV_K - 1 - RG_PAD_L
RG_HEADS = 8
RG_HEAD_DIM = RG_WIDTH // RG_HEADS
RG_C = 8.0
FFN_DIM = ((11 * D_MODEL // 4 + 127) // 128) * 128
FFN_CONV_K = 3
N_MOD = 6
LN_EPS = 1e-5
DEEPNORM_ALPHA = (2.0 * DEPTH) ** 0.25
DEEPNORM_BETA = (8.0 * DEPTH) ** -0.25
COL_CONV_GATE = CONV_WIDTH
COL_RG_X = 2 * CONV_WIDTH
COL_RG_GATE = 2 * CONV_WIDTH + RG_WIDTH
IN_COLS = 2 * CONV_WIDTH + 2 * RG_WIDTH

kernel_name = "hybrid_conformer_rglru_dit_trunk"

def _layer_norm(x, g, b):
    xf = x.astype(jnp.float32)
    mu = jnp.mean(xf, axis=-1, keepdims=True)
    var = jnp.mean(jnp.square(xf - mu), axis=-1, keepdims=True)
    y = (xf - mu) * lax.rsqrt(var + LN_EPS) * g.astype(jnp.float32) + b.astype(jnp.float32)
    return y.astype(x.dtype)

def _modulate(h, shift, scale):
    return h * (1.0 + scale) + shift

def _dwconv1d(x, w, b, pad_l, pad_r):
    ch = x.shape[-1]
    y = lax.conv_general_dilated(
        x, w[:, None, :].astype(x.dtype), window_strides=(1,), padding=[(pad_l, pad_r)],
        dimension_numbers=("NWC", "WIO", "NWC"), feature_group_count=ch)
    return y + b.astype(x.dtype)

def _dwconv2d(x, w, b):
    ch = x.shape[-1]
    y = lax.conv_general_dilated(
        x, w[:, :, None, :].astype(x.dtype), window_strides=(1, 1), padding="SAME",
        dimension_numbers=("NHWC", "HWIO", "NHWC"), feature_group_count=ch)
    return y + b.astype(x.dtype)

def _block_diag(x, w, b):
    bsz, t, _ = x.shape
    nh, dh, _ = w.shape
    y = jnp.einsum("bthi,hij->bthj", x.reshape(bsz, t, nh, dh), w)
    return y.reshape(bsz, t, nh * dh) + b

def _linear_scan(a, u, h0, reverse):
    if reverse:
        a, u = jnp.flip(a, axis=1), jnp.flip(u, axis=1)
    if h0 is not None:
        u = u.at[:, 0].add(a[:, 0] * h0)

    def combine(left, right):
        a_l, u_l = left
        a_r, u_r = right
        return a_l * a_r, a_r * u_l + u_r

    _, h = lax.associative_scan(combine, (a, u), axis=1)
    return jnp.flip(h, axis=1) if reverse else h

def _rglru(xc, wa, ba, wx, bx, lam, h0, reverse):
    f32 = jnp.float32
    xf = xc.astype(f32)
    r = jax.nn.sigmoid(_block_diag(xf, wa.astype(f32), ba.astype(f32)))
    i = jax.nn.sigmoid(_block_diag(xf, wx.astype(f32), bx.astype(f32)))
    log_a = -RG_C * r * jax.nn.softplus(-lam.astype(f32))
    a = jnp.exp(log_a)
    u = jnp.sqrt(-jnp.expm1(2.0 * log_a)) * (i * xf)
    return _linear_scan(a, u, h0, reverse)

def _in_proj(h, w_in):
    return jnp.split(h @ w_in, [COL_CONV_GATE, COL_RG_X, COL_RG_GATE], axis=-1)

def _conv_group(cv, cg, conv_w, conv_b, conv_ln_g, conv_ln_b):
    u = cv * jax.nn.sigmoid(cg)
    u = _dwconv1d(u, conv_w, conv_b, CONV_PAD, CONV_PAD)
    return jax.nn.silu(_layer_norm(u, conv_ln_g, conv_ln_b))

def _mixer(h_lat, h_ctx, w_in, conv_w, conv_b, conv_ln_g, conv_ln_b, rg_conv_w, rg_conv_b,
           rg_wa, rg_ba, rg_wx, rg_bx, rg_lambda, w_out, with_ctx_out):
    cv_l, cg_l, rx_l, rg_l = _in_proj(h_lat, w_in)
    if with_ctx_out:
        cv_c, cg_c, rx_c, rg_c = _in_proj(h_ctx, w_in)
    else:
        rx_c = h_ctx @ w_in[:, COL_RG_X:COL_RG_GATE]
    xr_l = _dwconv1d(rx_l, rg_conv_w, rg_conv_b, RG_PAD_L, RG_PAD_R)
    xr_c = _dwconv1d(rx_c, rg_conv_w, rg_conv_b, RG_PAD_L, RG_PAD_R)
    dir_f = (rg_wa[0], rg_ba[0], rg_wx[0], rg_bx[0], rg_lambda[0])
    dir_b = (rg_wa[1], rg_ba[1], rg_wx[1], rg_bx[1], rg_lambda[1])
    hc_f = _rglru(xr_c, *dir_f, None, False)
    hc_b = _rglru(xr_c, *dir_b, None, True)
    hl_f = _rglru(xr_l, *dir_f, hc_f[:, -1], False)
    hl_b = _rglru(xr_l, *dir_b, hc_b[:, 0], True)
    y_rg_l = (hl_f + hl_b).astype(h_lat.dtype) * jax.nn.gelu(rg_l)
    y_cv_l = _conv_group(cv_l, cg_l, conv_w, conv_b, conv_ln_g, conv_ln_b)
    out_lat = jnp.concatenate([y_cv_l, y_rg_l], axis=-1) @ w_out
    if not with_ctx_out:
        return out_lat, None
    y_rg_c = (hc_f + hc_b).astype(h_ctx.dtype) * jax.nn.gelu(rg_c)
    y_cv_c = _conv_group(cv_c, cg_c, conv_w, conv_b, conv_ln_g, conv_ln_b)
    out_ctx = jnp.concatenate([y_cv_c, y_rg_c], axis=-1) @ w_out
    return out_lat, out_ctx

def _conv_ffn(h, rows, cols, w_up, dw_w, dw_b, w_down):
    bsz, t, _ = h.shape
    z = h @ w_up
    z = _dwconv2d(z.reshape(bsz, rows, cols, -1), dw_w, dw_b).reshape(bsz, t, -1)
    u, g = jnp.split(z, 2, axis=-1)
    return (u * jax.nn.gelu(g)) @ w_down

def setup_inputs(seed: int = 0) -> dict:
    key = jax.random.key(seed)
    ks = jax.random.split(key, 28)
    f32 = jnp.float32
    L, D, F = DEPTH, D_MODEL, FFN_DIM

    def nrm(k, shape, scale):
        return jax.random.normal(k, shape, f32) * scale

    a8 = jax.random.uniform(ks[17], (L, 2, RG_WIDTH), f32, 0.9, 0.999)
    s = a8 ** (1.0 / RG_C)
    rg_lambda = jnp.log(s) - jnp.log1p(-s)
    return {
        "x": nrm(ks[0], (BATCH, SEQ, D), 1.0),
        "c": nrm(ks[1], (BATCH, D), 1.0),
        "ctx": nrm(ks[2], (BATCH, CTX_LEN, D), 1.0),
        "c_ctx": nrm(ks[3], (D,), 1.0),
        "w_ada": nrm(ks[4], (L, D, N_MOD * D), 0.5 * D ** -0.5),
        "b_ada": nrm(ks[5], (L, N_MOD * D), 0.02),
        "w_in": nrm(ks[6], (L, D, IN_COLS), D ** -0.5),
        "conv_w": nrm(ks[7], (L, CONV_K, CONV_WIDTH), CONV_K ** -0.5),
        "conv_b": nrm(ks[8], (L, CONV_WIDTH), 0.02),
        "conv_ln_g": 1.0 + nrm(ks[9], (L, CONV_WIDTH), 0.02),
        "conv_ln_b": nrm(ks[10], (L, CONV_WIDTH), 0.02),
        "rg_conv_w": nrm(ks[11], (L, RG_CONV_K, RG_WIDTH), RG_CONV_K ** -0.5),
        "rg_conv_b": nrm(ks[12], (L, RG_WIDTH), 0.02),
        "rg_wa": nrm(ks[13], (L, 2, RG_HEADS, RG_HEAD_DIM, RG_HEAD_DIM), RG_HEAD_DIM ** -0.5),
        "rg_ba": nrm(ks[14], (L, 2, RG_WIDTH), 0.02),
        "rg_wx": nrm(ks[15], (L, 2, RG_HEADS, RG_HEAD_DIM, RG_HEAD_DIM), RG_HEAD_DIM ** -0.5),
        "rg_bx": nrm(ks[16], (L, 2, RG_WIDTH), 0.02),
        "rg_lambda": rg_lambda,
        "w_out": nrm(ks[18], (L, MIX_WIDTH, D), DEEPNORM_BETA * MIX_WIDTH ** -0.5),
        "ln1_g": 1.0 + nrm(ks[19], (L, D), 0.02),
        "ln1_b": nrm(ks[20], (L, D), 0.02),
        "ffn_up": nrm(ks[21], (L, D, 2 * F), D ** -0.5),
        "ffn_dw": nrm(ks[22], (L, FFN_CONV_K, FFN_CONV_K, 2 * F), 1.0 / FFN_CONV_K),
        "ffn_dw_b": nrm(ks[23], (L, 2 * F), 0.02),
        "ffn_down": nrm(ks[24], (L, F, D), DEEPNORM_BETA * F ** -0.5),
        "ln2_g": 1.0 + nrm(ks[25], (L, D), 0.02),
        "ln2_b": nrm(ks[26], (L, D), 0.02),
    }

def reference(x, c, ctx, c_ctx, w_ada, b_ada, w_in, conv_w, conv_b, conv_ln_g, conv_ln_b,
              rg_conv_w, rg_conv_b, rg_wa, rg_ba, rg_wx, rg_bx, rg_lambda, w_out,
              ln1_g, ln1_b, ffn_up, ffn_dw, ffn_dw_b, ffn_down, ln2_g, ln2_b):
    rows = x.shape[1] // GRID_W
    silu_c = jax.nn.silu(c)
    silu_cc = jax.nn.silu(c_ctx)[None, :]
    for l in range(DEPTH):
        keep_ctx = l < DEPTH - 1
        sh1, sc1, g1, sh2, sc2, g2 = [m[:, None, :] for m in jnp.split(silu_c @ w_ada[l] + b_ada[l], N_MOD, axis=-1)]
        csh1, csc1, cg1, csh2, csc2, cg2 = [m[:, None, :] for m in jnp.split(silu_cc @ w_ada[l] + b_ada[l], N_MOD, axis=-1)]
        mix_lat, mix_ctx = _mixer(
            _modulate(x, sh1, sc1), _modulate(ctx, csh1, csc1), w_in[l], conv_w[l], conv_b[l],
            conv_ln_g[l], conv_ln_b[l], rg_conv_w[l], rg_conv_b[l], rg_wa[l], rg_ba[l], rg_wx[l],
            rg_bx[l], rg_lambda[l], w_out[l], keep_ctx)
        x = _layer_norm(DEEPNORM_ALPHA * x + g1 * mix_lat, ln1_g[l], ln1_b[l])
        ffn_lat = _conv_ffn(_modulate(x, sh2, sc2), rows, GRID_W, ffn_up[l], ffn_dw[l], ffn_dw_b[l], ffn_down[l])
        x = _layer_norm(DEEPNORM_ALPHA * x + g2 * ffn_lat, ln2_g[l], ln2_b[l])
        if keep_ctx:
            ctx = _layer_norm(DEEPNORM_ALPHA * ctx + cg1 * mix_ctx, ln1_g[l], ln1_b[l])
            ffn_ctx = _conv_ffn(_modulate(ctx, csh2, csc2), 1, ctx.shape[1], ffn_up[l], ffn_dw[l], ffn_dw_b[l], ffn_down[l])
            ctx = _layer_norm(DEEPNORM_ALPHA * ctx + cg2 * ffn_ctx, ln2_g[l], ln2_b[l])
    return x


_drawn_inputs = setup_inputs


def setup_inputs(seed=0):
    import zlib

    import numpy as np

    out = dict(_drawn_inputs(seed))
    spreads = {}
    factors = {'ctx': 7.147,
     'conv_b': 8.0,
     'conv_ln_g': 43.922,
     'conv_ln_b': 38.064,
     'rg_conv_b': 8.514,
     'rg_ba': 64.0,
     'rg_bx': 44.101,
     'ln1_g': 7.598,
     'ln1_b': 7.908,
     'ffn_dw_b': 23.384,
     'ln2_g': 22.794,
     'ln2_b': 22.195,
     'c_ctx': 4.469}
    for name, (base, spread) in spreads.items():
        noise = np.random.default_rng([zlib.crc32(name.encode()), seed]).standard_normal(out[name].shape)
        drawn = base * np.exp(spread * noise) if base else spread * noise
        out[name] = jnp.asarray(drawn.astype(out[name].dtype))
    for name, factor in factors.items():
        out[name] = (out[name] * factor).astype(out[name].dtype)
    return out
```

```python
from contextlib import ExitStack

import concourse.bass as bass
from concourse import mybir

P = 128
D = 1024
T = 2048
TC = 256
GRID_W = 64
ROWS = T // GRID_W
KT = D // P
CH = 512
NC = T // CH
CW = 512
GT = CW // P
F = 2816
NP = F // P
CONV_K = 31
PAD = (CONV_K - 1) // 2
RG_K = 4
RG_L = RG_K // 2
RG_R = RG_K - 1 - RG_L
ALPHA = 2.0 ** 0.25
EPS = 1e-5

F32 = mybir.dt.float32
ALU = mybir.AluOpType
ACT = mybir.ActivationFunctionType

ADA_G = 6
PJ_CONV, PJ_CONVB, PJ_RG, PJ_RGB, PJ_GB, PJ_TH, PJ_EX = 0, 31, 32, 36, 37, 41, 43
PJ_N = 45
TAP_N = 20
COLS = {}
_at = 0
for _name, _n in (("b_ada", ADA_G * KT), ("pj", GT * PJ_N), ("cln_g", GT), ("cln_b", GT), ("ln1_g", KT),
                  ("ln1_b", KT), ("ln2_g", KT), ("ln2_b", KT), ("taps", NP * TAP_N), ("c", KT * 2)):
    COLS[_name] = (_at, _n)
    _at += _n
NPAR = _at

W_HCTX = 0
W_RXP = W_HCTX + KT * TC
RXP = RG_L + TC + RG_R + RG_L + T + RG_R
W_SLOT = W_RXP + RXP
NSLOT = 3
W_XR = W_SLOT + NSLOT * D
W_TR = W_XR + TC + T
W_TI = W_TR + TC + T
W_S = W_TI + TC + T
W_G = W_S + TC + T
W_UP = W_G + T
UP = PAD + T + PAD
W_GW = W_UP + UP
W_N = W_GW + 4 * P
ZR, ZC = ROWS + 2, GRID_W + 2


def hybrid_layer(nc, xT, ctxT, par, w_ada, w_in, w_gate, w_out, w_up, w_down, outT):
    with ExitStack() as cx:
        def sb(name, shape):
            return cx.enter_context(nc.sbuf_tensor(name, shape, F32))

        def sem(name):
            return cx.enter_context(nc.semaphore(name))

        stream = sb("stream", [P, KT, T])
        side = sb("side", [P, KT, T])
        work = sb("work", [P, W_N])
        pars = sb("pars", [P, NPAR])
        silu_c = sb("silu_c", [P, KT, 2])
        mod0 = sb("mod0", [P, 2, KT, 2])
        mods = sb("mods", [P, 4, KT])
        mean_of_group = sb("mean_of_group", [P, P])
        mean_of_model = sb("mean_of_model", [P, P])
        pj_now = sb("pj_now", [P, PJ_N])
        sp = sb("sp", [P, 5, GT, 2])
        g1s = sb("g1s", [P, KT])
        g2s = sb("g2s", [P, KT])
        h2_scale = sb("h2_scale", [P, KT])
        h2_bias = sb("h2_bias", [P, KT])
        eps_now = sb("eps_now", [P, 2])
        tap_u = sb("tap_u", [P, 10])
        tap_g = sb("tap_g", [P, 10])
        ps = cx.enter_context(nc.psum_tensor("ps", [P, 8, CH], F32))

        def par_of(name):
            at, n = COLS[name]
            return pars[:, at:at + n]

        b_ada = par_of("b_ada").rearrange("p (g k) -> p g k", k=KT)
        pj = par_of("pj").rearrange("p (j c) -> p j c", c=PJ_N)
        taps = par_of("taps").rearrange("p (i c) -> p i c", c=TAP_N)
        cvec = par_of("c").rearrange("p (k c) -> p k c", c=2)
        cln_g, cln_b = par_of("cln_g"), par_of("cln_b")
        ln_g = {1: par_of("ln1_g"), 2: par_of("ln2_g")}
        ln_b = {1: par_of("ln1_b"), 2: par_of("ln2_b")}
        streamc = stream[:].rearrange("p k (n f) -> p k n f", f=CH)
        sidec = side[:].rearrange("p k (n f) -> p k n f", f=CH)
        ada_w = side[:].rearrange("p k (t c) -> p (k t) c", c=D)

        def area(at, n):
            return work[:, at:at + n]

        h_ctx = area(W_HCTX, KT * TC).rearrange("p (k t) -> p k t", t=TC)
        slot = [area(W_SLOT + s * D, D) for s in range(NSLOT)]
        gate_w = area(W_GW, 4 * P).rearrange("p (g m) -> p g m", m=P)
        rxp = area(W_RXP, RXP)
        LAT0 = RG_L + TC + RG_R
        rx_ctx = rxp[:, RG_L:RG_L + TC]
        rx_lat = rxp[:, LAT0 + RG_L:LAT0 + RG_L + T]
        xr = area(W_XR, TC + T)
        tr, ti, sq = area(W_TR, TC + T), area(W_TI, TC + T), area(W_S, TC + T)
        gelu_rg = area(W_G, T)
        upad = area(W_UP, UP)
        wo_at = [W_HCTX, W_HCTX + D, W_RXP, W_RXP + D, W_SLOT, W_SLOT + D, W_SLOT + 2 * D, W_XR]
        wo = [area(a, D) for a in wo_at]
        lsq = area(W_TR, KT * CH).rearrange("p (k f) -> p k f", f=CH)
        lsum, lsqs, lr0, lr = (area(W_TR + (KT + i) * CH, CH) for i in range(4))
        csq = area(W_UP, GT * CH).rearrange("p (k f) -> p k f", f=CH)
        cr0, cr = area(W_XR + D, CH), area(W_XR + D + CH, CH)
        fw_u, fw_g, fw_d = area(W_G, D), area(W_G + D, D), area(W_GW - D, D)
        zu = area(0, ZR * ZC).rearrange("p (r c) -> p r c", c=ZC)
        zg = area(ZR * ZC, ZR * ZC).rearrange("p (r c) -> p r c", c=ZC)
        yu = area(2 * ZR * ZC, T)
        act = area(2 * ZR * ZC + T, T)
        yg = area(W_TR + 2 * CH, T)

        par_loaded = sem("par_loaded")
        ctx_loaded = sem("ctx_loaded")
        gatew_loaded = sem("gatew_loaded")
        up_u_loaded = sem("up_u_loaded")
        up_g_loaded = sem("up_g_loaded")
        down_loaded = sem("down_loaded")
        stored = sem("stored")
        consts = sem("consts")
        pads = sem("pads")
        prep_step = sem("prep_step")
        scan_step = sem("scan_step")
        silu_done = sem("silu_done")
        ada_mm = sem("ada_mm")
        mod_done = sem("mod_done")
        prep = sem("prep")
        h_even = sem("h_even")
        h_odd = sem("h_odd")
        hctx_ready = sem("hctx_ready")
        jp_ready = sem("jp_ready")
        cg_mm = sem("cg_mm")
        cv_mm = sem("cv_mm")
        rx_mm = sem("rx_mm")
        rg_mm = sem("rg_mm")
        gate_mm = sem("gate_mm")
        cg_evac = sem("cg_evac")
        cv_evac = sem("cv_evac")
        rx_evac = sem("rx_evac")
        rg_evac = sem("rg_evac")
        gate_evac = sem("gate_evac")
        conv_tap = sem("conv_tap")
        rg_tap = sem("rg_tap")
        rg_act = sem("rg_act")
        unit_step = sem("unit_step")
        unit_done = sem("unit_done")
        mix_step = sem("mix_step")
        cmean_mm = sem("cmean_mm")
        cvar_mm = sem("cvar_mm")
        csub = sem("csub")
        csquare = sem("csquare")
        clog = sem("clog")
        cexp = sem("cexp")
        cnewton = sem("cnewton")
        cnorm = sem("cnorm")
        csilu = sem("csilu")
        out_mm = sem("out_mm")
        out_evac = sem("out_evac")
        psum_step = sem("psum_step")
        mean_mm = sem("mean_mm")
        lsub = sem("lsub")
        lsquare = sem("lsquare")
        qsum_step = sem("qsum_step")
        var_mm = sem("var_mm")
        llog = sem("llog")
        lexp = sem("lexp")
        lnewton = sem("lnewton")
        lnorm = sem("lnorm")
        h2_ready = sem("h2_ready")
        x1_ready = sem("x1_ready")
        zpads = sem("zpads")
        up_u_mm = sem("up_u_mm")
        up_g_mm = sem("up_g_mm")
        down_mm = sem("down_mm")
        zu_evac = sem("zu_evac")
        zg_evac = sem("zg_evac")
        tapu_ready = sem("tapu_ready")
        tapg_ready = sem("tapg_ready")
        first_u = sem("first_u")
        first_g = sem("first_g")
        conv_u = sem("conv_u")
        conv_g = sem("conv_g")
        gelu_done = sem("gelu_done")
        act_done = sem("act_done")
        down_evac = sem("down_evac")
        out_ready = sem("out_ready")
        ada_loaded = [sem(f"ada_loaded{i}") for i in range(4)]
        x_loaded = [sem(f"x_loaded{i}") for i in range(NC)]
        xr_loaded = [sem(f"x_again{i}") for i in range(NC)]
        slot_loaded = [sem(f"slot_loaded{i}") for i in range(NSLOT)]
        wo_loaded = [sem(f"wo_loaded{i}") for i in range(KT)]


        USES = ["cg", "cv", "rx"] + [f"ada{t}" for t in range(KT)] + ["rg"]
        SLOT = {"cg": 0, "cv": 1, "rx": 2, "rg": 2} | {f"ada{t}": t % 3 for t in range(KT)}

        def used(u, j):
            if u[:3] == "ada":
                return ada_mm, 1 + KT * j + int(u[3:]) + 1
            mm, n = {"cg": (cg_mm, NC), "cv": (cv_mm, NC), "rx": (rx_mm, NC + 1), "rg": (rg_mm, NC)}[u]
            return mm, n * (j + 1)

        loads = [[u for u in USES if SLOT[u] == q] for q in range(NSLOT)]
        before = {}
        for q in range(NSLOT):
            for i, u in enumerate(loads[q]):
                before[u] = (loads[q][i - 1], i > 0)
        nth = {u: loads[SLOT[u]].index(u) + 1 for u in USES}
        N_IN = {"cv": 0, "cg": GT, "rx": 2 * GT, "rg": 3 * GT}

        block = cx.enter_context(nc.Block())

        @block.sync
        def _(sp_):
            sp_.dma_start(pars[:], par).then_inc(par_loaded, 16)
            for i in range(4):
                sp_.dma_start(ada_w[:, 4 * i:4 * i + 4, :], w_ada[4 * i:4 * i + 4].rearrange("t p c -> p t c"))\
                   .then_inc(ada_loaded[i], 16)

            def load_slot(u, j, first):
                prev, same = before[u]
                if same:
                    sp_.wait_ge(*used(prev, j))
                elif not first:
                    sp_.wait_ge(*used(prev, j - 1))
                if u[:3] == "ada":
                    src = w_ada[2 * KT + j * KT + int(u[3:])]
                else:
                    src = w_in[N_IN[u] + j]
                sp_.dma_start(slot[SLOT[u]], src).then_inc(slot_loaded[SLOT[u]], 16)

            load_slot("cg", 0, True)
            load_slot("cv", 0, True)
            for n in range(NC):
                sp_.dma_start(streamc[:, :, n, :], xT[:, :, n * CH:(n + 1) * CH].rearrange("k p t -> p k t"))\
                   .then_inc(x_loaded[n], 16)
            sp_.dma_start(h_ctx, ctxT).then_inc(ctx_loaded, 16)

            def mixer_loads(j, first):
                if not first:
                    load_slot("cg", j, first)
                    load_slot("cv", j, first)
                load_slot("rx", j, first)
                if not first:
                    sp_.wait_ge(gate_mm, 20 * j)
                sp_.dma_start(gate_w, w_gate[j]).then_inc(gatew_loaded, 16)
                for t in range(KT):
                    load_slot(f"ada{t}", j, first)
                load_slot("rg", j, first)

            mixer_loads(0, True)
            with sp_.Fori(1, GT) as j:
                mixer_loads(j, False)
            sp_.wait_ge(rx_mm, 5 * GT)
            for m in (0, 1):
                sp_.dma_start(wo[m], w_out[m]).then_inc(wo_loaded[m], 16)
            sp_.wait_ge(rg_tap, 8 * GT)
            for m in (2, 3):
                sp_.dma_start(wo[m], w_out[m]).then_inc(wo_loaded[m], 16)
            sp_.wait_ge(rg_mm, NC * GT)
            for m in (4, 5, 6):
                sp_.dma_start(wo[m], w_out[m]).then_inc(wo_loaded[m], 16)
            for n in range(NC):
                sp_.dma_start(streamc[:, :, n, :], xT[:, :, n * CH:(n + 1) * CH].rearrange("k p t -> p k t"))\
                   .then_inc(xr_loaded[n], 16)
            sp_.wait_ge(unit_done, 2 * GT)
            sp_.dma_start(wo[7], w_out[7]).then_inc(wo_loaded[7], 16)

            sp_.wait_ge(unit_done, 2 * GT)
            sp_.dma_start(fw_u, w_up[0]).then_inc(up_u_loaded, 16)
            sp_.dma_start(fw_g, w_up[NP]).then_inc(up_g_loaded, 16)
            sp_.wait_ge(cvar_mm, NC)
            sp_.dma_start(fw_d, w_down[0]).then_inc(down_loaded, 16)
            with sp_.Fori(1, NP) as i:
                sp_.wait_ge(up_u_mm, NC * i)
                sp_.dma_start(fw_u, w_up[i]).then_inc(up_u_loaded, 16)
                sp_.wait_ge(up_g_mm, NC * i)
                sp_.dma_start(fw_g, w_up[NP + i]).then_inc(up_g_loaded, 16)
                sp_.wait_ge(down_mm, NC * KT * i)
                sp_.dma_start(fw_d, w_down[i]).then_inc(down_loaded, 16)
            for n in range(NC):
                sp_.wait_ge(out_ready, KT * (n + 1))
                sp_.dma_start(outT[:, :, n * CH:(n + 1) * CH].rearrange("k p t -> p k t"), streamc[:, :, n, :])\
                   .then_inc(stored, 16)
            sp_.wait_ge(stored, 16 * NC)

        @block.tensor
        def _(pe):
            pe.wait_ge(silu_done, 1)
            for t in range(2 * KT):
                if t % 4 == 0:
                    pe.wait_ge(ada_loaded[t // 4], 16)
                for k in range(KT):
                    mm = pe.matmul(ps[:, 7, 2 * t:2 * t + 2], ada_w[:, t, k * P:(k + 1) * P], silu_c[:, k, :],
                                   start=(k == 0), stop=(k == KT - 1))
            mm.then_inc(ada_mm, 1)

            def tile(u, j, first, evac, evac_at, done):
                pe.wait_ge(slot_loaded[SLOT[u]], 16 * (len(loads[SLOT[u]]) * j + nth[u]))
                for n in range(NC):
                    if evac is not None:
                        pe.wait_ge(evac, evac_at + n)
                    if u == "cg" and first:
                        pe.wait_ge(h_even, KT // 2 * (n + 1))
                        pe.wait_ge(h_odd, KT // 2 * (n + 1))
                    for k in range(KT):
                        mm = pe.matmul(ps[:, n, :], slot[SLOT[u]][:, k * P:(k + 1) * P], streamc[:, k, n, :],
                                       start=(k == 0), stop=(k == KT - 1))
                    mm.then_inc(done, 1)

            def gates(j, d, first):
                for i in range(10):
                    q = 10 * d + i
                    if not (first and q < 4):
                        pe.wait_ge(gate_evac, 20 * j + q - 3)
                    if q == 3:
                        pe.wait_ge(mod_done, j + 2)
                    at, n = (0, TC) if i % 5 == 0 else (TC + (i % 5 - 1) * CH, CH)
                    pe.matmul(ps[:, 4 + q % 4, 0:n], gate_w[:, 2 * d + i // 5, :], xr[:, at:at + n],
                              start=True, stop=True).then_inc(gate_mm, 1)

            def mixer(j, first):
                tile("cg", j, first, None if first else rg_evac, 4 * j - 3, cg_mm)
                tile("cv", j, first, cg_evac, 4 * j + 1, cv_mm)
                pe.wait_ge(slot_loaded[2], 16 * (len(loads[2]) * j + nth["rx"]))
                if first:
                    pe.wait_ge(hctx_ready, KT)
                else:
                    pe.wait_ge(gate_evac, 20 * j - 3)
                for k in range(KT):
                    mm = pe.matmul(ps[:, 4, 0:TC], slot[2][:, k * P:(k + 1) * P], h_ctx[:, k, :],
                                   start=(k == 0), stop=(k == KT - 1))
                mm.then_inc(rx_mm, 1)
                tile("rx", j, first, cv_evac, 4 * j + 1, rx_mm)
                if not first:
                    pe.wait_ge(gate_evac, 20 * j)
                else:
                    pe.wait_ge(mod_done, 1)
                for t in range(KT):
                    u = f"ada{t}"
                    pe.wait_ge(slot_loaded[SLOT[u]], 16 * (len(loads[SLOT[u]]) * j + nth[u]))
                    for k in range(KT):
                        mm = pe.matmul(ps[:, 7, t:t + 1], slot[SLOT[u]][:, k * P:(k + 1) * P], silu_c[:, k, 0:1],
                                       start=(k == 0), stop=(k == KT - 1))
                    mm.then_inc(ada_mm, 1)
                pe.wait_ge(gatew_loaded, 16 * (j + 1))
                pe.wait_ge(rg_tap, 8 * (j + 1))
                if first:
                    pe.wait_ge(rx_evac, 5)
                gates(j, 0, first)
                tile("rg", j, first, rx_evac, 5 * j + 2, rg_mm)
                gates(j, 1, first)

            mixer(0, True)
            with pe.Fori(1, GT) as j:
                mixer(j, False)

            def conv_stats(n, which):
                src = sidec[:, 0:GT, n, :] if which == 0 else csq
                for c in range(GT):
                    mm = pe.matmul(ps[:, 4 + which, :], mean_of_group[:], src[:, c, :],
                                   start=(c == 0), stop=(c == GT - 1))
                mm.then_inc((cmean_mm, cvar_mm)[which], 1)

            def chunk(n, conv, out, norm, first=False):
                for m in range(KT):
                    if out:
                        if first:
                            pe.wait_ge(wo_loaded[m], 16)
                            if m == 0:
                                pe.wait_ge(unit_done, 2 * GT)
                        if m == 0:
                            pe.wait_ge(csilu, GT * (n + 1))
                        if not (first and m < 4):
                            pe.wait_ge(out_evac, KT * n + m - 3)
                        for k in range(KT):
                            kk = (k + GT) % KT
                            mm = pe.matmul(ps[:, m % 4, :], wo[m][:, kk * P:(kk + 1) * P], sidec[:, kk, n, :],
                                           start=(k == 0), stop=(k == KT - 1))
                        mm.then_inc(out_mm, 1)
                    if m == 0 and conv:
                        if out:
                            pe.wait_ge(csub, GT * (n + 1))
                        conv_stats(n + 1, 0)
                    if m == 1 and norm:
                        pe.wait_ge(psum_step, (KT - 1) * (n))
                        pe.matmul(ps[:, 6, :], mean_of_model[:], lsum, start=True, stop=True).then_inc(mean_mm, 1)
                    if m == 3 and conv:
                        pe.wait_ge(csquare, GT * (n + 2))
                        if out:
                            pe.wait_ge(cnewton, 4 * (n + 1))
                        conv_stats(n + 1, 1)
                    if m == 4 and norm:
                        pe.wait_ge(qsum_step, (KT - 1) * (n))
                        pe.matmul(ps[:, 7, :], mean_of_model[:], lsqs, start=True, stop=True).then_inc(var_mm, 1)

            pe.wait_ge(consts, 2)
            pe.wait_ge(conv_tap, CONV_K * GT)
            pe.wait_ge(gate_evac, 20 * GT)
            chunk(-1, True, False, False)
            pe.wait_ge(rg_evac, NC * GT)
            chunk(0, True, True, False, first=True)
            with pe.Fori(1, NC - 1) as n:
                chunk(n, True, True, True)
            chunk(NC - 1, False, True, True)

            def up(w, i, done, loaded, evac_at, evac, first):
                pe.wait_ge(loaded, 16 * (i + 1))
                for n in range(NC):
                    if first and done is up_u_mm:
                        pe.wait_ge(h2_ready, KT * (n + 1))
                        if n == 0:
                            pe.wait_ge(out_evac, KT * NC)
                    else:
                        pe.wait_ge(evac, evac_at + n)
                    for k in range(KT):
                        mm = pe.matmul(ps[:, n, :], w[:, k * P:(k + 1) * P], sidec[:, k, n, :],
                                       start=(k == 0), stop=(k == KT - 1))
                    mm.then_inc(done, 1)
                    if first and done is up_u_mm and n == 0:
                        pe.wait_ge(psum_step, (KT - 1) * (NC))
                        pe.matmul(ps[:, 6, :], mean_of_model[:], lsum, start=True, stop=True).then_inc(mean_mm, 1)
                    if first and done is up_u_mm and n == 1:
                        pe.wait_ge(qsum_step, (KT - 1) * (NC))
                        pe.matmul(ps[:, 7, :], mean_of_model[:], lsqs, start=True, stop=True).then_inc(var_mm, 1)

            def down(i, n, m, head):
                if not (head and n == 0 and m < 4):
                    pe.wait_ge(down_evac, NC * KT * i + n * KT + m - 3)
                if n == 0 and m == 0:
                    pe.wait_ge(down_loaded, 16 * (i + 1))
                    pe.wait_ge(act_done, i + 1)
                pe.matmul(ps[:, 4 + m % 4, :], fw_d[:, m * P:(m + 1) * P], act[:, n * CH:(n + 1) * CH],
                          start=True, stop=True).then_inc(down_mm, 1)

            def ffn(i, first, head):
                up(fw_u, i, up_u_mm, up_u_loaded, NC * (i - 1) + 1, zg_evac, first)
                up(fw_g, i, up_g_mm, up_g_loaded, NC * i + 1, zu_evac, first)
                if not first:
                    for n in range(NC):
                        for m in range(KT):
                            down(i - 1, n, m, head)

            ffn(0, True, True)
            pe.wait_ge(lnewton, 4 * NC)
            ffn(1, False, True)
            with pe.Fori(2, NP) as i:
                ffn(i, False, False)
            for n in range(NC + 1):
                if n < NC:
                    for m in range(KT):
                        down(NP - 1, n, m, False)
                if n == 1:
                    pe.wait_ge(zg_evac, NC * NP)
                if n > 1:
                    pe.wait_ge(lnewton, 4 * (NC + n - 1))
                if n > 0:
                    pe.wait_ge(psum_step, (KT - 1) * (NC + n))
                    pe.matmul(ps[:, 0, :], mean_of_model[:], lsum, start=True, stop=True).then_inc(mean_mm, 1)
                    pe.wait_ge(qsum_step, (KT - 1) * (NC + n))
                    pe.matmul(ps[:, 1, :], mean_of_model[:], lsqs, start=True, stop=True).then_inc(var_mm, 1)

        @block.scalar
        def _(a):
            a.wait_ge(par_loaded, 16)
            a.activation(silu_c[:], cvec, ACT.Silu).then_inc(silu_done, 1)
            a.wait_ge(prep, 1)
            a.activation(sp[:, 1], sp[:, 0], ACT.Exp, scale=-1.0).then_inc(prep, 1)
            a.wait_ge(mod_done, 1)
            for n in range(NC):
                a.wait_ge(x_loaded[n], 16)
                for k in range(0, KT, 2):
                    a.activation(streamc[:, k, n, :], streamc[:, k, n, :], ACT.Identity, scale=mod0[:, 1, k, 0:1],
                                 bias=mod0[:, 0, k, 0:1]).then_inc(h_even, 1)

            def unit(j, d):
                q = 2 * j + d
                a.wait_ge(gate_evac, 20 * j + 10 * d + 5)
                a.activation(sq, tr, ACT.Tanh, scale=pj_now[:, PJ_TH + d:PJ_TH + d + 1],
                             bias=pj_now[:, PJ_TH + d:PJ_TH + d + 1]).then_inc(rg_act, 1)
                a.wait_ge(rg_act, 3 * q + 1)
                a.activation(tr, tr, ACT.Exp, scale=pj_now[:, PJ_EX + d:PJ_EX + d + 1],
                             bias=pj_now[:, PJ_EX + d:PJ_EX + d + 1]).then_inc(rg_act, 1)
                a.activation(sq, sq, ACT.Sqrt, scale=0.25).then_inc(rg_act, 1)

            def gates(j, d, first):
                if not (first and d == 0):
                    a.wait_ge(unit_done, 2 * j + d)
                for i in range(10):
                    a.wait_ge(gate_mm, 20 * j + 10 * d + i + 1)
                    at, n = (0, TC) if i % 5 == 0 else (TC + (i % 5 - 1) * CH, CH)
                    dst = (tr, ti)[i // 5]
                    g = PJ_GB + 2 * d + i // 5
                    a.activation(dst[:, at:at + n], ps[:, 4 + (10 * d + i) % 4, 0:n], ACT.Tanh, scale=0.5,
                                 bias=pj_now[:, g:g + 1]).then_inc(gate_evac, 1)

            def mixer(j, first):
                for n in range(NC):
                    if not first and n == 0:
                        a.wait_ge(rg_tap, 8 * j)
                    a.wait_ge(cg_mm, 4 * j + n + 1)
                    a.activation(rx_lat[:, n * CH:(n + 1) * CH], ps[:, n, :], ACT.Sigmoid).then_inc(cg_evac, 1)
                a.wait_ge(rx_mm, 5 * j + 1)
                a.activation(rx_ctx, ps[:, 4, 0:TC], ACT.Copy).then_inc(rx_evac, 1)
                for n in range(NC):
                    a.wait_ge(cv_evac, 4 * j + n + 1)
                    a.wait_ge(rx_mm, 5 * j + n + 2)
                    a.activation(rx_lat[:, n * CH:(n + 1) * CH], ps[:, n, :], ACT.Copy).then_inc(rx_evac, 1)
                a.wait_ge(jp_ready, j + 1)
                gates(j, 0, first)
                unit(j, 0)
                for n in range(NC):
                    a.wait_ge(rg_mm, 4 * j + n + 1)
                    a.activation(gelu_rg[:, n * CH:(n + 1) * CH], ps[:, n, :], ACT.Gelu_apprx_tanh)\
                     .then_inc(rg_evac, 1)
                gates(j, 1, first)
                unit(j, 1)

            mixer(0, True)
            with a.Fori(1, GT) as j:
                mixer(j, False)

            def chunk(n, conv, norm, later=True):
                if conv:
                    if n != -1:
                        a.wait_ge(cvar_mm, n + 1)
                    for c in range(GT):
                        a.wait_ge(csub, GT * (n + 1) + c + 1)
                        a.activation(csq[:, c, :], sidec[:, c, n + 1, :], ACT.Square).then_inc(csquare, 1)
                if norm:
                    if later:
                        a.wait_ge(qsum_step, (KT - 1) * (n - 1))
                    for m in range(KT):
                        a.wait_ge(lsub, KT * (n - 1) + m + 1)
                        a.activation(lsq[:, m, :], streamc[:, m, n - 1, :], ACT.Square).then_inc(lsquare, 1)
                if conv:
                    a.wait_ge(cvar_mm, n + 2)
                    a.activation(cr0, ps[:, 5, :], ACT.Ln, bias=eps_now[:, 0:1]).then_inc(clog, 1)
                    a.wait_ge(clog, n + 2)
                    a.activation(cr0, cr0, ACT.Exp, scale=-0.5).then_inc(cexp, 1)
                    for c in range(GT):
                        a.wait_ge(cnorm, GT * (n + 1) + c + 1)
                        a.activation(sidec[:, c, n + 1, :], sidec[:, c, n + 1, :], ACT.Silu, scale=cln_g[:, c:c + 1],
                                     bias=cln_b[:, c:c + 1]).then_inc(csilu, 1)
                if norm:
                    rstd_guess(n, 7)
                    for m in range(KT):
                        a.wait_ge(lnorm, KT * (n - 1) + m + 1)
                        if m == 0:
                            a.wait_ge(out_mm, KT * n)
                        a.activation(sidec[:, m, n - 1, :], streamc[:, m, n - 1, :], ACT.Identity,
                                     scale=h2_scale[:, m:m + 1], bias=h2_bias[:, m:m + 1]).then_inc(h2_ready, 1)
                        a.wait_ge(h2_ready, KT * (n - 1) + m + 1)
                        a.activation(streamc[:, m, n - 1, :], streamc[:, m, n - 1, :], ACT.Identity,
                                     scale=ln_g[1][:, m:m + 1], bias=ln_b[1][:, m:m + 1]).then_inc(x1_ready, 1)

            def rstd_guess(n, bank):
                a.wait_ge(var_mm, n)
                a.activation(lr0, ps[:, bank, :], ACT.Ln, bias=eps_now[:, 1:2]).then_inc(llog, 1)
                a.wait_ge(llog, n)
                a.activation(lr0, lr0, ACT.Exp, scale=-0.5).then_inc(lexp, 1)

            chunk(-1, True, False)
            chunk(0, True, False)
            chunk(1, True, True, later=False)
            with a.Fori(2, NC - 1) as n:
                chunk(n, True, True)
            chunk(NC - 1, False, True)
            chunk(NC, False, True)

            def z_evac(z, bank, mm, i, n, done):
                a.wait_ge(mm, NC * i + n + 1)
                r = CH // GRID_W
                a.activation(z[:, 1 + n * r:1 + (n + 1) * r, 1:1 + GRID_W],
                             ps[:, bank, :].rearrange("p (r c) -> p r c", c=GRID_W), ACT.Copy).then_inc(done, 1)

            def first_tap(y, z, tap, evac, i, done):
                a.wait_ge(evac, NC * (i + 1))
                a.activation(y.rearrange("p (r c) -> p r c", c=GRID_W), z[:, 0:ROWS, 0:GRID_W], ACT.Identity,
                             scale=tap[:, 0:1], bias=tap[:, 9:10]).then_inc(done, 1)

            def gelu(i):
                a.wait_ge(conv_g, 8 * (i + 1))
                a.activation(yg, yg, ACT.Gelu_apprx_tanh).then_inc(gelu_done, 1)

            def ffn(i, first):
                if first:
                    a.wait_ge(zpads, 1)
                else:
                    a.wait_ge(conv_u, 8 * i)
                for n in range(NC):
                    if n == NC - 1 and not first:
                        gelu(i - 1)
                    z_evac(zu, n, up_u_mm, i, n, zu_evac)
                a.wait_ge(tapu_ready, i + 1)
                if not first:
                    a.wait_ge(act_done, i)
                first_tap(yu, zu, tap_u, zu_evac, i, first_u)
                if not first:
                    a.wait_ge(conv_g, 8 * i)
                for n in range(NC):
                    z_evac(zg, n, up_g_mm, i, n, zg_evac)
                a.wait_ge(tapg_ready, i + 1)
                first_tap(yg, zg, tap_g, zg_evac, i, first_g)

            ffn(0, True)
            with a.Fori(1, NP) as i:
                ffn(i, False)
            gelu(NP - 1)

            for n in range(NC):
                a.wait_ge(qsum_step, (KT - 1) * (NC + n))
                for m in range(KT):
                    a.wait_ge(lsub, KT * (NC + n) + m + 1)
                    a.activation(lsq[:, m, :], streamc[:, m, n, :], ACT.Square).then_inc(lsquare, 1)
                rstd_guess(NC + n + 1, 1)
                for m in range(KT):
                    a.wait_ge(lnorm, KT * (NC + n) + m + 1)
                    a.activation(streamc[:, m, n, :], streamc[:, m, n, :], ACT.Identity,
                                 scale=ln_g[2][:, m:m + 1], bias=ln_b[2][:, m:m + 1]).then_inc(out_ready, 1)

        @block.vector
        def _(v):
            v.wait_ge(par_loaded, 16)
            lam = pj[:, :, PJ_TH:PJ_TH + 2]
            v.tensor_scalar(sp[:, 4], lam, -1.0, None, ALU.mult).then_inc(prep_step, 1)
            v.wait_ge(prep_step, 1)
            v.tensor_tensor(sp[:, 0], sp[:, 4], lam, ALU.max).then_inc(prep, 1)
            v.tensor_scalar(pj[:, :, PJ_GB:PJ_GB + 4], pj[:, :, PJ_GB:PJ_GB + 4], 0.5, None, ALU.mult)\
             .then_inc(prep_step, 1)
            v.memset(eps_now[:, 0:1], EPS).then_inc(prep_step, 1)
            v.memset(eps_now[:, 1:2], EPS / (ALPHA * ALPHA)).then_inc(prep_step, 1)
            c = 4

            def link(i):
                nonlocal c
                c += 1
                i.then_inc(prep_step, 1)
                v.wait_ge(prep_step, c)

            v.wait_ge(prep, 2)
            e, r, r2, acc, neg = (sp[:, i] for i in (1, 0, 2, 3, 4))
            link(v.tensor_scalar(r2, e, 2.0, None, ALU.add))
            link(v.reciprocal(acc, r2))
            link(v.tensor_tensor(r, e, acc, ALU.mult))
            link(v.tensor_tensor(r2, r, r, ALU.mult))
            link(v.tensor_scalar(acc, r2, 1.0 / 17, 1.0 / 15, ALU.mult, ALU.add))
            for odd in (13, 11, 9, 7, 5, 3, 1):
                link(v.tensor_tensor(acc, acc, r2, ALU.mult))
                link(v.tensor_scalar(acc, acc, 1.0 / odd, None, ALU.add))
            link(v.tensor_tensor(acc, acc, r, ALU.mult))
            link(v.tensor_scalar(neg, neg, 0.0, 0.5, ALU.max, ALU.mult))
            link(v.tensor_tensor(acc, acc, neg, ALU.add))
            link(v.tensor_scalar(pj[:, :, PJ_EX:PJ_EX + 2], acc, -8.0, None, ALU.mult))
            link(v.tensor_scalar(pj[:, :, PJ_TH:PJ_TH + 2], acc, 4.0, None, ALU.mult))

            v.wait_ge(ada_mm, 1)
            for cc in range(2):
                link(v.tensor_tensor(mod0[:, :, :, cc], ps[:, 7, 0:4 * KT].rearrange("p (g k c) -> p g k c", k=KT, c=2)[:, :, :, cc],
                                     b_ada[:, 0:2, :], ALU.add))
            v.tensor_scalar(mod0[:, 1], mod0[:, 1], 1.0, None, ALU.add).then_inc(mod_done, 1)
            v.wait_ge(mod_done, 1)
            for n in range(NC):
                v.wait_ge(x_loaded[n], 16)
                for k in range(1, KT, 2):
                    v.tensor_scalar(streamc[:, k, n, :], streamc[:, k, n, :], mod0[:, 1, k, 0:1],
                                    mod0[:, 0, k, 0:1], ALU.mult, ALU.add).then_inc(h_odd, 1)
            v.wait_ge(ctx_loaded, 16)
            for k in range(KT):
                v.tensor_scalar(h_ctx[:, k, :], h_ctx[:, k, :], mod0[:, 1, k, 1:2], mod0[:, 0, k, 1:2],
                                ALU.mult, ALU.add).then_inc(hctx_ready, 1)

            def conv_taps(j, lo, hi):
                for k in range(lo, hi):
                    if k == 0:
                        v.wait_ge(jp_ready, j + 1)
                        v.wait_ge(cv_evac, NC * (j + 1))
                        i = v.tensor_scalar(side[:, j, :], upad[:, 0:T], pj_now[:, 0:1],
                                            pj_now[:, PJ_CONVB:PJ_CONVB + 1], ALU.mult, ALU.add)
                    else:
                        v.wait_ge(conv_tap, CONV_K * j + k)
                        i = v.scalar_tensor_tensor(out=side[:, j, :], in0=upad[:, k:k + T], scalar=pj_now[:, k:k + 1],
                                                   in1=side[:, j, :], op0=ALU.mult, op1=ALU.add)
                    i.then_inc(conv_tap, 1)

            def rg_conv(j):
                for k in range(RG_K):
                    w, b = pj_now[:, PJ_RG + k:PJ_RG + k + 1], pj_now[:, PJ_RGB:PJ_RGB + 1]
                    for half, (dst, src) in enumerate(((xr[:, TC:TC + T], rxp[:, LAT0 + k:LAT0 + k + T]),
                                                       (xr[:, 0:TC], rxp[:, k:k + TC]))):
                        if k == 0:
                            i = v.tensor_scalar(dst, src, w, b, ALU.mult, ALU.add)
                        else:
                            v.wait_ge(rg_tap, 8 * j + 2 * (k - 1) + half + 1)
                            i = v.scalar_tensor_tensor(out=dst, in0=src, scalar=w, in1=dst, op0=ALU.mult, op1=ALU.add)
                        i.then_inc(rg_tap, 1)

            def unit(j, d):
                q = 2 * j + d
                v.wait_ge(gate_evac, 20 * j + 10 * d + 10)
                v.scalar_tensor_tensor(out=ti, in0=ti, scalar=1.0, in1=xr, op0=ALU.add, op1=ALU.mult)\
                 .then_inc(unit_step, 1)
                v.wait_ge(rg_act, 3 * (q + 1))
                v.scalar_tensor_tensor(out=sq, in0=tr, scalar=1.0, in1=sq, op0=ALU.add, op1=ALU.mult)\
                 .then_inc(unit_step, 1)
                v.wait_ge(unit_step, 4 * q + 2)
                v.tensor_tensor(sq, sq, ti, ALU.mult).then_inc(unit_step, 1)
                v.wait_ge(unit_step, 4 * q + 3)
                back = slice(None, None, -1)
                if d == 0:
                    v.tensor_tensor_scan(out=ti[:, 0:TC], data0=tr[:, 0:TC], data1=sq[:, 0:TC], initial=0.0,
                                         op0=ALU.mult, op1=ALU.add).then_inc(unit_step, 1)
                    v.wait_ge(unit_step, 4 * q + 4)
                    v.tensor_tensor_scan(out=side[:, GT + j, :], data0=tr[:, TC:], data1=sq[:, TC:],
                                         initial=ti[:, TC - 1:TC], op0=ALU.mult, op1=ALU.add).then_inc(unit_done, 1)
                else:
                    v.tensor_tensor_scan(out=ti[:, 0:TC][:, back], data0=tr[:, 0:TC][:, back],
                                         data1=sq[:, 0:TC][:, back], initial=0.0,
                                         op0=ALU.mult, op1=ALU.add).then_inc(unit_step, 1)
                    v.wait_ge(unit_step, 4 * q + 4)
                    v.tensor_tensor_scan(out=ti[:, TC:][:, back], data0=tr[:, TC:][:, back],
                                         data1=sq[:, TC:][:, back], initial=ti[:, 0:1],
                                         op0=ALU.mult, op1=ALU.add).then_inc(scan_step, 1)
                    v.wait_ge(scan_step, j + 1)
                    v.wait_ge(unit_done, 2 * j + 1)
                    v.tensor_tensor(side[:, GT + j, :], side[:, GT + j, :], ti[:, TC:], ALU.add)\
                     .then_inc(mix_step, 1)
                    v.wait_ge(rg_evac, NC * (j + 1))
                    v.wait_ge(mix_step, j + 1)
                    v.tensor_tensor(side[:, GT + j, :], side[:, GT + j, :], gelu_rg, ALU.mult)\
                     .then_inc(unit_done, 1)

            def mixer(j, first):
                if not first:
                    v.wait_ge(unit_done, 2 * j)
                v.tensor_copy(pj_now[:], pj[:, j, :]).then_inc(jp_ready, 1)
                for n in range(NC):
                    v.wait_ge(cg_evac, NC * j + n + 1)
                    v.wait_ge(cv_mm, NC * j + n + 1)
                    v.tensor_tensor(upad[:, PAD + n * CH:PAD + (n + 1) * CH], ps[:, n, :],
                                    rx_lat[:, n * CH:(n + 1) * CH], ALU.mult).then_inc(cv_evac, 1)
                conv_taps(j, 0, 13)
                v.wait_ge(rx_evac, 5 * (j + 1))
                rg_conv(j)
                v.wait_ge(ada_mm, 1 + KT * (j + 1))
                v.tensor_tensor(mods[:, j, :], ps[:, 7, 0:KT], b_ada[:, 2 + j, :], ALU.add).then_inc(mod_done, 1)
                conv_taps(j, 13, 20)
                unit(j, 0)
                conv_taps(j, 20, CONV_K)
                unit(j, 1)

            v.wait_ge(pads, 5)
            mixer(0, True)
            with v.Fori(1, GT) as j:
                mixer(j, False)

            v.wait_ge(mod_done, GT + 1)
            link(v.tensor_scalar(g1s[:], mods[:, 0, :], 1.0 / ALPHA, None, ALU.mult))
            link(v.tensor_scalar(g2s[:], mods[:, 3, :], 1.0 / ALPHA, None, ALU.mult))
            link(v.tensor_scalar(mods[:, 2, :], mods[:, 2, :], 1.0, None, ALU.add))
            link(v.tensor_tensor(h2_scale[:], ln_g[1], mods[:, 2, :], ALU.mult))
            link(v.tensor_tensor(h2_bias[:], ln_b[1], mods[:, 2, :], ALU.mult))
            link(v.tensor_tensor(h2_bias[:], h2_bias[:], mods[:, 1, :], ALU.add))

            def newton(var, eps, r0, r, done, base, nth_guess, guess):
                v.wait_ge(guess, nth_guess)
                v.scalar_tensor_tensor(out=r, in0=var, scalar=eps, in1=r0, op0=ALU.add, op1=ALU.mult).then_inc(done, 1)
                v.wait_ge(done, base + 1)
                v.tensor_tensor(r, r, r0, ALU.mult).then_inc(done, 1)
                v.wait_ge(done, base + 2)
                v.tensor_scalar(r, r, -0.5, 1.5, ALU.mult, ALU.add).then_inc(done, 1)
                v.wait_ge(done, base + 3)
                v.tensor_tensor(r, r, r0, ALU.mult).then_inc(done, 1)
                v.wait_ge(done, base + 4)

            def ln_sub(q, n, bank):
                v.wait_ge(mean_mm, q + 1)
                for m in range(KT):
                    v.tensor_tensor(streamc[:, m, n, :], streamc[:, m, n, :], ps[:, bank, :], ALU.subtract)\
                     .then_inc(lsub, 1)

            def ln_mul(q, n, bank):
                newton(ps[:, bank, :], eps_now[:, 1:2], lr0, lr, lnewton, 4 * q, q + 1, lexp)
                for m in range(KT):
                    v.tensor_tensor(streamc[:, m, n, :], streamc[:, m, n, :], lr, ALU.mult).then_inc(lnorm, 1)

            def chunk(n, conv, out, norm, first=False):
                for m in range(KT):
                    if out:
                        if m == 0 and first:
                            for i in range(NC):
                                v.wait_ge(xr_loaded[i], 16)
                        v.wait_ge(out_mm, KT * n + m + 1)
                        v.scalar_tensor_tensor(out=streamc[:, m, n, :], in0=ps[:, m % 4, :], scalar=g1s[:, m:m + 1],
                                               in1=streamc[:, m, n, :], op0=ALU.mult, op1=ALU.add)\
                         .then_inc(out_evac, 1)
                    if m == 0 and conv:
                        v.wait_ge(cmean_mm, n + 2)
                        for c_ in range(GT):
                            v.tensor_tensor(sidec[:, c_, n + 1, :], sidec[:, c_, n + 1, :], ps[:, 4, :], ALU.subtract)\
                             .then_inc(csub, 1)
                    if m == 1 and norm:
                        ln_sub(n - 1, n - 1, 6)
                    if m == 3 and conv:
                        newton(ps[:, 5, :], eps_now[:, 0:1], cr0, cr, cnewton, 4 * (n + 1), n + 2, cexp)
                        for c_ in range(GT):
                            v.tensor_tensor(sidec[:, c_, n + 1, :], sidec[:, c_, n + 1, :], cr, ALU.mult)\
                             .then_inc(cnorm, 1)
                    if m == 5 and norm:
                        ln_mul(n - 1, n - 1, 7)

            chunk(-1, True, False, False)
            chunk(0, True, True, False, first=True)
            with v.Fori(1, NC - 1) as n:
                chunk(n, True, True, True)
            chunk(NC - 1, False, True, True)
            chunk(NC, False, False, True)

            def taps3(y, z, tap, i, first_done, done):
                y3 = y.rearrange("p (r c) -> p r c", c=GRID_W)
                v.wait_ge(first_done, i + 1)
                for k in range(1, 9):
                    dr, dc = k // 3, k % 3
                    if k > 1:
                        v.wait_ge(done, 8 * i + k - 1)
                    v.scalar_tensor_tensor(out=y3, in0=z[:, dr:dr + ROWS, dc:dc + GRID_W], scalar=tap[:, k:k + 1],
                                           in1=y3, op0=ALU.mult, op1=ALU.add).then_inc(done, 1)

            def gate(i, first):
                taps3(yg, zg, tap_g, i, first_g, conv_g)
                v.wait_ge(gelu_done, i + 1)
                v.wait_ge(conv_u, 8 * (i + 1))
                if not first:
                    v.wait_ge(down_mm, NC * KT * i)
                v.tensor_tensor(act, yu, yg, ALU.mult).then_inc(act_done, 1)

            def add_down(i, n, head):
                for m in range(KT):
                    if head and m == 0:
                        v.wait_ge(x1_ready, KT * NC)
                    v.wait_ge(down_mm, NC * KT * i + n * KT + m + 1)
                    if not head:
                        v.wait_ge(down_evac, NC * KT * (i - 1) + n * KT + m + 1)
                    v.scalar_tensor_tensor(out=streamc[:, m, n, :], in0=ps[:, 4 + m % 4, :], scalar=g2s[:, m:m + 1],
                                           in1=streamc[:, m, n, :], op0=ALU.mult, op1=ALU.add)\
                     .then_inc(down_evac, 1)

            def ffn(i, first, head):
                if not first:
                    v.wait_ge(conv_u, 8 * i)
                v.tensor_copy(tap_u[:], taps[:, i, 0:10]).then_inc(tapu_ready, 1)
                if not first:
                    gate(i - 1, head)
                v.tensor_copy(tap_g[:], taps[:, i, 10:20]).then_inc(tapg_ready, 1)
                taps3(yu, zu, tap_u, i, first_u, conv_u)
                if not first:
                    for n in range(NC):
                        add_down(i - 1, n, head)

            ffn(0, True, False)
            ffn(1, False, True)
            with v.Fori(2, NP) as i:
                ffn(i, False, False)
            gate(NP - 1, False)
            for n in range(NC):
                add_down(NP - 1, n, False)
                if n > 0:
                    ln_sub(NC + n - 1, n - 1, 0)
                    ln_mul(NC + n - 1, n - 1, 1)
            ln_sub(2 * NC - 1, NC - 1, 0)
            ln_mul(2 * NC - 1, NC - 1, 1)

        @block.gpsimd
        def _(g):
            g.memset(mean_of_group[:], 1.0 / CW).then_inc(consts, 1)
            g.memset(mean_of_model[:], 1.0 / D).then_inc(consts, 1)
            g.memset(upad[:, 0:PAD], 0.0).then_inc(pads, 1)
            g.memset(upad[:, PAD + T:], 0.0).then_inc(pads, 1)
            g.memset(rxp[:, 0:RG_L], 0.0).then_inc(pads, 1)
            g.memset(rxp[:, RG_L + TC:LAT0 + RG_L], 0.0).then_inc(pads, 1)
            g.memset(rxp[:, LAT0 + RG_L + T:], 0.0).then_inc(pads, 1)

            def sums(q, n, src_ready, base, first=False):
                if not first:
                    g.wait_ge(mean_mm, q)
                for m in range(1, KT):
                    g.wait_ge(src_ready, base + KT * n + m + 1)
                    if m > 1:
                        g.wait_ge(psum_step, (KT - 1) * q + m - 1)
                    a = streamc[:, 0, n, :] if m == 1 else lsum
                    i = g.tensor_tensor(lsum, a, streamc[:, m, n, :], ALU.add)
                    i.then_inc(psum_step, 1)
                if not first:
                    g.wait_ge(var_mm, q)
                for m in range(1, KT):
                    g.wait_ge(lsquare, KT * q + m + 1)
                    if m > 1:
                        g.wait_ge(qsum_step, (KT - 1) * q + m - 1)
                    a = lsq[:, 0, :] if m == 1 else lsqs
                    i = g.tensor_tensor(lsqs, a, lsq[:, m, :], ALU.add)
                    i.then_inc(qsum_step, 1)

            g.wait_ge(unit_done, 2 * GT)
            sums(0, 0, out_evac, 0, first=True)
            with g.Fori(1, NC) as n:
                sums(n, n, out_evac, 0)
            g.wait_ge(out_mm, KT * NC)
            for z in (zu, zg):
                g.memset(z[:, 0, :], 0.0)
                g.memset(z[:, ZR - 1, :], 0.0)
                g.memset(z[:, 1:ZR - 1, 0:1], 0.0)
                i = g.memset(z[:, 1:ZR - 1, ZC - 1:ZC], 0.0)
            i.then_inc(zpads, 1)

            for n in range(NC):
                sums(NC + n, n, down_evac, NC * KT * (NP - 1))


def _tiles(w, rows, cols):
    return w.reshape(rows, P, cols, P).transpose(2, 1, 0, 3).reshape(cols, P, rows * P)


def _col(v):
    return v.reshape(-1, P).T


def kernel(x, c, ctx, c_ctx, w_ada, b_ada, w_in, conv_w, conv_b, conv_ln_g, conv_ln_b, rg_conv_w, rg_conv_b,
           rg_wa, rg_ba, rg_wx, rg_bx, rg_lambda, w_out, ln1_g, ln1_b, ffn_up, ffn_dw, ffn_dw_b, ffn_down,
           ln2_g, ln2_b):
    import concourse.bacc as bacc
    import numpy as np
    from concourse.bass_utils import run_bass_kernel_spmd

    A = np.asarray
    x, c, ctx, c_ctx = A(x), A(c), A(ctx), A(c_ctx)
    par = np.zeros((P, NPAR), x.dtype)

    def put(name, a):
        at, n = COLS[name]
        par[:, at:at + n] = np.ascontiguousarray(a).reshape(P, n)

    put("b_ada", _col(A(b_ada)[0]))
    pj = np.zeros((P, GT, PJ_N), x.dtype)
    pj[:, :, PJ_CONV:PJ_CONVB] = A(conv_w)[0].reshape(CONV_K, GT, P).transpose(2, 1, 0)
    pj[:, :, PJ_CONVB] = _col(A(conv_b)[0])
    pj[:, :, PJ_RG:PJ_RGB] = A(rg_conv_w)[0].reshape(RG_K, GT, P).transpose(2, 1, 0)
    pj[:, :, PJ_RGB] = _col(A(rg_conv_b)[0])
    for d in range(2):
        pj[:, :, PJ_GB + 2 * d] = _col(A(rg_ba)[0, d])
        pj[:, :, PJ_GB + 2 * d + 1] = _col(A(rg_bx)[0, d])
        pj[:, :, PJ_TH + d] = _col(A(rg_lambda)[0, d])
    put("pj", pj)
    for name, a in (("cln_g", conv_ln_g), ("cln_b", conv_ln_b), ("ln1_g", ln1_g), ("ln1_b", ln1_b),
                    ("ln2_g", ln2_g), ("ln2_b", ln2_b)):
        put(name, _col(A(a)[0]))
    taps = np.zeros((P, NP, 2, 10), x.dtype)
    taps[:, :, :, 0:9] = A(ffn_dw)[0].reshape(9, 2, NP, P).transpose(3, 2, 1, 0)
    taps[:, :, :, 9] = A(ffn_dw_b)[0].reshape(2, NP, P).transpose(2, 1, 0)
    put("taps", taps)
    put("c", np.stack([_col(c[0]), _col(c_ctx)], axis=-1))

    gate = np.zeros((GT, P, 4, P), x.dtype)
    for d in range(2):
        for g, w in enumerate((A(rg_wa), A(rg_wx))):
            w2 = w[0, d].reshape(GT, 2, 64, 64)
            for h in range(2):
                gate[:, 64 * h:64 * h + 64, 2 * d + g, 64 * h:64 * h + 64] = w2[:, h]

    arrays = {
        "xT": x[0].T.reshape(KT, P, T),
        "ctxT": ctx[0].T.reshape(KT, P, TC).transpose(1, 0, 2),
        "par": par,
        "w_ada": _tiles(A(w_ada)[0], KT, ADA_G * KT),
        "w_in": _tiles(A(w_in)[0], KT, 4 * GT),
        "w_gate": gate,
        "w_out": _tiles(A(w_out)[0], KT, KT),
        "w_up": _tiles(A(ffn_up)[0], KT, 2 * NP),
        "w_down": A(ffn_down)[0].reshape(NP, P, D),
    }
    nc = bacc.Bacc("TRN2", target_bir_lowering=False, num_devices=1, dynamic_dma_scratch_size=64)
    feeds, args = {}, []
    for name, a in arrays.items():
        feeds[name] = np.ascontiguousarray(a)
        args.append(nc.dram_tensor(name, a.shape, F32, kind="ExternalInput").ap())
    args.append(nc.dram_tensor("outT", (KT, P, T), F32, kind="ExternalOutput").ap())
    hybrid_layer(nc, *args)
    r = run_bass_kernel_spmd(nc, [feeds], core_ids=[0])
    out = np.asarray(r.results[0]["outT"]).reshape(D, T).T
    return np.ascontiguousarray(out).reshape(1, T, D)
```

```python
from contextlib import ExitStack

import concourse.bass as bass
from concourse import mybir

P = 128
D = 1024
T = 2048
TC = 256
GRID_W = 64
ROWS = T // GRID_W
KT = D // P
CH = 512
NC = T // CH
CW = 512
GT = CW // P
F = 2816
NP = F // P
CONV_K = 31
PAD = (CONV_K - 1) // 2
RG_K = 4
RG_L = RG_K // 2
RG_R = RG_K - 1 - RG_L
ALPHA = 2.0 ** 0.25
EPS = 1e-5

F32 = mybir.dt.float32
F16 = mybir.dt.float16
BF16 = mybir.dt.bfloat16
I32 = mybir.dt.int32
ALU = mybir.AluOpType
ACT = mybir.ActivationFunctionType

ADA_G = 6
PJ_CONV, PJ_CONVB, PJ_RG, PJ_RGB, PJ_GB, PJ_TH, PJ_EX = 0, 31, 32, 36, 37, 41, 43
PJ_N = 45
TAP_N = 20
COLS = {}
_at = 0
for _name, _n in (("b_ada", ADA_G * KT), ("pj", GT * PJ_N), ("cln_g", GT), ("cln_b", GT), ("ln1_g", KT),
                  ("ln1_b", KT), ("ln2_g", KT), ("ln2_b", KT)):
    COLS[_name] = (_at, _n)
    _at += _n
NPAR = _at

W_HCTX = 0
W_RXP = W_HCTX + KT * TC
RXP = RG_L + TC + RG_R + RG_L + T + RG_R
W_SLOT = W_RXP + RXP
NSLOT = 3
TAPS_1, TAPS_2, TAPS_3 = 7, 10, 14
W_XR = W_SLOT + NSLOT * D
W_TR = W_XR + TC + T
W_TI = W_TR + TC + T
W_S = W_TI + TC + T
W_G = W_S + TC + T
W_UP = W_G + T
UP = PAD + T + PAD
W_GW = W_UP + UP
W_LAND = W_GW + 4 * P
W_N = W_LAND + 2 * D
ZR, ZC = ROWS + 2, GRID_W + 2
F_ZU = 0
F_ZG = F_ZU + ZR * ZC
F_YUA = F_ZG + ZR * ZC
F_YUB = F_YUA + T
F_ACTA = F_YUB + T
F_YG = F_ACTA + T
F_ACT16 = F_YG + T
F_UP16 = F_ACT16 + 2 * T
F_DOWN16 = F_UP16 + 2 * D
NI = NP // 2
NG = NC * KT
DB = 3
SCALE_TOP = (200 << 23)
SCALE_TOP_DOUBLE = (199 << 23)
EXPONENT = 0x7F800000
INVERSE = (254 << 23)


def hybrid_layer(nc, xT, ctxT, par, w_ada, w_in, w_gate, w_out, w_up, w_down, ffn_taps, c_rows, outT):
    AFFINE_STEP = 37
    with ExitStack() as cx:
        def sb(name, shape, dtype=F32):
            return cx.enter_context(nc.sbuf_tensor(name, shape, dtype))

        def sem(name):
            return cx.enter_context(nc.semaphore(name))

        stream = sb("stream", [P, KT, T])
        side = sb("side", [P, KT, T])
        work = sb("work", [P, W_N])
        pars = sb("pars", [P, NPAR])
        mod_raw = sb("mod_raw", [P, 2 * KT, 2])
        ada_sum = sb("ada_sum", [P, KT])
        mod0 = sb("mod0", [P, 2, KT, 2])
        mods = sb("mods", [P, 4, KT])
        mean_of_group = sb("mean_of_group", [P, P])
        mean_of_model = sb("mean_of_model", [P, P])
        pj_now = sb("pj_now", [P, PJ_N])
        pj_prev = sb("pj_prev", [P, PJ_N])
        sp = sb("sp", [P, 5, GT, 2])
        g1s = sb("g1s", [P, KT])
        g2s = sb("g2s", [P, KT])
        h2_scale = sb("h2_scale", [P, KT])
        h2_bias = sb("h2_bias", [P, KT])
        eps_now = sb("eps_now", [P, 2])
        g2_now = sb("g2_now", [P, KT])
        tap_now = sb("tap_now", [P, 2, TAP_N])
        w_sumsq = sb("w_sumsq", [P, 2])
        act_sumsq = sb("act_sumsq", [P, 2])
        h2_sumsq = sb("h2_sumsq", [P, 2])
        bound_junk = sb("bound_junk", [P, 2, KT])
        half_bits = sb("half_bits", [P, 1], I32)
        up_scale = sb("up_scale", [P, 1], I32)
        down_scale = sb("down_scale", [P, 1], I32)
        act_scale = sb("act_scale", [P, 1], I32)
        h2_pow = sb("h2_pow", [P, 1], I32)
        up_inv = sb("up_inv", [P, 2], I32)
        down_inv = sb("down_inv", [P, 1], I32)
        act_inv = sb("act_inv", [P, 1], I32)
        h2_inv = sb("h2_inv", [P, 1], I32)
        ps = cx.enter_context(nc.psum_tensor("ps", [P, 8, CH], F32))

        def par_of(name):
            at, n = COLS[name]
            return pars[:, at:at + n]

        b_ada = par_of("b_ada").rearrange("p (g k) -> p g k", k=KT)
        pj = par_of("pj").rearrange("p (j c) -> p j c", c=PJ_N)
        cln_g, cln_b = par_of("cln_g"), par_of("cln_b")
        ln_g = {1: par_of("ln1_g"), 2: par_of("ln2_g")}
        ln_b = {1: par_of("ln1_b"), 2: par_of("ln2_b")}
        streamc = stream[:].rearrange("p k (n f) -> p k n f", f=CH)
        sidec = side[:].rearrange("p k (n f) -> p k n f", f=CH)
        ada_w = side[:].rearrange("p k (t c) -> p (k t) c", c=D)

        def area(at, n):
            return work[:, at:at + n]

        silu_rows = area(W_LAND, 2 * D).rearrange("p (c k) -> p c k", k=D)
        ada_junk = [area(W_TR + i * D, D) for i in range(4)]
        ada_prod = [area(W_TI + TC + T + i * D, D) for i in range(2)]
        h_ctx = area(W_HCTX, KT * TC).rearrange("p (k t) -> p k t", t=TC)
        slot = [area(W_SLOT + s * D, D) for s in range(NSLOT)]
        gate_w = area(W_GW, 4 * P).rearrange("p (g m) -> p g m", m=P)
        rxp = area(W_RXP, RXP)
        LAT0 = RG_L + TC + RG_R
        rx_ctx = rxp[:, RG_L:RG_L + TC]
        rx_lat = rxp[:, LAT0 + RG_L:LAT0 + RG_L + T]
        xr = area(W_XR, TC + T)
        tr, ti, sq = area(W_TR, TC + T), area(W_TI, TC + T), area(W_S, TC + T)
        gelu_rg = area(W_G, T)
        upad = area(W_UP, UP)
        wo_at = [W_HCTX, W_HCTX + D, W_RXP, W_RXP + D, W_SLOT, W_SLOT + D, W_SLOT + 2 * D, W_XR]
        wo = [area(a, D) for a in wo_at]
        lsq = area(W_TR, KT * CH).rearrange("p (k f) -> p k f", f=CH)
        lsum, lsqs, lr0, lr = (area(W_TR + (KT + i) * CH, CH) for i in range(4))
        csq = area(W_UP, GT * CH).rearrange("p (k f) -> p k f", f=CH)
        cr0, cr = area(W_XR + D, CH), area(W_XR + D + CH, CH)
        h2_f32 = [area(W_TR + (KT + 4) * CH, CH), area(W_GW, CH)]
        ln1_scratch = (lsq, lsum, lsqs, lr0, lr)
        side16 = side[:].bitcast(F16).rearrange("p k (n two f) -> p k n two f", two=2, f=CH)

        def pair16(at, n):
            return area(at, 2 * n).bitcast(F16).rearrange("p (q two f) -> p q two f", two=2, f=n)

        zu = area(F_ZU, ZR * ZC).rearrange("p (r c) -> p r c", c=ZC)
        zg = area(F_ZG, ZR * ZC).rearrange("p (r c) -> p r c", c=ZC)
        yu = [area(F_YUA, T), area(F_YUB, T)]
        yg = area(F_YG, T)
        act = [area(F_ACTA, T), yu[1]]
        act16, up16, down16 = pair16(F_ACT16, T), pair16(F_UP16, D), pair16(F_DOWN16, D)
        land = [area(W_LAND, D), area(W_LAND + D, D)]
        lsq2 = area(F_ZU, KT * CH).rearrange("p (k f) -> p k f", f=CH)
        ln2_scratch = (lsq2,) + tuple(area(F_YUA + i * CH, CH) for i in range(4))

        par_loaded = sem("par_loaded")
        ctx_loaded = sem("ctx_loaded")
        gatew_loaded = sem("gatew_loaded")
        stored = sem("stored")
        consts = sem("consts")
        pads = sem("pads")
        prep_step = sem("prep_step")
        scan_step = sem("scan_step")
        rows_loaded = sem("rows_loaded")
        silu_done = sem("silu_done")
        ada_c = sem("ada_c")
        ada_ctx_prod = sem("ada_ctx_prod")
        ada_ctx_sum = sem("ada_ctx_sum")
        ada_prod_done = sem("ada_prod_done")
        ada_sum_done = sem("ada_sum_done")
        ctx_mod_done = sem("ctx_mod_done")
        mod_done = sem("mod_done")
        prep = sem("prep")
        h_even = sem("h_even")
        h_odd = sem("h_odd")
        hctx_ready = sem("hctx_ready")
        jp_ready = sem("jp_ready")
        jp_kept = sem("jp_kept")
        cg_mm = sem("cg_mm")
        cv_mm = sem("cv_mm")
        rx_mm = sem("rx_mm")
        rg_mm = sem("rg_mm")
        gate_mm = sem("gate_mm")
        cg_evac = sem("cg_evac")
        cv_evac = sem("cv_evac")
        rx_evac = sem("rx_evac")
        rg_evac = sem("rg_evac")
        gate_evac = sem("gate_evac")
        conv_tap = sem("conv_tap")
        rg_tap = sem("rg_tap")
        rg_act = sem("rg_act")
        unit_step = sem("unit_step")
        unit_done = sem("unit_done")
        mix_step = sem("mix_step")
        cmean_mm = sem("cmean_mm")
        cvar_mm = sem("cvar_mm")
        csub = sem("csub")
        csquare = sem("csquare")
        clog = sem("clog")
        cexp = sem("cexp")
        cnewton = sem("cnewton")
        cnorm = sem("cnorm")
        csilu = sem("csilu")
        out_mm = sem("out_mm")
        out_evac = sem("out_evac")
        psum_step = sem("psum_step")
        mean_mm = sem("mean_mm")
        lsub = sem("lsub")
        lsquare = sem("lsquare")
        qsum_step = sem("qsum_step")
        var_mm = sem("var_mm")
        llog = sem("llog")
        lexp = sem("lexp")
        lnewton = sem("lnewton")
        lnorm = sem("lnorm")
        h2_ready = sem("h2_ready")
        h2_hi = sem("h2_hi")
        x1_ready = sem("x1_ready")
        zpads = sem("zpads")
        down_mm = sem("down_mm")
        first_u = sem("first_u")
        first_g = sem("first_g")
        conv_u = sem("conv_u")
        conv_g = sem("conv_g")
        gelu_done = sem("gelu_done")
        bound_sq = sem("bound_sq")
        bound_mm = sem("bound_mm")
        h2_scaled = sem("h2_scaled")
        land_u_loaded = sem("land_u_loaded")
        land_g_loaded = sem("land_g_loaded")
        tap_a_loaded = sem("tap_a_loaded")
        tap_b_loaded = sem("tap_b_loaded")
        w_square = sem("w_square")
        w_sum_mm = sem("w_sum_mm")
        up_scale_step = sem("up_scale_step")
        down_scale_step = sem("down_scale_step")
        w_hi = sem("w_hi")
        w_lo = sem("w_lo")
        up_mm = sem("up_mm")
        z_evac = sem("z_evac")
        act_square = sem("act_square")
        act_sum_mm = sem("act_sum_mm")
        act_scale_step = sem("act_scale_step")
        act_hi = sem("act_hi")
        act_lo = sem("act_lo")
        act_a_done = sem("act_a_done")
        act_b_done = sem("act_b_done")
        down_bank_free = sem("down_bank_free")
        h2_lo = sem("h2_lo")
        out_ready = sem("out_ready")
        ada_loaded = [sem(f"ada_loaded{i}") for i in range(4)]
        x_loaded = [sem(f"x_loaded{i}") for i in range(NC)]
        xr_loaded = [sem(f"x_again{i}") for i in range(NC)]
        slot_loaded = [sem(f"slot_loaded{i}") for i in range(NSLOT)]
        wo_loaded = [sem(f"wo_loaded{i}") for i in range(KT)]


        USES = ["cg", "cv", "rx", "rg"] + [f"ada{t}" for t in range(KT)]
        SLOT = {"cg": 0, "cv": 1, "rx": 2, "rg": 0} | {f"ada{t}": 1 + t % 2 for t in range(KT)}

        def used(u, j):
            if u[:3] == "ada":
                return ada_sum_done, KT * j + int(u[3:]) + 1
            mm, n = {"cg": (cg_mm, NC), "cv": (cv_mm, NC), "rx": (rx_mm, NC + 1), "rg": (rg_mm, NC)}[u]
            return mm, n * (j + 1)

        loads = [[u for u in USES if SLOT[u] == q] for q in range(NSLOT)]
        before = {}
        for q in range(NSLOT):
            for i, u in enumerate(loads[q]):
                before[u] = (loads[q][i - 1], i > 0)
        nth = {u: loads[SLOT[u]].index(u) + 1 for u in USES}
        N_IN = {"cv": 0, "cg": GT, "rx": 2 * GT, "rg": 3 * GT}

        block = cx.enter_context(nc.Block())

        @block.sync
        def _(sp_):
            sp_.dma_start(silu_rows, c_rows).then_inc(rows_loaded, 16)
            sp_.dma_start(pars[:], par).then_inc(par_loaded, 16)
            for i in range(4):
                sp_.dma_start(ada_w[:, 4 * i:4 * i + 4, :], w_ada[4 * i:4 * i + 4].rearrange("t p c -> p t c"))\
                   .then_inc(ada_loaded[i], 16)

            def load_slot(u, j, first):
                prev, same = before[u]
                if same:
                    sp_.wait_ge(*used(prev, j))
                elif not first:
                    sp_.wait_ge(*used(prev, j - 1))
                if u[:3] == "ada":
                    src = w_ada[2 * KT + j * KT + int(u[3:])]
                else:
                    src = w_in[N_IN[u] + j]
                sp_.dma_start(slot[SLOT[u]], src).then_inc(slot_loaded[SLOT[u]], 16)

            load_slot("cg", 0, True)
            load_slot("cv", 0, True)
            for n in range(NC):
                sp_.dma_start(streamc[:, :, n, :], xT[:, :, n * CH:(n + 1) * CH].rearrange("k p t -> p k t"))\
                   .then_inc(x_loaded[n], 16)
            sp_.dma_start(h_ctx, ctxT).then_inc(ctx_loaded, 16)

            def mixer_loads(j, first):
                if not first:
                    load_slot("cg", j, first)
                    load_slot("cv", j, first)
                load_slot("rx", j, first)
                if not first:
                    sp_.wait_ge(gate_mm, 20 * j)
                sp_.dma_start(gate_w, w_gate[j]).then_inc(gatew_loaded, 16)
                load_slot("rg", j, first)
                for t in range(KT):
                    load_slot(f"ada{t}", j, first)

            mixer_loads(0, True)
            sp_.dma_start(tap_now[:, 0, :], ffn_taps[0]).then_inc(tap_a_loaded, 16)
            sp_.dma_start(tap_now[:, 1, :], ffn_taps[1]).then_inc(tap_b_loaded, 16)
            with sp_.Fori(1, GT) as j:
                mixer_loads(j, False)
            sp_.wait_ge(rx_mm, 5 * GT)
            for m in (0, 1):
                sp_.dma_start(wo[m], w_out[m]).then_inc(wo_loaded[m], 16)
            sp_.wait_ge(rg_tap, 8 * GT)
            for m in (2, 3):
                sp_.dma_start(wo[m], w_out[m]).then_inc(wo_loaded[m], 16)
            sp_.wait_ge(rg_mm, NC * GT)
            sp_.dma_start(wo[4], w_out[4]).then_inc(wo_loaded[4], 16)
            for n in range(NC):
                sp_.dma_start(streamc[:, :, n, :], xT[:, :, n * CH:(n + 1) * CH].rearrange("k p t -> p k t"))\
                   .then_inc(xr_loaded[n], 16)
            sp_.wait_ge(unit_done, 2 * GT)
            sp_.dma_start(wo[7], w_out[7]).then_inc(wo_loaded[7], 16)
            sp_.wait_ge(ada_sum_done, KT * GT)
            for m in (5, 6):
                sp_.dma_start(wo[m], w_out[m]).then_inc(wo_loaded[m], 16)
            sp_.dma_start(land[0], w_up[0]).then_inc(land_u_loaded, 16)
            sp_.dma_start(land[1], w_up[NP]).then_inc(land_g_loaded, 16)

            def land_pair(src_u, src_g, p):
                for q, (src, done) in enumerate(((src_u, land_u_loaded), (src_g, land_g_loaded))):
                    sp_.wait_ge(w_lo, 2 * (p - 1) + q + 1)
                    sp_.dma_start(land[q], src).then_inc(done, 16)

            def ffn_loads(i, last):
                land_pair(w_up[2 * i + 1], w_up[NP + 2 * i + 1], 3 * i + 1)
                land_pair(w_down[2 * i], w_down[2 * i + 1], 3 * i + 2)
                if not last:
                    land_pair(w_up[2 * i + 2], w_up[NP + 2 * i + 2], 3 * i + 3)
                    sp_.wait_ge(conv_g, 8 * (2 * i + 1))
                    sp_.dma_start(tap_now[:, 0, :], ffn_taps[2 * i + 2]).then_inc(tap_a_loaded, 16)
                    sp_.wait_ge(conv_g, 8 * (2 * i + 2))
                    sp_.dma_start(tap_now[:, 1, :], ffn_taps[2 * i + 3]).then_inc(tap_b_loaded, 16)

            ffn_loads(0, False)
            with sp_.Fori(1, NI - 1) as i:
                ffn_loads(i, False)
            ffn_loads(NI - 1, True)
            for n in range(NC):
                sp_.wait_ge(out_ready, KT * (n + 1))
                sp_.dma_start(outT[:, :, n * CH:(n + 1) * CH].rearrange("k p t -> p k t"), streamc[:, :, n, :])\
                   .then_inc(stored, 16)
            sp_.wait_ge(stored, 16 * NC)

        @block.tensor
        def _(pe):
            def tile(u, j, first, evac, evac_at, done):
                pe.wait_ge(slot_loaded[SLOT[u]], 16 * (len(loads[SLOT[u]]) * j + nth[u]))
                for n in range(NC):
                    if evac is not None:
                        pe.wait_ge(evac, evac_at + n)
                    if u == "cg" and first:
                        pe.wait_ge(h_even, KT // 2 * (n + 1))
                        pe.wait_ge(h_odd, KT // 2 * (n + 1))
                    for k in range(KT):
                        mm = pe.matmul(ps[:, n, :], slot[SLOT[u]][:, k * P:(k + 1) * P], streamc[:, k, n, :],
                                       start=(k == 0), stop=(k == KT - 1))
                    mm.then_inc(done, 1)

            def gates(j, d, first):
                for i in range(10):
                    q = 10 * d + i
                    if not (first and q < 4):
                        pe.wait_ge(gate_evac, 20 * j + q - 3)
                    at, n = (0, TC) if i % 5 == 0 else (TC + (i % 5 - 1) * CH, CH)
                    pe.matmul(ps[:, 4 + q % 4, 0:n], gate_w[:, 2 * d + i // 5, :], xr[:, at:at + n],
                              start=True, stop=True).then_inc(gate_mm, 1)

            def mixer(j, first):
                tile("cg", j, first, None if first else rg_evac, 4 * j - 3, cg_mm)
                if not first:
                    gates(j - 1, 1, first)
                tile("cv", j, first, cg_evac, 4 * j + 1, cv_mm)
                pe.wait_ge(slot_loaded[2], 16 * (len(loads[2]) * j + nth["rx"]))
                if first:
                    pe.wait_ge(hctx_ready, KT)
                else:
                    pe.wait_ge(gate_evac, 20 * j - 3)
                for k in range(KT):
                    mm = pe.matmul(ps[:, 4, 0:TC], slot[2][:, k * P:(k + 1) * P], h_ctx[:, k, :],
                                   start=(k == 0), stop=(k == KT - 1))
                mm.then_inc(rx_mm, 1)
                tile("rx", j, first, cv_evac, 4 * j + 1, rx_mm)
                tile("rg", j, first, rx_evac, 5 * j + 2, rg_mm)
                pe.wait_ge(gatew_loaded, 16 * (j + 1))
                pe.wait_ge(rg_tap, 8 * (j + 1))
                if first:
                    pe.wait_ge(rx_evac, 5)
                gates(j, 0, first)

            mixer(0, True)
            with pe.Fori(1, GT) as j:
                mixer(j, False)
            gates(GT - 1, 1, False)

            def sum_pair(sumsq, col, squared, at, done):
                pe.wait_ge(squared, at)
                pe.matmul(ps[:, 7, col:col + 1], mean_of_model[:], sumsq[:, 0:1], start=True, stop=False)
                pe.matmul(ps[:, 7, col:col + 1], mean_of_model[:], sumsq[:, 1:2], start=False, stop=True)\
                  .then_inc(done, 1)

            def conv_stats(n, which):
                src = sidec[:, 0:GT, n, :] if which == 0 else csq
                for c in range(GT):
                    mm = pe.matmul(ps[:, 4 + which, :], mean_of_group[:], src[:, c, :],
                                   start=(c == 0), stop=(c == GT - 1))
                mm.then_inc((cmean_mm, cvar_mm)[which], 1)

            def chunk(n, conv, out, norm, first=False):
                for m in range(KT):
                    if out:
                        if first:
                            pe.wait_ge(wo_loaded[m], 16)
                            if m == 0:
                                pe.wait_ge(unit_done, 2 * GT)
                        if m == 0:
                            pe.wait_ge(csilu, GT * (n + 1))
                        if not (first and m < 4):
                            pe.wait_ge(out_evac, KT * n + m - 3)
                        for k in range(KT):
                            kk = (k + GT) % KT
                            mm = pe.matmul(ps[:, m % 4, :], wo[m][:, kk * P:(kk + 1) * P], sidec[:, kk, n, :],
                                           start=(k == 0), stop=(k == KT - 1))
                        mm.then_inc(out_mm, 1)
                    if m == 0 and conv:
                        if out:
                            pe.wait_ge(csub, GT * (n + 1))
                        conv_stats(n + 1, 0)
                    if m == 1 and norm:
                        pe.wait_ge(psum_step, (KT - 1) * (n))
                        pe.matmul(ps[:, 6, :], mean_of_model[:], lsum, start=True, stop=True).then_inc(mean_mm, 1)
                    if m == 3 and conv:
                        pe.wait_ge(csquare, GT * (n + 2))
                        if out:
                            pe.wait_ge(cnewton, 4 * (n + 1))
                        conv_stats(n + 1, 1)
                    if m == 4 and norm:
                        pe.wait_ge(qsum_step, (KT - 1) * (n))
                        pe.matmul(ps[:, 7, :], mean_of_model[:], lsqs, start=True, stop=True).then_inc(var_mm, 1)

            pe.wait_ge(consts, 2)
            pe.wait_ge(gate_evac, 20 * GT)
            pe.wait_ge(conv_tap, CONV_K * GT)
            chunk(-1, True, False, False)
            sum_pair(h2_sumsq, 0, bound_sq, 2, bound_mm)
            pe.wait_ge(h2_scaled, 1)
            sum_pair(w_sumsq, 1, w_square, 2, w_sum_mm)
            pe.wait_ge(rg_evac, NC * GT)
            chunk(0, True, True, False, first=True)
            with pe.Fori(1, NC - 1) as n:
                chunk(n, True, True, True)
            chunk(NC - 1, False, True, True)

            def products(out, w16, x16, start, stop):
                for q, (a, b) in enumerate(((0, 0), (0, 1), (1, 0))):
                    mm = pe.matmul(out, w16[:, a], x16[:, b], start=start and q == 0, stop=stop and q == 2)
                return mm

            def variance(q, bank, squares):
                for m in range(KT):
                    pe.wait_ge(lsquare, KT * q + m + 1)
                    mm = pe.matmul(ps[:, bank, :], mean_of_model[:], squares[:, m, :],
                                   start=(m == 0), stop=(m == KT - 1))
                mm.then_inc(var_mm, 1)

            def up(i, q, n, first):
                if n == 0:
                    pe.wait_ge(w_lo, (6 * i, 6 * i + 2)[q // 2] + q % 2 + 1)
                if first and q == 0:
                    pe.wait_ge(h2_lo, KT * (n + 1))
                    if n == 0:
                        pe.wait_ge(out_evac, KT * NC)
                else:
                    pe.wait_ge(z_evac, 4 * (4 * i + q - 1) + n + 1)
                for k in range(KT):
                    mm = products(ps[:, n, :], up16[:, q % 2, :, k * P:(k + 1) * P], side16[:, k, n],
                                  k == 0, k == KT - 1)
                mm.then_inc(up_mm, 1)

            def down(i, g):
                n, m = g // KT, g % KT
                pe.wait_ge(down_bank_free, NG * i + max(g + 1, DB))
                if g == 0:
                    pe.wait_ge(w_lo, 6 * i + 6)
                    pe.wait_ge(act_lo, 2 * (i + 1))
                for q in range(2):
                    mm = products(ps[:, 4 + g % DB, :],
                                  down16[:, q, :, m * P:(m + 1) * P], act16[:, q, :, n * CH:(n + 1) * CH],
                                  q == 0, q == 1)
                mm.then_inc(down_mm, 1)

            def ffn(i, first, last):
                for n in range(NC):
                    up(i, 0, n, first)
                    if first and n == 0:
                        pe.wait_ge(psum_step, (KT - 1) * NC)
                        pe.matmul(ps[:, 6, :], mean_of_model[:], lsum, start=True, stop=True).then_inc(mean_mm, 1)
                    if first and n == 1:
                        variance(NC - 1, 7, lsq)
                for n in range(NC):
                    up(i, 1, n, first)
                    if n == 0 and first:
                        pe.wait_ge(lnewton, 4 * NC)
                    if n == 1 and not first:
                        sum_pair(act_sumsq, 2, act_square, 2 * i, act_sum_mm)
                    if n == 2:
                        if not first:
                            pe.wait_ge(act_scale_step, 5 * (i - 1) + 1)
                        sum_pair(w_sumsq, 0, w_square, 6 * i + 4, w_sum_mm)
                if not first:
                    for g in range(NG):
                        down(i - 1, g)
                for n in range(NC):
                    up(i, 2, n, first)
                    if n == 0:
                        sum_pair(w_sumsq, 1, w_square, 6 * i + 6, w_sum_mm)
                for n in range(NC):
                    up(i, 3, n, first)
                    if n == 0 and not last:
                        sum_pair(w_sumsq, 0, w_square, 6 * i + 8, w_sum_mm)

            ffn(0, True, False)
            with pe.Fori(1, NI - 1) as i:
                ffn(i, False, False)
            ffn(NI - 1, False, True)
            sum_pair(act_sumsq, 2, act_square, 2 * NI, act_sum_mm)
            pe.wait_ge(z_evac, 4 * 4 * NI)
            for n in range(NC + 1):
                for m in range(KT):
                    if n < NC:
                        down(NI - 1, n * KT + m)
                    if n > 0 and m == (KT // 2 - 1 if n < NC else 0):
                        variance(NC + n - 1, 2 * ((n - 1) % 2) + 1, lsq2)
                if n < NC:
                    pe.wait_ge(psum_step, (KT - 1) * (NC + n + 1))
                    if n > 1:
                        pe.wait_ge(lsub, KT * (NC + n - 1))
                    pe.matmul(ps[:, 2 * (n % 2), :], mean_of_model[:], ln2_scratch[1], start=True, stop=True)\
                      .then_inc(mean_mm, 1)

        @block.scalar
        def _(a):
            a.wait_ge(rows_loaded, 16)
            a.activation(silu_rows, silu_rows, ACT.Silu).then_inc(silu_done, 1)
            a.wait_ge(prep, 1)
            a.activation(sp[:, 1], sp[:, 0], ACT.Exp, scale=-1.0).then_inc(prep, 1)
            def ctx_sum(t):
                a.wait_ge(ada_ctx_prod, t + 1)
                a.activation(ada_prod[t % 2], ada_prod[t % 2], ACT.Copy, accum_out=mod_raw[:, t, 1:2])\
                 .then_inc(ada_ctx_sum, 1)

            for t in range(KT + 2):
                ctx_sum(t)
            a.wait_ge(mod_done, 1)
            for n in range(NC):
                a.wait_ge(x_loaded[n], 16)
                for t in range(KT + 2 + 2 * n, min(KT + 4 + 2 * n, 2 * KT)):
                    ctx_sum(t)
                for k in range(0, KT, 2):
                    a.activation(streamc[:, k, n, :], streamc[:, k, n, :], ACT.Identity, scale=mod0[:, 1, k, 0:1],
                                 bias=mod0[:, 0, k, 0:1]).then_inc(h_even, 1)

            pj_of = (pj_now, pj_prev)

            def unit(j, d):
                q = 2 * j + d
                pj_now = pj_of[d]
                a.wait_ge(gate_evac, 20 * j + 10 * d + 5)
                a.activation(sq, tr, ACT.Tanh, scale=pj_now[:, PJ_TH + d:PJ_TH + d + 1],
                             bias=pj_now[:, PJ_TH + d:PJ_TH + d + 1]).then_inc(rg_act, 1)
                a.wait_ge(rg_act, 3 * q + 1)
                a.activation(tr, tr, ACT.Exp, scale=pj_now[:, PJ_EX + d:PJ_EX + d + 1],
                             bias=pj_now[:, PJ_EX + d:PJ_EX + d + 1]).then_inc(rg_act, 1)
                a.activation(sq, sq, ACT.Sqrt, scale=0.25).then_inc(rg_act, 1)

            def gates(j, d, first):
                if not (first and d == 0):
                    a.wait_ge(unit_done, 2 * j + d)
                for i in range(10):
                    a.wait_ge(gate_mm, 20 * j + 10 * d + i + 1)
                    at, n = (0, TC) if i % 5 == 0 else (TC + (i % 5 - 1) * CH, CH)
                    dst = (tr, ti)[i // 5]
                    g = PJ_GB + 2 * d + i // 5
                    a.activation(dst[:, at:at + n], ps[:, 4 + (10 * d + i) % 4, 0:n], ACT.Tanh, scale=0.5,
                                 bias=pj_of[d][:, g:g + 1]).then_inc(gate_evac, 1)

            def ada_sums(j, lo, hi):
                for t in range(lo, hi):
                    s_ = slot[SLOT[f"ada{t}"]]
                    a.wait_ge(ada_prod_done, KT * j + t + 1)
                    a.activation(s_, s_, ACT.Copy, accum_out=ada_sum[:, t:t + 1]).then_inc(ada_sum_done, 1)

            def mixer(j, first):
                for n in range(NC):
                    if not first and n == 0:
                        a.wait_ge(rg_tap, 8 * j)
                    a.wait_ge(cg_mm, 4 * j + n + 1)
                    a.activation(rx_lat[:, n * CH:(n + 1) * CH], ps[:, n, :], ACT.Sigmoid).then_inc(cg_evac, 1)
                if not first:
                    backward(j - 1)
                a.wait_ge(rx_mm, 5 * j + 1)
                a.activation(rx_ctx, ps[:, 4, 0:TC], ACT.Copy).then_inc(rx_evac, 1)
                for n in range(NC):
                    if n == 2:
                        if not first:
                            a.wait_ge(mod_done, j + 1)
                        ada_sums(j, 0, 2)
                    a.wait_ge(cv_evac, 4 * j + n + 1)
                    a.wait_ge(rx_mm, 5 * j + n + 2)
                    a.activation(rx_lat[:, n * CH:(n + 1) * CH], ps[:, n, :], ACT.Copy).then_inc(rx_evac, 1)
                ada_sums(j, 2, 4)
                if not first:
                    a.wait_ge(unit_done, 2 * j)
                for n in range(NC):
                    a.wait_ge(rg_mm, 4 * j + n + 1)
                    a.activation(gelu_rg[:, n * CH:(n + 1) * CH], ps[:, n, :], ACT.Gelu_apprx_tanh)\
                     .then_inc(rg_evac, 1)
                    ada_sums(j, 4 + n, 5 + n)
                a.wait_ge(jp_ready, j + 1)
                gates(j, 0, first)
                unit(j, 0)

            def backward(j):
                a.wait_ge(jp_kept, j + 1)
                gates(j, 1, False)
                unit(j, 1)

            mixer(0, True)
            with a.Fori(1, GT) as j:
                mixer(j, False)
            backward(GT - 1)

            def chunk(n, conv, norm, later=True):
                if conv:
                    if n != -1:
                        a.wait_ge(cvar_mm, n + 1)
                    for c in range(GT):
                        a.wait_ge(csub, GT * (n + 1) + c + 1)
                        a.activation(csq[:, c, :], sidec[:, c, n + 1, :], ACT.Square).then_inc(csquare, 1)
                if norm:
                    if later:
                        a.wait_ge(qsum_step, (KT - 1) * (n - 1))
                    for m in range(KT):
                        a.wait_ge(lsub, KT * (n - 1) + m + 1)
                        a.activation(lsq[:, m, :], streamc[:, m, n - 1, :], ACT.Square).then_inc(lsquare, 1)
                if conv:
                    a.wait_ge(cvar_mm, n + 2)
                    a.activation(cr0, ps[:, 5, :], ACT.Ln, bias=eps_now[:, 0:1]).then_inc(clog, 1)
                    a.wait_ge(clog, n + 2)
                    a.activation(cr0, cr0, ACT.Exp, scale=-0.5).then_inc(cexp, 1)
                    for c in range(GT):
                        a.wait_ge(cnorm, GT * (n + 1) + c + 1)
                        a.activation(sidec[:, c, n + 1, :], sidec[:, c, n + 1, :], ACT.Silu, scale=cln_g[:, c:c + 1],
                                     bias=cln_b[:, c:c + 1]).then_inc(csilu, 1)
                if norm:
                    rstd_guess(n, 7, lr0)
                    a.wait_ge(out_mm, KT * n)
                    a.wait_ge(h2_scaled, 6)
                    for m in range(KT):
                        a.wait_ge(lnorm, KT * (n - 1) + m + 1)
                        a.activation(side16[:, m, n - 1, 0], streamc[:, m, n - 1, :], ACT.Identity,
                                     scale=h2_scale[:, m:m + 1], bias=h2_bias[:, m:m + 1]).then_inc(h2_hi, 1)
                    for m in range(KT):
                        a.wait_ge(h2_ready, KT * (n - 1) + m + 1)
                        a.activation(streamc[:, m, n - 1, :], streamc[:, m, n - 1, :], ACT.Identity,
                                     scale=ln_g[1][:, m:m + 1], bias=ln_b[1][:, m:m + 1]).then_inc(x1_ready, 1)

            def rstd_guess(n, bank, lr0):
                a.wait_ge(var_mm, n)
                a.activation(lr0, ps[:, bank, :], ACT.Ln, bias=eps_now[:, 1:2]).then_inc(llog, 1)
                a.wait_ge(llog, n)
                a.activation(lr0, lr0, ACT.Exp, scale=-0.5).then_inc(lexp, 1)

            def square_pair(p, junk):
                for q, loaded in enumerate((land_u_loaded, land_g_loaded)):
                    a.wait_ge(loaded, 16 * (p + 1))
                    a.activation(junk[:, 0, q].bitcast(BF16), land[q], ACT.Square,
                                 accum_out=w_sumsq[:, q:q + 1]).then_inc(w_square, 1)

            def high_part(x16, q, scale, ready, at):
                a.wait_ge(ready, at)
                a.activation(x16[:, q, 0], land[q], ACT.Copy, scale=scale[:].bitcast(F32))
                a.activation(land[q], land[q], ACT.Copy, scale=scale[:].bitcast(F32)).then_inc(w_hi, 1)

            chunk(-1, True, False)
            a.wait_ge(prep_step, AFFINE_STEP)
            a.activation(bound_junk[:, 0], h2_scale[:], ACT.Square, scale=float(D) ** 0.5,
                         accum_out=h2_sumsq[:, 0:1]).then_inc(bound_sq, 1)
            a.activation(bound_junk[:, 1], h2_bias[:], ACT.Square, accum_out=h2_sumsq[:, 1:2]).then_inc(bound_sq, 1)
            a.wait_ge(unit_done, 2 * GT)
            square_pair(0, up16)
            chunk(0, True, False)
            high_part(up16, 0, up_scale, up_scale_step, 3)
            chunk(1, True, True, later=False)
            with a.Fori(2, NC - 1) as n:
                chunk(n, True, True)
            chunk(NC - 1, False, True)
            chunk(NC, False, True)

            def evac_z(i, q, n):
                if n == 0:
                    a.wait_ge(up_scale_step, 5 * (2 * i + q // 2) + 5)
                a.wait_ge(up_mm, 4 * (4 * i + q) + n + 1)
                r = CH // GRID_W
                a.activation((zu, zg)[q % 2][:, 1 + n * r:1 + (n + 1) * r, 1:1 + GRID_W],
                             ps[:, n, :].rearrange("p (r c) -> p r c", c=GRID_W), ACT.Copy,
                             scale=up_inv[:, q // 2:q // 2 + 1].bitcast(F32)).then_inc(z_evac, 1)

            def first_tap(i, q):
                y, z, done = ((yu[q // 2], zu, first_u), (yg, zg, first_g))[q % 2]
                c_ = 10 * (q % 2)
                a.wait_ge(z_evac, 4 * (4 * i + q) + NC)
                a.activation(y.rearrange("p (r c) -> p r c", c=GRID_W), z[:, 0:ROWS, 0:GRID_W], ACT.Identity,
                             scale=tap_now[:, q // 2, c_:c_ + 1], bias=tap_now[:, q // 2, c_ + 9:c_ + 10])\
                 .then_inc(done, 1)

            def gelu(tile):
                a.wait_ge(conv_g, 8 * (tile + 1))
                a.activation(yg, yg, ACT.Gelu_apprx_tanh).then_inc(gelu_done, 1)

            def square_act(i, t):
                a.wait_ge((act_a_done, act_b_done)[t], i + 1)
                a.activation(act16[:, t, 0].bitcast(BF16), act[t], ACT.Square,
                             accum_out=act_sumsq[:, t:t + 1]).then_inc(act_square, 1)

            def high_acts(i):
                a.wait_ge(act_scale_step, 5 * i + 3)
                for t in range(2):
                    a.activation(act16[:, t, 0], act[t], ACT.Copy, scale=act_scale[:].bitcast(F32)).then_inc(act_hi, 1)

            def ffn(i, first, last):
                if first:
                    a.wait_ge(zpads, 1)
                    a.wait_ge(cvar_mm, NC)
                else:
                    a.wait_ge(up_mm, 16 * i)
                high_part(up16, 1, up_scale, up_scale_step, 5 * 2 * i + 3)
                if not first:
                    a.wait_ge(conv_u, 8 * 2 * i)
                for n in range(3):
                    evac_z(i, 0, n)
                if not first:
                    gelu(2 * i - 1)
                evac_z(i, 0, 3)
                a.wait_ge(tap_a_loaded, 16 * (i + 1))
                if not first:
                    a.wait_ge(act_a_done, i)
                first_tap(i, 0)
                if first:
                    a.wait_ge(h2_lo, KT * NC)
                else:
                    a.wait_ge(conv_g, 8 * 2 * i)
                evac_z(i, 1, 0)
                if not first:
                    square_act(i - 1, 1)
                a.wait_ge(up_mm, 16 * i + 4)
                square_pair(3 * i + 1, up16)
                evac_z(i, 1, 1)
                if not first:
                    high_acts(i - 1)
                evac_z(i, 1, 2)
                evac_z(i, 1, 3)
                if not first:
                    a.wait_ge(act_b_done, i)
                first_tap(i, 1)
                high_part(up16, 0, up_scale, up_scale_step, 5 * (2 * i + 1) + 3)
                a.wait_ge(up_mm, 16 * i + 8)
                high_part(up16, 1, up_scale, up_scale_step, 5 * (2 * i + 1) + 3)
                if not first:
                    a.wait_ge(down_mm, NG * i)
                square_pair(3 * i + 2, down16)
                a.wait_ge(conv_u, 8 * (2 * i + 1))
                evac_z(i, 2, 0)
                gelu(2 * i)
                high_part(down16, 0, down_scale, down_scale_step, 4 * i + 3)
                high_part(down16, 1, down_scale, down_scale_step, 4 * i + 3)
                evac_z(i, 2, 1)
                evac_z(i, 2, 2)
                square_act(i, 0)
                evac_z(i, 2, 3)
                a.wait_ge(tap_b_loaded, 16 * (i + 1))
                if not first:
                    a.wait_ge(act_lo, 2 * i)
                first_tap(i, 2)
                if not last:
                    a.wait_ge(up_mm, 16 * i + 12)
                    square_pair(3 * i + 3, up16)
                evac_z(i, 3, 0)
                if not last:
                    high_part(up16, 0, up_scale, up_scale_step, 5 * (2 * i + 2) + 3)
                for n in range(1, NC):
                    evac_z(i, 3, n)
                first_tap(i, 3)

            ffn(0, True, False)
            with a.Fori(1, NI - 1) as i:
                ffn(i, False, False)
            ffn(NI - 1, False, True)
            gelu(2 * NI - 1)
            square_act(NI - 1, 1)
            high_acts(NI - 1)

            for n in range(NC):
                a.wait_ge(var_mm, NC + n)
                for m in range(KT):
                    a.wait_ge(lsub, KT * (NC + n) + m + 1)
                    a.activation(lsq2[:, m, :], streamc[:, m, n, :], ACT.Square).then_inc(lsquare, 1)
                rstd_guess(NC + n + 1, 2 * (n % 2) + 1, ln2_scratch[3])
                for m in range(KT):
                    a.wait_ge(lnorm, KT * (NC + n) + m + 1)
                    a.activation(streamc[:, m, n, :], streamc[:, m, n, :], ACT.Identity,
                                 scale=ln_g[2][:, m:m + 1], bias=ln_b[2][:, m:m + 1]).then_inc(out_ready, 1)

        @block.vector
        def _(v):
            v.wait_ge(par_loaded, 16)
            lam = pj[:, :, PJ_TH:PJ_TH + 2]
            v.tensor_scalar(sp[:, 4], lam, -1.0, None, ALU.mult).then_inc(prep_step, 1)
            v.wait_ge(prep_step, 1)
            v.tensor_tensor(sp[:, 0], sp[:, 4], lam, ALU.max).then_inc(prep, 1)
            v.tensor_scalar(pj[:, :, PJ_GB:PJ_GB + 4], pj[:, :, PJ_GB:PJ_GB + 4], 0.5, None, ALU.mult)\
             .then_inc(prep_step, 1)
            v.memset(eps_now[:, 0:1], EPS).then_inc(prep_step, 1)
            v.memset(eps_now[:, 1:2], EPS / (ALPHA * ALPHA)).then_inc(prep_step, 1)
            c = 4

            def link(i):
                nonlocal c
                c += 1
                i.then_inc(prep_step, 1)
                v.wait_ge(prep_step, c)

            v.wait_ge(prep, 2)
            e, r, r2, acc, neg = (sp[:, i] for i in (1, 0, 2, 3, 4))
            link(v.tensor_scalar(r2, e, 2.0, None, ALU.add))
            link(v.reciprocal(acc, r2))
            link(v.tensor_tensor(r, e, acc, ALU.mult))
            link(v.tensor_tensor(r2, r, r, ALU.mult))
            link(v.tensor_scalar(acc, r2, 1.0 / 17, 1.0 / 15, ALU.mult, ALU.add))
            for odd in (13, 11, 9, 7, 5, 3, 1):
                link(v.tensor_tensor(acc, acc, r2, ALU.mult))
                link(v.tensor_scalar(acc, acc, 1.0 / odd, None, ALU.add))
            link(v.tensor_tensor(acc, acc, r, ALU.mult))
            link(v.tensor_scalar(neg, neg, 0.0, 0.5, ALU.max, ALU.mult))
            link(v.tensor_tensor(acc, acc, neg, ALU.add))
            link(v.tensor_scalar(pj[:, :, PJ_EX:PJ_EX + 2], acc, -8.0, None, ALU.mult))
            link(v.tensor_scalar(pj[:, :, PJ_TH:PJ_TH + 2], acc, 4.0, None, ALU.mult))

            raw = mod_raw[:].rearrange("p (g k) c -> p g k c", k=KT)
            v.wait_ge(silu_done, 1)
            for t in range(2 * KT):
                if t % 4 == 0:
                    v.wait_ge(ada_loaded[t // 4], 16)
                if t > 3:
                    v.wait_ge(ada_c, t - 3)
                v.scalar_tensor_tensor(out=ada_junk[t % 4], in0=ada_w[:, t, :], scalar=1.0, in1=silu_rows[:, 0, :],
                                       op0=ALU.mult, op1=ALU.mult, accum_out=mod_raw[:, t, 0:1]).then_inc(ada_c, 1)
            v.wait_ge(ada_c, 2 * KT)
            link(v.tensor_tensor(mod0[:, :, :, 0], raw[:, :, :, 0], b_ada[:, 0:2, :], ALU.add))
            v.tensor_scalar(mod0[:, 1, :, 0], mod0[:, 1, :, 0], 1.0, None, ALU.add).then_inc(mod_done, 1)
            v.wait_ge(mod_done, 1)
            for n in range(NC):
                v.wait_ge(x_loaded[n], 16)
                for k in range(1, KT, 2):
                    v.tensor_scalar(streamc[:, k, n, :], streamc[:, k, n, :], mod0[:, 1, k, 0:1],
                                    mod0[:, 0, k, 0:1], ALU.mult, ALU.add).then_inc(h_odd, 1)
            v.wait_ge(ada_ctx_sum, 2 * KT)
            link(v.tensor_tensor(mod0[:, :, :, 1], raw[:, :, :, 1], b_ada[:, 0:2, :], ALU.add))
            link(v.tensor_scalar(mod0[:, 1, :, 1], mod0[:, 1, :, 1], 1.0, None, ALU.add))
            v.wait_ge(ctx_loaded, 16)
            for k in range(KT):
                v.tensor_scalar(h_ctx[:, k, :], h_ctx[:, k, :], mod0[:, 1, k, 1:2], mod0[:, 0, k, 1:2],
                                ALU.mult, ALU.add).then_inc(hctx_ready, 1)

            def conv_taps(j, lo, hi, pj_now=pj_now):
                for k in range(lo, hi):
                    if k == 0:
                        v.wait_ge(jp_ready, j + 1)
                        v.wait_ge(cv_evac, NC * (j + 1))
                        i = v.tensor_scalar(side[:, j, :], upad[:, 0:T], pj_now[:, 0:1],
                                            pj_now[:, PJ_CONVB:PJ_CONVB + 1], ALU.mult, ALU.add)
                    else:
                        v.wait_ge(conv_tap, CONV_K * j + k)
                        i = v.scalar_tensor_tensor(out=side[:, j, :], in0=upad[:, k:k + T], scalar=pj_now[:, k:k + 1],
                                                   in1=side[:, j, :], op0=ALU.mult, op1=ALU.add)
                    i.then_inc(conv_tap, 1)

            def rg_conv(j):
                for k in range(RG_K):
                    w, b = pj_now[:, PJ_RG + k:PJ_RG + k + 1], pj_now[:, PJ_RGB:PJ_RGB + 1]
                    for half, (dst, src) in enumerate(((xr[:, TC:TC + T], rxp[:, LAT0 + k:LAT0 + k + T]),
                                                       (xr[:, 0:TC], rxp[:, k:k + TC]))):
                        if k == 0:
                            i = v.tensor_scalar(dst, src, w, b, ALU.mult, ALU.add)
                        else:
                            v.wait_ge(rg_tap, 8 * j + 2 * (k - 1) + half + 1)
                            i = v.scalar_tensor_tensor(out=dst, in0=src, scalar=w, in1=dst, op0=ALU.mult, op1=ALU.add)
                        i.then_inc(rg_tap, 1)

            def unit(j, d):
                q = 2 * j + d
                v.wait_ge(gate_evac, 20 * j + 10 * d + 10)
                v.scalar_tensor_tensor(out=ti, in0=ti, scalar=1.0, in1=xr, op0=ALU.add, op1=ALU.mult)\
                 .then_inc(unit_step, 1)
                v.wait_ge(rg_act, 3 * (q + 1))
                v.scalar_tensor_tensor(out=sq, in0=tr, scalar=1.0, in1=sq, op0=ALU.add, op1=ALU.mult)\
                 .then_inc(unit_step, 1)
                v.wait_ge(unit_step, 4 * q + 2)
                v.tensor_tensor(sq, sq, ti, ALU.mult).then_inc(unit_step, 1)
                v.wait_ge(unit_step, 4 * q + 3)
                back = slice(None, None, -1)
                if d == 0:
                    v.tensor_tensor_scan(out=ti[:, 0:TC], data0=tr[:, 0:TC], data1=sq[:, 0:TC], initial=0.0,
                                         op0=ALU.mult, op1=ALU.add).then_inc(unit_step, 1)
                    v.wait_ge(unit_step, 4 * q + 4)
                    v.tensor_tensor_scan(out=side[:, GT + j, :], data0=tr[:, TC:], data1=sq[:, TC:],
                                         initial=ti[:, TC - 1:TC], op0=ALU.mult, op1=ALU.add).then_inc(unit_done, 1)
                else:
                    v.tensor_tensor_scan(out=ti[:, 0:TC][:, back], data0=tr[:, 0:TC][:, back],
                                         data1=sq[:, 0:TC][:, back], initial=0.0,
                                         op0=ALU.mult, op1=ALU.add).then_inc(unit_step, 1)
                    v.wait_ge(unit_step, 4 * q + 4)
                    v.tensor_tensor_scan(out=ti[:, TC:][:, back], data0=tr[:, TC:][:, back],
                                         data1=sq[:, TC:][:, back], initial=ti[:, 0:1],
                                         op0=ALU.mult, op1=ALU.add).then_inc(scan_step, 1)
                    v.wait_ge(scan_step, j + 1)
                    v.wait_ge(unit_done, 2 * j + 1)
                    v.tensor_tensor(side[:, GT + j, :], side[:, GT + j, :], ti[:, TC:], ALU.add)\
                     .then_inc(mix_step, 1)
                    v.wait_ge(rg_evac, NC * (j + 1))
                    v.wait_ge(mix_step, j + 1)
                    v.tensor_tensor(side[:, GT + j, :], side[:, GT + j, :], gelu_rg, ALU.mult)\
                     .then_inc(unit_done, 1)

            def leftover(j):
                conv_taps(j, TAPS_2, TAPS_3)
                unit(j, 0)
                v.tensor_copy(pj_prev[:], pj_now[:]).then_inc(jp_kept, 1)
                v.wait_ge(jp_kept, j + 1)
                conv_taps(j, TAPS_3, CONV_K, pj_prev)

            def backward(j):
                unit(j, 1)
                v.wait_ge(ada_sum_done, KT * (j + 1))
                v.tensor_tensor(mods[:, j, :], ada_sum[:], b_ada[:, 2 + j, :], ALU.add).then_inc(mod_done, 1)

            def mixer(j, first):
                if not first:
                    leftover(j - 1)
                    v.wait_ge(conv_tap, CONV_K * j)
                v.tensor_copy(pj_now[:], pj[:, j, :]).then_inc(jp_ready, 1)
                for n in range(NC):
                    v.wait_ge(cg_evac, NC * j + n + 1)
                    v.wait_ge(cv_mm, NC * j + n + 1)
                    v.tensor_tensor(upad[:, PAD + n * CH:PAD + (n + 1) * CH], ps[:, n, :],
                                    rx_lat[:, n * CH:(n + 1) * CH], ALU.mult).then_inc(cv_evac, 1)
                if not first:
                    backward(j - 1)
                conv_taps(j, 0, TAPS_1)
                v.wait_ge(rx_evac, 5 * (j + 1))
                rg_conv(j)
                conv_taps(j, TAPS_1, TAPS_2)

            v.wait_ge(pads, 5)
            mixer(0, True)
            with v.Fori(1, GT) as j:
                mixer(j, False)
            leftover(GT - 1)
            backward(GT - 1)

            v.wait_ge(mod_done, GT + 1)
            link(v.tensor_scalar(g1s[:], mods[:, 0, :], 1.0 / ALPHA, None, ALU.mult))
            link(v.tensor_scalar(g2s[:], mods[:, 3, :], 1.0 / ALPHA, None, ALU.mult))
            link(v.tensor_scalar(mods[:, 2, :], mods[:, 2, :], 1.0, None, ALU.add))
            link(v.tensor_tensor(h2_scale[:], ln_g[1], mods[:, 2, :], ALU.mult))
            link(v.tensor_tensor(h2_bias[:], ln_b[1], mods[:, 2, :], ALU.mult))
            link(v.tensor_tensor(h2_bias[:], h2_bias[:], mods[:, 1, :], ALU.add))
            assert c == AFFINE_STEP, c

            def scale_of(col, top, scale, inv, done, at):
                v.tensor_scalar(half_bits[:], ps[:, 7, col:col + 1].bitcast(I32), 1, None, ALU.logical_shift_right)\
                 .then_inc(done, 1)
                v.wait_ge(done, at + 1)
                v.tensor_scalar(scale[:], half_bits[:], -1.0, float(top), ALU.mult, ALU.add).then_inc(done, 1)
                v.wait_ge(done, at + 2)
                v.tensor_scalar(scale[:], scale[:], EXPONENT, None, ALU.bitwise_and).then_inc(done, 1)
                v.wait_ge(done, at + 3)
                v.tensor_scalar(inv, scale[:], -1.0, float(INVERSE), ALU.mult, ALU.add).then_inc(done, 1)
                v.wait_ge(done, at + 4)

            def up_scales(half, nth_, p, col=0):
                v.wait_ge(w_sum_mm, p + 1)
                inv = up_inv[:, half:half + 1]
                scale_of(col, SCALE_TOP, up_scale, inv, up_scale_step, 5 * nth_)
                v.tensor_scalar(inv.bitcast(F32), inv.bitcast(F32), h2_inv[:].bitcast(F32), None, ALU.mult)\
                 .then_inc(up_scale_step, 1)


            def newton(var, eps, r0, r, done, base, nth_guess, guess):
                v.wait_ge(guess, nth_guess)
                v.scalar_tensor_tensor(out=r, in0=var, scalar=eps, in1=r0, op0=ALU.add, op1=ALU.mult).then_inc(done, 1)
                v.wait_ge(done, base + 1)
                v.tensor_tensor(r, r, r0, ALU.mult).then_inc(done, 1)
                v.wait_ge(done, base + 2)
                v.tensor_scalar(r, r, -0.5, 1.5, ALU.mult, ALU.add).then_inc(done, 1)
                v.wait_ge(done, base + 3)
                v.tensor_tensor(r, r, r0, ALU.mult).then_inc(done, 1)
                v.wait_ge(done, base + 4)

            def ln_sub(q, n, bank):
                v.wait_ge(mean_mm, q + 1)
                for m in range(KT):
                    v.tensor_tensor(streamc[:, m, n, :], streamc[:, m, n, :], ps[:, bank, :], ALU.subtract)\
                     .then_inc(lsub, 1)

            def ln_mul(q, n, bank, lr0=lr0, lr=lr):
                newton(ps[:, bank, :], eps_now[:, 1:2], lr0, lr, lnewton, 4 * q, q + 1, lexp)
                for m in range(KT):
                    v.tensor_tensor(streamc[:, m, n, :], streamc[:, m, n, :], lr, ALU.mult).then_inc(lnorm, 1)

            def h2_low(n):
                for m in range(KT + 1):
                    if m < KT:
                        v.wait_ge(lnorm, KT * n + m + 1)
                        if m > 1:
                            v.wait_ge(h2_lo, KT * n + m - 1)
                        v.tensor_scalar(h2_f32[m % 2], streamc[:, m, n, :], h2_scale[:, m:m + 1], h2_bias[:, m:m + 1],
                                        ALU.mult, ALU.add).then_inc(h2_ready, 1)
                    if m > 0:
                        v.wait_ge(h2_ready, KT * n + m)
                        v.wait_ge(h2_hi, KT * n + m)
                        v.tensor_tensor(side16[:, m - 1, n, 1], h2_f32[(m - 1) % 2], side16[:, m - 1, n, 0],
                                        ALU.subtract).then_inc(h2_lo, 1)
                v.wait_ge(h2_lo, KT * (n + 1))

            def chunk(n, conv, out, norm, first=False):
                for m in range(KT):
                    if out:
                        if m == 0 and first:
                            for i in range(NC):
                                v.wait_ge(xr_loaded[i], 16)
                        v.wait_ge(out_mm, KT * n + m + 1)
                        v.scalar_tensor_tensor(out=streamc[:, m, n, :], in0=ps[:, m % 4, :], scalar=g1s[:, m:m + 1],
                                               in1=streamc[:, m, n, :], op0=ALU.mult, op1=ALU.add)\
                         .then_inc(out_evac, 1)
                    if m == 0 and conv:
                        v.wait_ge(cmean_mm, n + 2)
                        for c_ in range(GT):
                            v.tensor_tensor(sidec[:, c_, n + 1, :], sidec[:, c_, n + 1, :], ps[:, 4, :], ALU.subtract)\
                             .then_inc(csub, 1)
                    if m == 1 and norm:
                        ln_sub(n - 1, n - 1, 6)
                    if m == 3 and conv:
                        newton(ps[:, 5, :], eps_now[:, 0:1], cr0, cr, cnewton, 4 * (n + 1), n + 2, cexp)
                        for c_ in range(GT):
                            v.tensor_tensor(sidec[:, c_, n + 1, :], sidec[:, c_, n + 1, :], cr, ALU.mult)\
                             .then_inc(cnorm, 1)
                    if m == 5 and norm:
                        ln_mul(n - 1, n - 1, 7)
                        h2_low(n - 1)

            chunk(-1, True, False, False)
            v.wait_ge(bound_mm, 1)
            scale_of(0, SCALE_TOP_DOUBLE, h2_pow, h2_inv[:], h2_scaled, 0)
            for affine in (h2_scale, h2_bias):
                v.tensor_scalar(affine[:], affine[:], h2_pow[:].bitcast(F32), None, ALU.mult).then_inc(h2_scaled, 1)
            up_scales(0, 0, 0, col=1)
            chunk(0, True, True, False, first=True)
            with v.Fori(1, NC - 1) as n:
                chunk(n, True, True, True)
            chunk(NC - 1, False, True, True)
            chunk(NC, False, False, True)

            def tap3(i, q, k):
                y, z, first_done, done = ((yu[q // 2], zu, first_u, conv_u), (yg, zg, first_g, conv_g))[q % 2]
                tile = 2 * i + q // 2
                dr, dc = k // 3, k % 3
                c_ = 10 * (q % 2) + k
                y3 = y.rearrange("p (r c) -> p r c", c=GRID_W)
                if k == 1:
                    v.wait_ge(first_done, tile + 1)
                else:
                    v.wait_ge(done, 8 * tile + k - 1)
                v.scalar_tensor_tensor(out=y3, in0=z[:, dr:dr + ROWS, dc:dc + GRID_W],
                                       scalar=tap_now[:, q // 2, c_:c_ + 1],
                                       in1=y3, op0=ALU.mult, op1=ALU.add).then_inc(done, 1)

            def gate(i, t):
                v.wait_ge(gelu_done, 2 * i + t + 1)
                v.wait_ge(conv_u, 8 * (2 * i + t + 1))
                v.tensor_tensor(act[t], yu[t], yg, ALU.mult).then_inc((act_a_done, act_b_done)[t], 1)

            def act_scales(i):
                v.wait_ge(act_sum_mm, i + 1)
                scale_of(2, SCALE_TOP, act_scale, act_inv[:], act_scale_step, 5 * i)
                v.tensor_scalar(g2_now[:], g2s[:], act_inv[:].bitcast(F32), down_inv[:].bitcast(F32),
                                ALU.mult, ALU.mult).then_inc(act_scale_step, 1)

            def act_low(i, t):
                v.wait_ge(act_hi, 2 * i + t + 1)
                v.scalar_tensor_tensor(out=act16[:, t, 1], in0=act[t], scalar=act_scale[:].bitcast(F32),
                                       in1=act16[:, t, 0], op0=ALU.mult, op1=ALU.subtract).then_inc(act_lo, 1)

            def add_down(i, g):
                n, m = g // KT, g % KT
                if g == 0:
                    v.wait_ge(down_bank_free, NG * i + DB)
                    v.wait_ge(act_scale_step, 5 * (i + 1))
                v.wait_ge(down_mm, NG * i + g + 1)
                v.scalar_tensor_tensor(out=streamc[:, m, n, :], in0=ps[:, 4 + g % DB, :], scalar=g2_now[:, m:m + 1],
                                       in1=streamc[:, m, n, :], op0=ALU.mult, op1=ALU.add)\
                 .then_inc(down_bank_free, 1)

            def ffn(i, first, last):
                if not first:
                    for k in range(1, 9):
                        tap3(i - 1, 3, k)
                    gate(i - 1, 1)
                for k in range(1, 6):
                    tap3(i, 0, k)
                    if k == 2 and not first:
                        act_scales(i - 1)
                    if k == 3 and not first:
                        act_low(i - 1, 0)
                        act_low(i - 1, 1)
                up_scales(1, 2 * i + 1, 3 * i + 1)
                rest = [(0, k) for k in range(6, 9)] + [(1, k) for k in range(1, 9)]
                if first:
                    for q, k in rest:
                        tap3(i, q, k)
                    v.wait_ge(x1_ready, KT * NC)
                    v.tensor_copy(g2_now[:], g2s[:]).then_inc(down_bank_free, DB)
                else:
                    for g in range(NG):
                        add_down(i - 1, g)
                        if g % 4 == 1:
                            tap3(i, *rest.pop(0))
                    for q, k in rest:
                        tap3(i, q, k)
                v.wait_ge(w_sum_mm, 3 * i + 3)
                scale_of(1, SCALE_TOP, down_scale, down_inv[:], down_scale_step, 4 * i)
                gate(i, 0)
                for k in range(1, 9):
                    tap3(i, 2, k)
                    if k == 2 and not last:
                        up_scales(0, 2 * i + 2, 3 * i + 3)

            ffn(0, True, False)
            with v.Fori(1, NI - 1) as i:
                ffn(i, False, False)
            ffn(NI - 1, False, True)
            for k in range(1, 9):
                tap3(NI - 1, 3, k)
            gate(NI - 1, 1)
            act_scales(NI - 1)
            act_low(NI - 1, 0)
            act_low(NI - 1, 1)
            for n in range(NC + 1):
                if n < NC:
                    for m in range(KT):
                        add_down(NI - 1, n * KT + m)
                if n > 0:
                    ln_mul(NC + n - 1, n - 1, 2 * ((n - 1) % 2) + 1, *ln2_scratch[3:])
                if n < NC:
                    ln_sub(NC + n, n, 2 * (n % 2))

        @block.gpsimd
        def _(g):
            g.memset(mean_of_group[:], 1.0 / CW).then_inc(consts, 1)
            g.memset(mean_of_model[:], 1.0 / D).then_inc(consts, 1)
            g.memset(upad[:, 0:PAD], 0.0).then_inc(pads, 1)
            g.memset(upad[:, PAD + T:], 0.0).then_inc(pads, 1)
            g.memset(rxp[:, 0:RG_L], 0.0).then_inc(pads, 1)
            g.memset(rxp[:, RG_L + TC:LAT0 + RG_L], 0.0).then_inc(pads, 1)
            g.memset(rxp[:, LAT0 + RG_L + T:], 0.0).then_inc(pads, 1)

            g.wait_ge(silu_done, 1)
            for t in range(2 * KT):
                if t % 4 == 0:
                    g.wait_ge(ada_loaded[t // 4], 16)
                if t > 1:
                    g.wait_ge(ada_ctx_sum, t - 1)
                g.tensor_tensor(ada_prod[t % 2], ada_w[:, t, :], silu_rows[:, 1, :], ALU.mult).then_inc(ada_ctx_prod, 1)

            def ada_products(j):
                for t in range(KT):
                    u = f"ada{t}"
                    g.wait_ge(slot_loaded[SLOT[u]], 16 * (len(loads[SLOT[u]]) * j + nth[u]))
                    g.tensor_tensor(slot[SLOT[u]], slot[SLOT[u]], silu_rows[:, 0, :], ALU.mult).then_inc(ada_prod_done, 1)

            ada_products(0)
            with g.Fori(1, GT) as j:
                ada_products(j)

            def sums(q, n, src_ready, base, first=False, scratch=ln1_scratch, squares=True):
                lsq, lsum, lsqs = scratch[:3]
                if not first:
                    g.wait_ge(mean_mm, q)
                for m in range(1, KT):
                    g.wait_ge(src_ready, base + KT * n + m + 1)
                    if m > 1:
                        g.wait_ge(psum_step, (KT - 1) * q + m - 1)
                    a = streamc[:, 0, n, :] if m == 1 else lsum
                    i = g.tensor_tensor(lsum, a, streamc[:, m, n, :], ALU.add)
                    i.then_inc(psum_step, 1)
                if not squares:
                    return
                if not first:
                    g.wait_ge(var_mm, q)
                for m in range(1, KT):
                    g.wait_ge(lsquare, KT * q + m + 1)
                    if m > 1:
                        g.wait_ge(qsum_step, (KT - 1) * q + m - 1)
                    a = lsq[:, 0, :] if m == 1 else lsqs
                    i = g.tensor_tensor(lsqs, a, lsq[:, m, :], ALU.add)
                    i.then_inc(qsum_step, 1)

            def low_part(x16, q, nth_):
                g.wait_ge(w_hi, nth_ + 1)
                g.tensor_tensor(x16[:, q, 1], land[q], x16[:, q, 0], ALU.subtract).then_inc(w_lo, 1)

            g.wait_ge(unit_done, 2 * GT)
            sums(0, 0, out_evac, 0, first=True)
            low_part(up16, 0, 0)
            with g.Fori(1, NC - 1) as n:
                sums(n, n, out_evac, 0)
            sums(NC - 1, NC - 1, out_evac, 0, squares=False)
            g.wait_ge(out_mm, KT * NC)
            for z in (zu, zg):
                g.memset(z[:, 0, :], 0.0)
                g.memset(z[:, ZR - 1, :], 0.0)
                g.memset(z[:, 1:ZR - 1, 0:1], 0.0)
                i = g.memset(z[:, 1:ZR - 1, ZC - 1:ZC], 0.0)
            i.then_inc(zpads, 1)

            def ffn(i, first, last):
                low_part(up16, 1, 6 * i + 1)
                low_part(up16, 0, 6 * i + 2)
                low_part(up16, 1, 6 * i + 3)
                low_part(down16, 0, 6 * i + 4)
                low_part(down16, 1, 6 * i + 5)
                if not last:
                    low_part(up16, 0, 6 * i + 6)

            ffn(0, True, False)
            with g.Fori(1, NI - 1) as i:
                ffn(i, False, False)
            ffn(NI - 1, False, True)
            g.wait_ge(conv_g, 8 * 2 * NI)
            for n in range(NC):
                sums(NC + n, n, down_bank_free, NG * (NI - 1) + DB, scratch=ln2_scratch, squares=False)


def _tiles(w, rows, cols):
    return w.reshape(rows, P, cols, P).transpose(2, 1, 0, 3).reshape(cols, P, rows * P)


def _col(v):
    return v.reshape(-1, P).T


def kernel(x, c, ctx, c_ctx, w_ada, b_ada, w_in, conv_w, conv_b, conv_ln_g, conv_ln_b, rg_conv_w, rg_conv_b,
           rg_wa, rg_ba, rg_wx, rg_bx, rg_lambda, w_out, ln1_g, ln1_b, ffn_up, ffn_dw, ffn_dw_b, ffn_down,
           ln2_g, ln2_b):
    import concourse.bacc as bacc
    import numpy as np
    from concourse.bass_utils import run_bass_kernel_spmd

    A = np.asarray
    x, c, ctx, c_ctx = A(x), A(c), A(ctx), A(c_ctx)
    par = np.zeros((P, NPAR), x.dtype)

    def put(name, a):
        at, n = COLS[name]
        par[:, at:at + n] = np.ascontiguousarray(a).reshape(P, n)

    put("b_ada", _col(A(b_ada)[0]))
    pj = np.zeros((P, GT, PJ_N), x.dtype)
    pj[:, :, PJ_CONV:PJ_CONVB] = A(conv_w)[0].reshape(CONV_K, GT, P).transpose(2, 1, 0)
    pj[:, :, PJ_CONVB] = _col(A(conv_b)[0])
    pj[:, :, PJ_RG:PJ_RGB] = A(rg_conv_w)[0].reshape(RG_K, GT, P).transpose(2, 1, 0)
    pj[:, :, PJ_RGB] = _col(A(rg_conv_b)[0])
    for d in range(2):
        pj[:, :, PJ_GB + 2 * d] = _col(A(rg_ba)[0, d])
        pj[:, :, PJ_GB + 2 * d + 1] = _col(A(rg_bx)[0, d])
        pj[:, :, PJ_TH + d] = _col(A(rg_lambda)[0, d])
    put("pj", pj)
    for name, a in (("cln_g", conv_ln_g), ("cln_b", conv_ln_b), ("ln1_g", ln1_g), ("ln1_b", ln1_b),
                    ("ln2_g", ln2_g), ("ln2_b", ln2_b)):
        put(name, _col(A(a)[0]))
    taps = np.zeros((P, NP, 2, 10), x.dtype)
    taps[:, :, :, 0:9] = A(ffn_dw)[0].reshape(9, 2, NP, P).transpose(3, 2, 1, 0)
    taps[:, :, :, 9] = A(ffn_dw_b)[0].reshape(2, NP, P).transpose(2, 1, 0)

    gate = np.zeros((GT, P, 4, P), x.dtype)
    for d in range(2):
        for g, w in enumerate((A(rg_wa), A(rg_wx))):
            w2 = w[0, d].reshape(GT, 2, 64, 64)
            for h in range(2):
                gate[:, 64 * h:64 * h + 64, 2 * d + g, 64 * h:64 * h + 64] = w2[:, h]

    arrays = {
        "xT": x[0].T.reshape(KT, P, T),
        "ctxT": ctx[0].T.reshape(KT, P, TC).transpose(1, 0, 2),
        "par": par,
        "w_ada": A(w_ada)[0].T.reshape(ADA_G * KT, P, D),
        "w_in": _tiles(A(w_in)[0], KT, 4 * GT),
        "w_gate": gate,
        "w_out": _tiles(A(w_out)[0], KT, KT),
        "w_up": _tiles(A(ffn_up)[0], KT, 2 * NP),
        "w_down": A(ffn_down)[0].reshape(NP, P, D),
        "ffn_taps": taps.transpose(1, 0, 2, 3).reshape(NP, P, TAP_N),
        "c_rows": np.broadcast_to(np.stack([c[0], c_ctx]), (P, 2, D)),
    }
    nc = bacc.Bacc("TRN2", target_bir_lowering=False, num_devices=1, dynamic_dma_scratch_size=64)
    feeds, args = {}, []
    for name, a in arrays.items():
        feeds[name] = np.ascontiguousarray(a)
        args.append(nc.dram_tensor(name, a.shape, F32, kind="ExternalInput").ap())
    args.append(nc.dram_tensor("outT", (KT, P, T), F32, kind="ExternalOutput").ap())
    hybrid_layer(nc, *args)
    r = run_bass_kernel_spmd(nc, [feeds], core_ids=[0])
    out = np.asarray(r.results[0]["outT"]).reshape(D, T).T
    return np.ascontiguousarray(out).reshape(1, T, D)
```

```python
from contextlib import ExitStack

import concourse.bass as bass
from concourse import mybir

P = 128
D = 1024
T = 2048
TC = 256
GRID_W = 64
ROWS = T // GRID_W
KT = D // P
CH = 512
NC = T // CH
CW = 512
GT = CW // P
F = 2816
NP = F // P
CONV_K = 31
PAD = (CONV_K - 1) // 2
RG_K = 4
RG_L = RG_K // 2
RG_R = RG_K - 1 - RG_L
ALPHA = 2.0 ** 0.25
EPS = 1e-5

F32 = mybir.dt.float32
F16 = mybir.dt.float16
BF16 = mybir.dt.bfloat16
I32 = mybir.dt.int32
ALU = mybir.AluOpType
ACT = mybir.ActivationFunctionType

ADA_G = 6
PJ_CONV, PJ_CONVB, PJ_RG, PJ_RGB, PJ_GB, PJ_TH, PJ_EX = 0, 31, 32, 36, 37, 41, 43
PJ_N = 45
TAP_N = 20
COLS = {}
_at = 0
for _name, _n in (("b_ada", ADA_G * KT), ("pj", GT * PJ_N), ("cln_g", GT), ("cln_b", GT), ("ln1_g", KT),
                  ("ln1_b", KT), ("ln2_g", KT), ("ln2_b", KT)):
    COLS[_name] = (_at, _n)
    _at += _n
NPAR = _at

W_HCTX = 0
W_RXP = W_HCTX + KT * TC
RXP = RG_L + TC + RG_R + RG_L + T + RG_R
W_SLOT = W_RXP + RXP
NSLOT = 3
TAPS_RG, TAPS_CONV, TAPS_END, TAPS_UNIT, TAPS_RX = 3, 8, 15, 20, 27
TAPS_SHARED = 6
CONV_TAPS_ALL = CONV_K * GT - TAPS_SHARED + 1
W_XR = W_SLOT + NSLOT * D
W_TR = W_XR + TC + T
W_TI = W_TR + TC + T
W_S = W_TI + TC + T
W_G = W_S + TC + T
W_UP = W_G + T
UP = PAD + T + PAD
W_GW = W_UP + UP
W_LAND = W_GW + 4 * P
W_N = W_LAND + 2 * D
ZR, ZC = ROWS + 2, GRID_W + 2
F_ZU = 0
F_ZG = F_ZU + ZR * ZC
F_YUA = F_ZG + ZR * ZC
F_YUB = F_YUA + T
F_ACTA = F_YUB + T
F_YG = F_ACTA + T
F_ACT16 = F_YG + T
F_UP16 = F_ACT16 + 2 * T
F_DOWN16 = F_UP16 + 2 * D
NI = NP // 2
NG = NC * KT
DB = 3
SCALE_TOP = (200 << 23)
SCALE_TOP_DOUBLE = (199 << 23)
EXPONENT = 0x7F800000
INVERSE = (254 << 23)


def hybrid_layer(nc, xT, ctxT, par, w_ada, w_in, w_gate, w_out, w_up, w_down, ffn_taps, c_rows, outT):
    AFFINE_STEP = 36
    with ExitStack() as cx:
        def sb(name, shape, dtype=F32):
            return cx.enter_context(nc.sbuf_tensor(name, shape, dtype))

        def sem(name):
            return cx.enter_context(nc.semaphore(name))

        stream = sb("stream", [P, KT, T])
        side = sb("side", [P, KT, T])
        work = sb("work", [P, W_N])
        pars = sb("pars", [P, NPAR])
        mod_raw = sb("mod_raw", [P, 2 * KT, 2])
        ada_sum = sb("ada_sum", [P, KT])
        mod0 = sb("mod0", [P, 2, KT, 2])
        mod_of = sb("mod_of", [P, NC + 1, 2, KT])
        mod_junk = sb("mod_junk", [P, 2, KT])
        mod_sumsq = sb("mod_sumsq", [P, 2])
        mod_bound = sb("mod_bound", [P, 2])
        x_sumsq = sb("x_sumsq", [P, NC + 1])
        h_bound = sb("h_bound", [P, 1])
        h_pow = sb("h_pow", [P, 1], I32)
        h_inv = sb("h_inv", [P, NC + 1], I32)
        in_sumsq = sb("in_sumsq", [P, 1])
        in_scale = sb("in_scale", [P, 1], I32)
        in_inv_w = sb("in_inv_w", [P, 1], I32)
        in_inv = sb("in_inv", [P, 4, NC + 1])
        mods = sb("mods", [P, 4, KT])
        mean_of_group = sb("mean_of_group", [P, P])
        mean_of_model = sb("mean_of_model", [P, P])
        pj_now = sb("pj_now", [P, PJ_N])
        pj_prev = sb("pj_prev", [P, PJ_N])
        sp = sb("sp", [P, 5, GT, 2])
        g1s = sb("g1s", [P, KT])
        g2s = sb("g2s", [P, KT])
        h2_scale = sb("h2_scale", [P, KT])
        h2_bias = sb("h2_bias", [P, KT])
        eps_now = sb("eps_now", [P, 2])
        g2_now = sb("g2_now", [P, KT])
        tap_now = sb("tap_now", [P, 2, TAP_N])
        w_sumsq = sb("w_sumsq", [P, 2])
        act_sumsq = sb("act_sumsq", [P, 2])
        h2_sumsq = sb("h2_sumsq", [P, 2])
        bound_junk = sb("bound_junk", [P, 2, KT])
        half_bits = sb("half_bits", [P, 1], I32)
        up_scale = sb("up_scale", [P, 1], I32)
        down_scale = sb("down_scale", [P, 1], I32)
        act_scale = sb("act_scale", [P, 1], I32)
        h2_pow = sb("h2_pow", [P, 1], I32)
        up_inv = sb("up_inv", [P, 2], I32)
        down_inv = sb("down_inv", [P, 1], I32)
        act_inv = sb("act_inv", [P, 1], I32)
        h2_inv = sb("h2_inv", [P, 1], I32)
        ps = cx.enter_context(nc.psum_tensor("ps", [P, 8, CH], F32))

        def par_of(name):
            at, n = COLS[name]
            return pars[:, at:at + n]

        b_ada = par_of("b_ada").rearrange("p (g k) -> p g k", k=KT)
        pj = par_of("pj").rearrange("p (j c) -> p j c", c=PJ_N)
        cln_g, cln_b = par_of("cln_g"), par_of("cln_b")
        ln_g = {1: par_of("ln1_g"), 2: par_of("ln2_g")}
        ln_b = {1: par_of("ln1_b"), 2: par_of("ln2_b")}
        streamc = stream[:].rearrange("p k (n f) -> p k n f", f=CH)
        sidec = side[:].rearrange("p k (n f) -> p k n f", f=CH)
        ada_w = side[:].rearrange("p k (t c) -> p (k t) c", c=D)

        def area(at, n):
            return work[:, at:at + n]

        silu_rows = area(W_LAND, 2 * D).rearrange("p (c k) -> p c k", k=D)
        ada_junk = [area(W_TR + i * D, D) for i in range(4)]
        ada_prod = [area(W_TI + TC + T + i * D, D) for i in range(2)]
        h_ctx = area(W_HCTX, KT * TC).rearrange("p (k t) -> p k t", t=TC)
        slot = [area(W_SLOT + s * D, D) for s in range(NSLOT)]
        in16 = [area(at, D).bitcast(F16).rearrange("p (two f) -> p two f", two=2)
                for at in (W_SLOT + 2 * D, W_LAND + D)]
        stream16 = stream[:].bitcast(F16).rearrange("p k (n two f) -> p k n two f", two=2, f=CH)
        ctx16 = area(W_HCTX, KT * TC).bitcast(F16).rearrange("p (k two f) -> p k two f", two=2, f=TC)
        shared_sum = area(W_HCTX, T)
        shared_tap = [area(W_RXP, T), area(W_SLOT, T)]
        h_tmp = [area(W_G + i * CH, CH) for i in range(4)]
        gate_w = area(W_GW, 4 * P).rearrange("p (g m) -> p g m", m=P)
        rxp = area(W_RXP, RXP)
        LAT0 = RG_L + TC + RG_R
        rx_ctx = rxp[:, RG_L:RG_L + TC]
        rx_lat = rxp[:, LAT0 + RG_L:LAT0 + RG_L + T]
        xr = area(W_XR, TC + T)
        tr, ti, sq = area(W_TR, TC + T), area(W_TI, TC + T), area(W_S, TC + T)
        gelu_rg = area(W_G, T)
        upad = area(W_UP, UP)
        wo_at = [W_HCTX, W_HCTX + D, W_RXP, W_RXP + D, W_SLOT, W_SLOT + D, W_SLOT + 2 * D, W_XR]
        wo = [area(a, D) for a in wo_at]
        lsq = area(W_TR, KT * CH).rearrange("p (k f) -> p k f", f=CH)
        lsum, lsqs, lr0, lr = (area(W_TR + (KT + i) * CH, CH) for i in range(4))
        csq = area(W_UP, GT * CH).rearrange("p (k f) -> p k f", f=CH)
        cr0, cr = area(W_XR + D, CH), area(W_XR + D + CH, CH)
        h2_f32 = [area(W_TR + (KT + 4) * CH, CH), area(W_GW, CH)]
        ln1_scratch = (lsq, lsum, lsqs, lr0, lr)
        side16 = side[:].bitcast(F16).rearrange("p k (n two f) -> p k n two f", two=2, f=CH)

        def pair16(at, n):
            return area(at, 2 * n).bitcast(F16).rearrange("p (q two f) -> p q two f", two=2, f=n)

        zu = area(F_ZU, ZR * ZC).rearrange("p (r c) -> p r c", c=ZC)
        zg = area(F_ZG, ZR * ZC).rearrange("p (r c) -> p r c", c=ZC)
        yu = [area(F_YUA, T), area(F_YUB, T)]
        yg = area(F_YG, T)
        act = [area(F_ACTA, T), yu[1]]
        act16, up16, down16 = pair16(F_ACT16, T), pair16(F_UP16, D), pair16(F_DOWN16, D)
        land = [area(W_LAND, D), area(W_LAND + D, D)]
        lsq2 = area(F_ZU, KT * CH).rearrange("p (k f) -> p k f", f=CH)
        ln2_scratch = (lsq2,) + tuple(area(F_YUA + i * CH, CH) for i in range(4))

        par_loaded = sem("par_loaded")
        ctx_loaded = sem("ctx_loaded")
        gatew_loaded = sem("gatew_loaded")
        stored = sem("stored")
        consts = sem("consts")
        pads = sem("pads")
        prep_step = sem("prep_step")
        scan_step = sem("scan_step")
        rows_loaded = sem("rows_loaded")
        silu_done = sem("silu_done")
        ada_c = sem("ada_c")
        ada_ctx_prod = sem("ada_ctx_prod")
        ada_ctx_sum = sem("ada_ctx_sum")
        ada_prod_done = sem("ada_prod_done")
        ada_sum_done = sem("ada_sum_done")
        ctx_mod_done = sem("ctx_mod_done")
        mod_done = sem("mod_done")
        prep = sem("prep")
        mod_square = sem("mod_square")
        mod_sum_mm = sem("mod_sum_mm")
        mod_bound_step = sem("mod_bound_step")
        x_square = sem("x_square")
        x_sum_mm = sem("x_sum_mm")
        h_scale_step = sem("h_scale_step")
        h_tmp_ready = sem("h_tmp_ready")
        h_hi = sem("h_hi")
        h_lo = sem("h_lo")
        in_square = sem("in_square")
        in_sum_mm = sem("in_sum_mm")
        in_scale_step = sem("in_scale_step")
        in_hi = sem("in_hi")
        in_lo = sem("in_lo")
        jp_ready = sem("jp_ready")
        jp_kept = sem("jp_kept")
        cg_mm = sem("cg_mm")
        cv_mm = sem("cv_mm")
        rx_mm = sem("rx_mm")
        rg_mm = sem("rg_mm")
        gate_mm = sem("gate_mm")
        cg_evac = sem("cg_evac")
        cv_evac = sem("cv_evac")
        rx_evac = sem("rx_evac")
        rg_evac = sem("rg_evac")
        gate_evac = sem("gate_evac")
        conv_tap = sem("conv_tap")
        shared_tap_made = sem("shared_tap_made")
        shared_tap_added = sem("shared_tap_added")
        rg_tap = sem("rg_tap")
        rg_act = sem("rg_act")
        unit_step = sem("unit_step")
        ti_step = sem("ti_step")
        rg_first = sem("rg_first")
        unit_done = sem("unit_done")
        mix_step = sem("mix_step")
        cmean_mm = sem("cmean_mm")
        cvar_mm = sem("cvar_mm")
        csub = sem("csub")
        csquare = sem("csquare")
        clog = sem("clog")
        cexp = sem("cexp")
        cnewton = sem("cnewton")
        cnorm = sem("cnorm")
        csilu = sem("csilu")
        out_mm = sem("out_mm")
        out_evac = sem("out_evac")
        psum_step = sem("psum_step")
        mean_mm = sem("mean_mm")
        lsub = sem("lsub")
        lsquare = sem("lsquare")
        qsum_step = sem("qsum_step")
        var_mm = sem("var_mm")
        llog = sem("llog")
        lexp = sem("lexp")
        lnewton = sem("lnewton")
        lnorm = sem("lnorm")
        h2_ready = sem("h2_ready")
        h2_hi = sem("h2_hi")
        x1_ready = sem("x1_ready")
        zpads = sem("zpads")
        down_mm = sem("down_mm")
        first_u = sem("first_u")
        first_g = sem("first_g")
        conv_u = sem("conv_u")
        conv_g = sem("conv_g")
        gelu_done = sem("gelu_done")
        bound_sq = sem("bound_sq")
        bound_mm = sem("bound_mm")
        h2_scaled = sem("h2_scaled")
        land_u_loaded = sem("land_u_loaded")
        land_g_loaded = sem("land_g_loaded")
        tap_a_loaded = sem("tap_a_loaded")
        tap_b_loaded = sem("tap_b_loaded")
        w_square = sem("w_square")
        w_sum_mm = sem("w_sum_mm")
        up_scale_step = sem("up_scale_step")
        down_scale_step = sem("down_scale_step")
        w_hi = sem("w_hi")
        w_lo = sem("w_lo")
        up_mm = sem("up_mm")
        z_evac = sem("z_evac")
        act_square = sem("act_square")
        act_sum_mm = sem("act_sum_mm")
        act_scale_step = sem("act_scale_step")
        act_hi = sem("act_hi")
        act_lo = sem("act_lo")
        act_a_done = sem("act_a_done")
        act_b_done = sem("act_b_done")
        down_bank_free = sem("down_bank_free")
        h2_lo = sem("h2_lo")
        out_ready = sem("out_ready")
        ada_loaded = [sem(f"ada_loaded{i}") for i in range(4)]
        x_loaded = [sem(f"x_loaded{i}") for i in range(NC)]
        xr_loaded = [sem(f"x_again{i}") for i in range(NC)]
        slot_loaded = [sem(f"slot_loaded{i}") for i in range(2)]
        wo_loaded = [sem(f"wo_loaded{i}") for i in range(KT)]


        TILES = ("cg", "cv", "rx", "rg")
        USES = TILES + tuple(f"ada{t}" for t in range(KT))
        SLOT = {"cg": 0, "cv": 1, "rx": 0, "rg": 1} | {f"ada{t}": t // 5 for t in range(KT)}

        def used(u, j):
            if u[:3] == "ada":
                return ada_sum_done, KT * j + int(u[3:]) + 1
            return in_lo, 4 * j + TILES.index(u) + 1

        def landed(u, j):
            return slot_loaded[SLOT[u]], 16 * (len(loads[SLOT[u]]) * j + nth[u])

        loads = [[u for u in USES if SLOT[u] == q] for q in range(2)]
        before = {}
        for q in range(2):
            for i, u in enumerate(loads[q]):
                before[u] = (loads[q][i - 1], i > 0)
        nth = {u: loads[SLOT[u]].index(u) + 1 for u in USES}
        N_IN = {"cv": 0, "cg": GT, "rx": 2 * GT, "rg": 3 * GT}

        block = cx.enter_context(nc.Block())

        @block.sync
        def _(sp_):
            sp_.dma_start(silu_rows, c_rows).then_inc(rows_loaded, 16)
            sp_.dma_start(pars[:], par).then_inc(par_loaded, 16)
            for i in range(4):
                sp_.dma_start(ada_w[:, 4 * i:4 * i + 4, :], w_ada[4 * i:4 * i + 4].rearrange("t p c -> p t c"))\
                   .then_inc(ada_loaded[i], 16)

            def load_slot(u, j, first):
                prev, same = before[u]
                if same:
                    sp_.wait_ge(*used(prev, j))
                elif not first:
                    sp_.wait_ge(*used(prev, j - 1))
                if u[:3] == "ada":
                    src = w_ada[2 * KT + j * KT + int(u[3:])]
                else:
                    src = w_in[N_IN[u] + j]
                sp_.dma_start(slot[SLOT[u]], src).then_inc(slot_loaded[SLOT[u]], 16)

            load_slot("cg", 0, True)
            load_slot("cv", 0, True)
            for n in range(NC):
                sp_.dma_start(streamc[:, :, n, :], xT[:, :, n * CH:(n + 1) * CH].rearrange("k p t -> p k t"))\
                   .then_inc(x_loaded[n], 16)
            sp_.dma_start(h_ctx, ctxT).then_inc(ctx_loaded, 16)

            def mixer_loads(j, first, last):
                if not first:
                    load_slot("cv", j, first)
                load_slot("rx", j, first)
                load_slot("rg", j, first)
                if not first:
                    sp_.wait_ge(gate_mm, 20 * j)
                sp_.dma_start(gate_w, w_gate[j]).then_inc(gatew_loaded, 16)
                for t in range(5):
                    load_slot(f"ada{t}", j, first)
                if not last:
                    load_slot("cg", j + 1, False)
                for t in range(5, KT):
                    load_slot(f"ada{t}", j, first)

            mixer_loads(0, True, False)
            sp_.dma_start(tap_now[:, 0, :], ffn_taps[0]).then_inc(tap_a_loaded, 16)
            sp_.dma_start(tap_now[:, 1, :], ffn_taps[1]).then_inc(tap_b_loaded, 16)
            with sp_.Fori(1, GT - 1) as j:
                mixer_loads(j, False, False)
            mixer_loads(GT - 1, False, True)
            sp_.wait_ge(rg_mm, NC * GT)
            for n in range(NC):
                sp_.dma_start(streamc[:, :, n, :], xT[:, :, n * CH:(n + 1) * CH].rearrange("k p t -> p k t"))\
                   .then_inc(xr_loaded[n], 16)
            sp_.dma_start(wo[6], w_out[6]).then_inc(wo_loaded[6], 16)
            sp_.wait_ge(ada_sum_done, KT * GT)
            sp_.dma_start(land[0], w_up[0]).then_inc(land_u_loaded, 16)
            sp_.dma_start(land[1], w_up[NP]).then_inc(land_g_loaded, 16)
            sp_.wait_ge(unit_done, 2 * GT)
            sp_.dma_start(wo[7], w_out[7]).then_inc(wo_loaded[7], 16)
            sp_.wait_ge(conv_tap, CONV_TAPS_ALL)
            for m in range(6):
                sp_.dma_start(wo[m], w_out[m]).then_inc(wo_loaded[m], 16)
            def land_pair(src_u, src_g, p):
                for q, (src, done) in enumerate(((src_u, land_u_loaded), (src_g, land_g_loaded))):
                    sp_.wait_ge(w_lo, 2 * (p - 1) + q + 1)
                    sp_.dma_start(land[q], src).then_inc(done, 16)

            def ffn_loads(i, last):
                land_pair(w_up[2 * i + 1], w_up[NP + 2 * i + 1], 3 * i + 1)
                land_pair(w_down[2 * i], w_down[2 * i + 1], 3 * i + 2)
                if not last:
                    land_pair(w_up[2 * i + 2], w_up[NP + 2 * i + 2], 3 * i + 3)
                    sp_.wait_ge(conv_g, 8 * (2 * i + 1))
                    sp_.dma_start(tap_now[:, 0, :], ffn_taps[2 * i + 2]).then_inc(tap_a_loaded, 16)
                    sp_.wait_ge(conv_g, 8 * (2 * i + 2))
                    sp_.dma_start(tap_now[:, 1, :], ffn_taps[2 * i + 3]).then_inc(tap_b_loaded, 16)

            ffn_loads(0, False)
            with sp_.Fori(1, NI - 1) as i:
                ffn_loads(i, False)
            ffn_loads(NI - 1, True)
            for n in range(NC):
                sp_.wait_ge(out_ready, KT * (n + 1))
                sp_.dma_start(outT[:, :, n * CH:(n + 1) * CH].rearrange("k p t -> p k t"), streamc[:, :, n, :])\
                   .then_inc(stored, 16)
            sp_.wait_ge(stored, 16 * NC)

        @block.tensor
        def _(pe):
            def products(out, w16, x16, start, stop):
                for q, (a, b) in enumerate(((0, 0), (0, 1), (1, 0))):
                    mm = pe.matmul(out, w16[:, a], x16[:, b], start=start and q == 0, stop=stop and q == 2)
                return mm

            def in_sum(u, j):
                pe.wait_ge(in_square, 4 * j + TILES.index(u) + 1)
                pe.matmul(ps[:, 7, 0:1], mean_of_model[:], in_sumsq[:], start=True, stop=True).then_inc(in_sum_mm, 1)

            def x_sum(n):
                pe.wait_ge(x_square, n + 1)
                if n > 1:
                    pe.wait_ge(h_scale_step, 6 * (n - 2) + 1)
                pe.matmul(ps[:, 5 + n % 2, 0:1], mean_of_model[:], x_sumsq[:, n:n + 1], start=True, stop=True)\
                  .then_inc(x_sum_mm, 1)

            def mod_sum(cc):
                pe.wait_ge(mod_square, 2 * cc + 2)
                if cc:
                    pe.wait_ge(mod_bound_step, 2)
                pe.matmul(ps[:, 4, 0:2], mean_of_model[:], mod_sumsq[:], start=True, stop=True).then_inc(mod_sum_mm, 1)

            def tile(u, j, first, evac, evac_at, done, after=None):
                pe.wait_ge(in_lo, 4 * j + TILES.index(u) + 1)
                for n in range(NC):
                    if evac is not None:
                        pe.wait_ge(evac, evac_at + n)
                    if u == "cg" and first:
                        pe.wait_ge(h_lo, KT * (n + 1))
                    for k in range(KT):
                        mm = products(ps[:, n, :], in16[TILES.index(u) % 2][:, :, k * P:(k + 1) * P],
                                      stream16[:, k, n], k == 0, k == KT - 1)
                    mm.then_inc(done, 1)
                    if after is not None:
                        after(n)

            def gates(j, d, first, last=False):
                for i in range(10):
                    q = 10 * d + i
                    if q == 3:
                        pe.wait_ge(in_scale_step, 20 * j + (16 if last else 21))
                    if q == 11:
                        pe.wait_ge(in_scale_step, 20 * j + (20 if last else 26))
                    if not (first and q < 4):
                        pe.wait_ge(gate_evac, 20 * j + q - 3)
                    at, n = (0, TC) if i % 5 == 0 else (TC + (i % 5 - 1) * CH, CH)
                    pe.matmul(ps[:, 4 + q % 4, 0:n], gate_w[:, 2 * d + i // 5, :], xr[:, at:at + n],
                              start=True, stop=True).then_inc(gate_mm, 1)

            def mixer(j, first, last):
                def in_cg(n):
                    if first:
                        if n < 3:
                            x_sum(n + 2)
                        if n == 2:
                            mod_sum(1)
                            in_sum("cv", j)
                    if n == 1 and not first:
                        pe.wait_ge(gate_evac, 20 * j - 10)
                        in_sum("cv", j)

                def in_cv(n):
                    if n == 0:
                        if not first:
                            pe.wait_ge(gate_evac, 20 * j)
                        in_sum("rx", j)

                def in_rx(n):
                    if n == 0:
                        in_sum("rg", j)

                def in_rg(n):
                    if n == 1 and not last:
                        in_sum("cg", j + 1)

                tile("cg", j, first, None if first else rg_evac, 4 * j - 3, cg_mm, in_cg)
                if not first:
                    gates(j - 1, 1, first)
                tile("cv", j, first, cg_evac, 4 * j + 1, cv_mm, in_cv)
                pe.wait_ge(in_lo, 4 * j + 3)
                if first:
                    pe.wait_ge(h_lo, KT * (NC + 1))
                for k in range(KT):
                    mm = products(ps[:, 4, 0:TC], in16[0][:, :, k * P:(k + 1) * P], ctx16[:, k], k == 0, k == KT - 1)
                mm.then_inc(rx_mm, 1)
                tile("rx", j, first, cv_evac, 4 * j + 1, rx_mm, in_rx)
                tile("rg", j, first, rx_evac, 5 * j + 2, rg_mm, in_rg)
                pe.wait_ge(gatew_loaded, 16 * (j + 1))
                pe.wait_ge(rg_tap, 6 * (j + 1))
                if first:
                    pe.wait_ge(rx_evac, 5)
                gates(j, 0, first, last)

            pe.wait_ge(consts, 2)
            mod_sum(0)
            in_sum("cg", 0)
            x_sum(0)
            x_sum(1)
            mixer(0, True, False)
            with pe.Fori(1, GT - 1) as j:
                mixer(j, False, False)
            mixer(GT - 1, False, True)
            gates(GT - 1, 1, False, True)

            def sum_pair(sumsq, col, squared, at, done):
                pe.wait_ge(squared, at)
                pe.matmul(ps[:, 7, col:col + 1], mean_of_model[:], sumsq[:, 0:1], start=True, stop=False)
                pe.matmul(ps[:, 7, col:col + 1], mean_of_model[:], sumsq[:, 1:2], start=False, stop=True)\
                  .then_inc(done, 1)

            def conv_stats(n, which):
                src = sidec[:, 0:GT, n, :] if which == 0 else csq
                for c in range(GT):
                    mm = pe.matmul(ps[:, 4 + which, :], mean_of_group[:], src[:, c, :],
                                   start=(c == 0), stop=(c == GT - 1))
                mm.then_inc((cmean_mm, cvar_mm)[which], 1)

            def out_half(n, m, group):
                for k in range(GT):
                    kk = GT * group + k
                    mm = pe.matmul(ps[:, m % 4, :], wo[m][:, kk * P:(kk + 1) * P], sidec[:, kk, n, :],
                                   start=(group == 1 and k == 0), stop=(group == 0 and k == GT - 1))
                if group == 0:
                    mm.then_inc(out_mm, 1)

            def early_half(m):
                pe.wait_ge(unit_done, 2 * GT)
                pe.wait_ge(rg_evac, NC * GT)
                pe.wait_ge(wo_loaded[m], 16)
                out_half(0, m, 1)

            def chunk(n, conv, out, norm, first=False):
                for m in range(KT):
                    if out:
                        if m == 0:
                            pe.wait_ge(csilu, GT * (n + 1))
                        if not (first and m < 4):
                            if first:
                                pe.wait_ge(wo_loaded[m], 16)
                            pe.wait_ge(out_evac, KT * n + m - 3)
                            out_half(n, m, 1)
                        out_half(n, m, 0)
                    if m == 0 and conv and not first:
                        if out:
                            pe.wait_ge(csub, GT * (n + 1))
                        conv_stats(n + 1, 0)
                        if not out:
                            early_half(0)
                    if m == 1 and norm:
                        pe.wait_ge(psum_step, (KT - 1) * (n))
                        pe.matmul(ps[:, 6, :], mean_of_model[:], lsum, start=True, stop=True).then_inc(mean_mm, 1)
                    if m == 3 and conv:
                        pe.wait_ge(csquare, GT * (n + 2))
                        if out:
                            pe.wait_ge(cnewton, 4 * (n + 1))
                        conv_stats(n + 1, 1)
                    if m == 4 and norm:
                        pe.wait_ge(qsum_step, (KT - 1) * (n))
                        pe.matmul(ps[:, 7, :], mean_of_model[:], lsqs, start=True, stop=True).then_inc(var_mm, 1)

            pe.wait_ge(gate_evac, 20 * GT)
            pe.wait_ge(conv_tap, CONV_TAPS_ALL)
            chunk(-1, True, False, False)
            sum_pair(h2_sumsq, 0, bound_sq, 2, bound_mm)
            pe.wait_ge(h2_scaled, 1)
            sum_pair(w_sumsq, 1, w_square, 2, w_sum_mm)
            for m in (1, 2, 3):
                early_half(m)
            pe.wait_ge(csub, GT)
            conv_stats(1, 0)
            chunk(0, True, True, False, first=True)
            with pe.Fori(1, NC - 1) as n:
                chunk(n, True, True, True)
            chunk(NC - 1, False, True, True)

            def variance(q, bank, squares):
                for m in range(KT):
                    pe.wait_ge(lsquare, KT * q + m + 1)
                    mm = pe.matmul(ps[:, bank, :], mean_of_model[:], squares[:, m, :],
                                   start=(m == 0), stop=(m == KT - 1))
                mm.then_inc(var_mm, 1)

            def up(i, q, n, first):
                if n == 0:
                    pe.wait_ge(w_lo, (6 * i, 6 * i + 2)[q // 2] + q % 2 + 1)
                if first and q == 0:
                    pe.wait_ge(h2_lo, KT * (n + 1))
                    if n == 0:
                        pe.wait_ge(out_evac, KT * NC)
                else:
                    pe.wait_ge(z_evac, 4 * (4 * i + q - 1) + n + 1)
                for k in range(KT):
                    mm = products(ps[:, n, :], up16[:, q % 2, :, k * P:(k + 1) * P], side16[:, k, n],
                                  k == 0, k == KT - 1)
                mm.then_inc(up_mm, 1)

            def down(i, g):
                n, m = g // KT, g % KT
                pe.wait_ge(down_bank_free, NG * i + max(g + 1, DB))
                if g == 0:
                    pe.wait_ge(w_lo, 6 * i + 6)
                    pe.wait_ge(act_lo, 2 * (i + 1))
                for q in range(2):
                    mm = products(ps[:, 4 + g % DB, :],
                                  down16[:, q, :, m * P:(m + 1) * P], act16[:, q, :, n * CH:(n + 1) * CH],
                                  q == 0, q == 1)
                mm.then_inc(down_mm, 1)

            def ffn(i, first, last):
                for n in range(NC):
                    up(i, 0, n, first)
                    if first and n == 0:
                        pe.wait_ge(psum_step, (KT - 1) * NC)
                        pe.matmul(ps[:, 6, :], mean_of_model[:], lsum, start=True, stop=True).then_inc(mean_mm, 1)
                    if first and n == 1:
                        variance(NC - 1, 7, lsq)
                for n in range(NC):
                    up(i, 1, n, first)
                    if n == 0 and first:
                        pe.wait_ge(lnewton, 4 * NC)
                    if n == 1 and not first:
                        sum_pair(act_sumsq, 2, act_square, 2 * i, act_sum_mm)
                    if n == 2:
                        if not first:
                            pe.wait_ge(act_scale_step, 5 * (i - 1) + 1)
                        sum_pair(w_sumsq, 0, w_square, 6 * i + 4, w_sum_mm)
                if not first and not last:
                    for g in range(NG):
                        down(i - 1, g)
                for n in range(NC):
                    up(i, 2, n, first)
                    if n == 0 and not last:
                        sum_pair(w_sumsq, 1, w_square, 6 * i + 6, w_sum_mm)
                for n in range(NC):
                    up(i, 3, n, first)
                    if n == 0 and not last:
                        sum_pair(w_sumsq, 0, w_square, 6 * i + 8, w_sum_mm)
                if last:
                    for g in range(NG):
                        if g == NG // 2:
                            sum_pair(w_sumsq, 1, w_square, 6 * i + 6, w_sum_mm)
                        down(i - 1, g)

            ffn(0, True, False)
            with pe.Fori(1, NI - 1) as i:
                ffn(i, False, False)
            ffn(NI - 1, False, True)
            sum_pair(act_sumsq, 2, act_square, 2 * NI, act_sum_mm)
            pe.wait_ge(z_evac, 4 * 4 * NI)
            for n in range(NC + 1):
                for m in range(KT):
                    if n < NC:
                        down(NI - 1, n * KT + m)
                    if n > 0 and m == (DB - 1 if n < NC else 0):
                        variance(NC + n - 1, 2 * ((n - 1) % 2) + 1, lsq2)
                if n < NC:
                    pe.wait_ge(psum_step, (KT - 1) * (NC + n + 1))
                    if n > 1:
                        pe.wait_ge(lsub, KT * (NC + n - 1))
                    pe.matmul(ps[:, 2 * (n % 2), :], mean_of_model[:], ln2_scratch[1], start=True, stop=True)\
                      .then_inc(mean_mm, 1)

        @block.scalar
        def _(a):
            a.wait_ge(rows_loaded, 16)
            a.activation(silu_rows, silu_rows, ACT.Silu).then_inc(silu_done, 1)
            a.wait_ge(prep, 1)
            a.activation(sp[:, 1], sp[:, 0], ACT.Exp, scale=-1.0).then_inc(prep, 1)
            def ctx_sum(t):
                a.wait_ge(ada_ctx_prod, t + 1)
                a.activation(ada_prod[t % 2], ada_prod[t % 2], ACT.Copy, accum_out=mod_raw[:, t, 1:2])\
                 .then_inc(ada_ctx_sum, 1)

            def in_square_(u, j):
                w_ = TILES.index(u)
                a.wait_ge(*landed(u, j))
                a.activation(in16[w_ % 2][:, 0].bitcast(BF16), slot[SLOT[u]], ACT.Square,
                             accum_out=in_sumsq[:]).then_inc(in_square, 1)

            def in_high(u, j):
                w_ = TILES.index(u)
                a.wait_ge(in_scale_step, 5 * (4 * j + w_) + 3)
                a.activation(in16[w_ % 2][:, 0], slot[SLOT[u]], ACT.Copy, scale=in_scale[:].bitcast(F32))
                a.activation(slot[SLOT[u]], slot[SLOT[u]], ACT.Copy, scale=in_scale[:].bitcast(F32)).then_inc(in_hi, 1)

            def undo(u, j, n):
                w_ = TILES.index(u)
                a.wait_ge(in_scale_step, 5 * (4 * j + w_) + 5)
                return in_inv[:, w_, n:n + 1]

            def mod_squares(cc):
                if cc:
                    a.wait_ge(mod_sum_mm, 1)
                for g_ in (0, 1):
                    a.activation(mod_junk[:, g_], mod0[:, g_, :, cc], ACT.Square, accum_out=mod_sumsq[:, g_:g_ + 1])\
                     .then_inc(mod_square, 1)

            def x_square_(n):
                a.wait_ge(*((x_loaded[n], 16) if n < NC else (ctx_loaded, 16)))
                src = streamc[:, :, n, :] if n < NC else h_ctx
                if n > 0:
                    a.wait_ge(x_square, n)
                junk = area(W_XR, KT * CH // 2).bitcast(BF16).rearrange("p (k f) -> p k f", k=KT)
                a.activation(junk[:, :, 0:CH if n < NC else TC], src, ACT.Square, accum_out=x_sumsq[:, n:n + 1])\
                 .then_inc(x_square, 1)

            def h_high(n, between=None):
                for k in range(KT):
                    if k == KT // 2 and between is not None:
                        x_square_(between)
                    a.wait_ge(h_tmp_ready, KT * n + k + 1)
                    dst, f = (stream16[:, k, n, 0], CH) if n < NC else (ctx16[:, k, 0], TC)
                    a.activation(dst, h_tmp[k % 4][:, 0:f], ACT.Copy).then_inc(h_hi, 1)

            for t in range(KT):
                ctx_sum(t)
            in_square_("cg", 0)
            ctx_sum(KT)
            a.wait_ge(mod_done, 1)
            mod_squares(0)
            x_square_(0)
            in_high("cg", 0)
            ctx_sum(KT + 1)
            for n in range(NC):
                h_high(n, n + 1)
                for t in range(KT + 2 + 2 * n, min(KT + 4 + 2 * n, 2 * KT)):
                    ctx_sum(t)
                if n == NC - 2:
                    a.wait_ge(ctx_mod_done, 1)
                    mod_squares(1)
            in_square_("cv", 0)
            in_high("cv", 0)
            h_high(NC)

            pj_of = (pj_now, pj_prev)

            def unit(j, d):
                q = 2 * j + d
                pj_now = pj_of[d]
                a.wait_ge(gate_evac, 20 * j + 10 * d + 5)
                a.activation(sq, tr, ACT.Tanh, scale=pj_now[:, PJ_TH + d:PJ_TH + d + 1],
                             bias=pj_now[:, PJ_TH + d:PJ_TH + d + 1]).then_inc(rg_act, 1)
                a.wait_ge(rg_act, 3 * q + 1)
                a.activation(tr, tr, ACT.Exp, scale=pj_now[:, PJ_EX + d:PJ_EX + d + 1],
                             bias=pj_now[:, PJ_EX + d:PJ_EX + d + 1]).then_inc(rg_act, 1)
                a.activation(sq, sq, ACT.Sqrt, scale=0.25).then_inc(rg_act, 1)

            def gates(j, d, first):
                if not (first and d == 0):
                    a.wait_ge(unit_done, 2 * j + d)
                for i in range(10):
                    a.wait_ge(gate_mm, 20 * j + 10 * d + i + 1)
                    at, n = (0, TC) if i % 5 == 0 else (TC + (i % 5 - 1) * CH, CH)
                    dst = (tr, ti)[i // 5]
                    g = PJ_GB + 2 * d + i // 5
                    a.activation(dst[:, at:at + n], ps[:, 4 + (10 * d + i) % 4, 0:n], ACT.Tanh, scale=0.5,
                                 bias=pj_of[d][:, g:g + 1]).then_inc(gate_evac, 1)

            def ada_sums(j, lo, hi):
                for t in range(lo, hi):
                    s_ = slot[SLOT[f"ada{t}"]]
                    a.wait_ge(ada_prod_done, KT * j + t + 1)
                    a.activation(s_, s_, ACT.Copy, accum_out=ada_sum[:, t:t + 1]).then_inc(ada_sum_done, 1)

            def mixer(j, first, last):
                for n in range(NC):
                    if not first and n == 0:
                        a.wait_ge(rg_tap, 6 * j)
                    if not first and n == 3:
                        in_high("cv", j)
                    a.wait_ge(cg_mm, 4 * j + n + 1)
                    a.activation(rx_lat[:, n * CH:(n + 1) * CH], ps[:, n, :], ACT.Sigmoid,
                                 scale=undo("cg", j, n)).then_inc(cg_evac, 1)
                in_square_("rx", j)
                if not first:
                    backward(j - 1)
                in_high("rx", j)
                if not first:
                    a.wait_ge(mod_done, j + 1)
                ada_sums(j, 0, 1)
                a.wait_ge(cv_mm, 4 * j + 4)
                in_square_("rg", j)
                a.wait_ge(rx_mm, 5 * j + 1)
                a.activation(rx_ctx, ps[:, 4, 0:TC], ACT.Copy, scale=undo("rx", j, NC)).then_inc(rx_evac, 1)
                ada_sums(j, 1, 2)
                for n in range(NC):
                    a.wait_ge(cv_evac, 4 * j + n + 1)
                    a.wait_ge(rx_mm, 5 * j + n + 2)
                    a.activation(rx_lat[:, n * CH:(n + 1) * CH], ps[:, n, :], ACT.Copy,
                                 scale=undo("rx", j, n)).then_inc(rx_evac, 1)
                    if n == 1:
                        ada_sums(j, 2, 3)
                        in_high("rg", j)
                    if n == 2:
                        ada_sums(j, 3, 4)
                if not first:
                    a.wait_ge(unit_done, 2 * j)
                a.wait_ge(jp_ready, j + 1)
                a.wait_ge(rx_evac, 5 * (j + 1))
                for dst, src in ((xr[:, TC:TC + T], rxp[:, LAT0:LAT0 + T]), (xr[:, 0:TC], rxp[:, 0:TC])):
                    a.activation(dst, src, ACT.Identity, scale=pj_now[:, PJ_RG:PJ_RG + 1],
                                 bias=pj_now[:, PJ_RGB:PJ_RGB + 1]).then_inc(rg_first, 1)
                ada_sums(j, 4, 5)
                if not last:
                    in_square_("cg", j + 1)
                if not first:
                    a.wait_ge(unit_done, 2 * j)
                for n in range(NC):
                    a.wait_ge(rg_mm, 4 * j + n + 1)
                    a.activation(gelu_rg[:, n * CH:(n + 1) * CH], ps[:, n, :], ACT.Gelu_apprx_tanh,
                                 scale=undo("rg", j, n)).then_inc(rg_evac, 1)
                    if n == 1:
                        ada_sums(j, 5, 6)
                        if not last:
                            in_high("cg", j + 1)
                    if n == 2:
                        ada_sums(j, 6, 7)
                a.wait_ge(jp_ready, j + 1)
                gates(j, 0, first)
                ada_sums(j, 7, 8)
                if not last:
                    in_square_("cv", j + 1)
                unit(j, 0)

            def backward(j):
                a.wait_ge(jp_kept, j + 1)
                gates(j, 1, False)
                unit(j, 1)

            mixer(0, True, False)
            with a.Fori(1, GT - 1) as j:
                mixer(j, False, False)
            mixer(GT - 1, False, True)

            def shared_products(lo, hi):
                for i in range(lo, hi):
                    k = CONV_K - TAPS_SHARED + i
                    if i > 2:
                        a.wait_ge(shared_tap_added, i - 2)
                    a.activation(shared_tap[i % 2] if i else shared_sum, upad[:, k:k + T], ACT.Copy,
                                 scale=pj_now[:, k:k + 1]).then_inc(shared_tap_made, 1)

            a.wait_ge(cv_evac, NC * GT)
            a.wait_ge(rx_mm, 5 * GT)
            a.wait_ge(rg_tap, 6 * GT)
            shared_products(0, 4)
            a.wait_ge(jp_kept, GT)
            gates(GT - 1, 1, False)
            shared_products(4, 5)
            unit(GT - 1, 1)
            shared_products(5, 6)

            def chunk(n, conv, norm, later=True, between=None):
                if conv:
                    if n != -1:
                        a.wait_ge(cvar_mm, n + 1)
                    for c in range(GT):
                        a.wait_ge(csub, GT * (n + 1) + c + 1)
                        a.activation(csq[:, c, :], sidec[:, c, n + 1, :], ACT.Square).then_inc(csquare, 1)
                if between is not None:
                    between()
                if norm:
                    if later:
                        a.wait_ge(qsum_step, (KT - 1) * (n - 1))
                    for m in range(KT):
                        a.wait_ge(lsub, KT * (n - 1) + m + 1)
                        a.activation(lsq[:, m, :], streamc[:, m, n - 1, :], ACT.Square).then_inc(lsquare, 1)
                if conv:
                    a.wait_ge(cvar_mm, n + 2)
                    a.activation(cr0, ps[:, 5, :], ACT.Ln, bias=eps_now[:, 0:1]).then_inc(clog, 1)
                    a.wait_ge(clog, n + 2)
                    a.activation(cr0, cr0, ACT.Exp, scale=-0.5).then_inc(cexp, 1)
                    for c in range(GT):
                        a.wait_ge(cnorm, GT * (n + 1) + c + 1)
                        a.activation(sidec[:, c, n + 1, :], sidec[:, c, n + 1, :], ACT.Silu, scale=cln_g[:, c:c + 1],
                                     bias=cln_b[:, c:c + 1]).then_inc(csilu, 1)
                if norm:
                    rstd_guess(n, 7, lr0)
                    a.wait_ge(out_mm, KT * n)
                    a.wait_ge(h2_scaled, 6)
                    for m in range(KT):
                        a.wait_ge(lnorm, KT * (n - 1) + m + 1)
                        a.activation(side16[:, m, n - 1, 0], streamc[:, m, n - 1, :], ACT.Identity,
                                     scale=h2_scale[:, m:m + 1], bias=h2_bias[:, m:m + 1]).then_inc(h2_hi, 1)
                    for m in range(KT):
                        a.wait_ge(h2_ready, KT * (n - 1) + m + 1)
                        a.activation(streamc[:, m, n - 1, :], streamc[:, m, n - 1, :], ACT.Identity,
                                     scale=ln_g[1][:, m:m + 1], bias=ln_b[1][:, m:m + 1]).then_inc(x1_ready, 1)

            def rstd_guess(n, bank, lr0):
                a.wait_ge(var_mm, n)
                a.activation(lr0, ps[:, bank, :], ACT.Ln, bias=eps_now[:, 1:2]).then_inc(llog, 1)
                a.wait_ge(llog, n)
                a.activation(lr0, lr0, ACT.Exp, scale=-0.5).then_inc(lexp, 1)

            def square_pair(p, junk):
                for q, loaded in enumerate((land_u_loaded, land_g_loaded)):
                    a.wait_ge(loaded, 16 * (p + 1))
                    a.activation(junk[:, 0, q].bitcast(BF16), land[q], ACT.Square,
                                 accum_out=w_sumsq[:, q:q + 1]).then_inc(w_square, 1)

            def high_part(x16, q, scale, ready, at):
                a.wait_ge(ready, at)
                a.activation(x16[:, q, 0], land[q], ACT.Copy, scale=scale[:].bitcast(F32))
                a.activation(land[q], land[q], ACT.Copy, scale=scale[:].bitcast(F32)).then_inc(w_hi, 1)

            def ffn_bounds():
                a.wait_ge(prep_step, AFFINE_STEP)
                a.activation(bound_junk[:, 0], h2_scale[:], ACT.Square, scale=float(D) ** 0.5,
                             accum_out=h2_sumsq[:, 0:1]).then_inc(bound_sq, 1)
                a.activation(bound_junk[:, 1], h2_bias[:], ACT.Square, accum_out=h2_sumsq[:, 1:2]).then_inc(bound_sq, 1)
                a.wait_ge(unit_done, 2 * GT)
                square_pair(0, up16)

            chunk(-1, True, False, between=ffn_bounds)
            chunk(0, True, False)
            high_part(up16, 0, up_scale, up_scale_step, 3)
            chunk(1, True, True, later=False)
            with a.Fori(2, NC - 1) as n:
                chunk(n, True, True)
            chunk(NC - 1, False, True)
            chunk(NC, False, True)

            def evac_z(i, q, n):
                if n == 0:
                    a.wait_ge(up_scale_step, 5 * (2 * i + q // 2) + 5)
                a.wait_ge(up_mm, 4 * (4 * i + q) + n + 1)
                r = CH // GRID_W
                a.activation((zu, zg)[q % 2][:, 1 + n * r:1 + (n + 1) * r, 1:1 + GRID_W],
                             ps[:, n, :].rearrange("p (r c) -> p r c", c=GRID_W), ACT.Copy,
                             scale=up_inv[:, q // 2:q // 2 + 1].bitcast(F32)).then_inc(z_evac, 1)

            def first_tap(i, q):
                y, z, done = ((yu[q // 2], zu, first_u), (yg, zg, first_g))[q % 2]
                c_ = 10 * (q % 2)
                a.wait_ge(z_evac, 4 * (4 * i + q) + NC)
                a.activation(y.rearrange("p (r c) -> p r c", c=GRID_W), z[:, 0:ROWS, 0:GRID_W], ACT.Identity,
                             scale=tap_now[:, q // 2, c_:c_ + 1], bias=tap_now[:, q // 2, c_ + 9:c_ + 10])\
                 .then_inc(done, 1)

            def gelu(tile):
                a.wait_ge(conv_g, 8 * (tile + 1))
                a.activation(yg, yg, ACT.Gelu_apprx_tanh).then_inc(gelu_done, 1)

            def square_act(i, t, junk=None):
                a.wait_ge((act_a_done, act_b_done)[t], i + 1)
                if junk is None:
                    junk, src = act16[:, t, 0], act[t]
                else:
                    src = act[t].rearrange("p (two f) -> p two f", two=2)
                a.activation(junk.bitcast(BF16), src, ACT.Square,
                             accum_out=act_sumsq[:, t:t + 1]).then_inc(act_square, 1)

            def high_acts(i):
                a.wait_ge(act_scale_step, 5 * i + 3)
                for t in range(2):
                    a.activation(act16[:, t, 0], act[t], ACT.Copy, scale=act_scale[:].bitcast(F32)).then_inc(act_hi, 1)

            def ffn(i, first, last):
                if first:
                    a.wait_ge(zpads, 1)
                    a.wait_ge(cvar_mm, NC)
                else:
                    a.wait_ge(up_mm, 16 * i)
                high_part(up16, 1, up_scale, up_scale_step, 5 * 2 * i + 3)
                if not first:
                    a.wait_ge(conv_u, 8 * 2 * i)
                for n in range(3):
                    evac_z(i, 0, n)
                if not first:
                    gelu(2 * i - 1)
                evac_z(i, 0, 3)
                a.wait_ge(tap_a_loaded, 16 * (i + 1))
                if not first:
                    a.wait_ge(act_a_done, i)
                first_tap(i, 0)
                if first:
                    a.wait_ge(h2_lo, KT * NC)
                else:
                    a.wait_ge(conv_g, 8 * 2 * i)
                evac_z(i, 1, 0)
                if not first:
                    square_act(i - 1, 1)
                a.wait_ge(up_mm, 16 * i + 4)
                square_pair(3 * i + 1, up16)
                evac_z(i, 1, 1)
                if not first:
                    high_acts(i - 1)
                evac_z(i, 1, 2)
                high_part(up16, 0, up_scale, up_scale_step, 5 * (2 * i + 1) + 3)
                evac_z(i, 1, 3)
                if not first:
                    a.wait_ge(act_b_done, i)
                first_tap(i, 1)
                a.wait_ge(up_mm, 16 * i + 8)
                high_part(up16, 1, up_scale, up_scale_step, 5 * (2 * i + 1) + 3)
                if not first and not last:
                    a.wait_ge(down_mm, NG * i)
                if not last:
                    square_pair(3 * i + 2, down16)
                a.wait_ge(conv_u, 8 * (2 * i + 1))
                evac_z(i, 2, 0)
                gelu(2 * i)
                if not last:
                    high_part(down16, 0, down_scale, down_scale_step, 4 * i + 3)
                    high_part(down16, 1, down_scale, down_scale_step, 4 * i + 3)
                evac_z(i, 2, 1)
                evac_z(i, 2, 2)
                if not last:
                    square_act(i, 0)
                evac_z(i, 2, 3)
                a.wait_ge(tap_b_loaded, 16 * (i + 1))
                if not first:
                    a.wait_ge(act_lo, 2 * i)
                first_tap(i, 2)
                if not last:
                    a.wait_ge(up_mm, 16 * i + 12)
                    square_pair(3 * i + 3, up16)
                evac_z(i, 3, 0)
                if not last:
                    high_part(up16, 0, up_scale, up_scale_step, 5 * (2 * i + 2) + 3)
                for n in range(1, NC):
                    evac_z(i, 3, n)
                if last:
                    a.wait_ge(act_a_done, i + 1)
                first_tap(i, 3)

            ffn(0, True, False)
            with a.Fori(1, NI - 1) as i:
                ffn(i, False, False)
            ffn(NI - 1, False, True)
            a.wait_ge(up_mm, 16 * NI)
            square_pair(3 * NI - 1, up16)
            square_act(NI - 1, 0, up16[:, 1])
            gelu(2 * NI - 1)
            a.wait_ge(down_mm, NG * (NI - 1))
            high_part(down16, 0, down_scale, down_scale_step, 4 * NI - 1)
            a.wait_ge(act_square, 2 * NI - 1)
            square_act(NI - 1, 1, up16[:, 1])
            high_part(down16, 1, down_scale, down_scale_step, 4 * NI - 1)
            high_acts(NI - 1)

            for n in range(NC):
                a.wait_ge(var_mm, NC + n)
                for m in range(KT):
                    a.wait_ge(lsub, KT * (NC + n) + m + 1)
                    a.activation(lsq2[:, m, :], streamc[:, m, n, :], ACT.Square).then_inc(lsquare, 1)
                rstd_guess(NC + n + 1, 2 * (n % 2) + 1, ln2_scratch[3])
                for m in range(KT):
                    a.wait_ge(lnorm, KT * (NC + n) + m + 1)
                    a.activation(streamc[:, m, n, :], streamc[:, m, n, :], ACT.Identity,
                                 scale=ln_g[2][:, m:m + 1], bias=ln_b[2][:, m:m + 1]).then_inc(out_ready, 1)

        @block.vector
        def _(v):
            def scale_of(mean_square, top, scale, inv, done, at):
                v.tensor_scalar(half_bits[:], mean_square.bitcast(I32), 1, None, ALU.logical_shift_right)\
                 .then_inc(done, 1)
                v.wait_ge(done, at + 1)
                v.tensor_scalar(scale[:], half_bits[:], -1.0, float(top), ALU.mult, ALU.add).then_inc(done, 1)
                v.wait_ge(done, at + 2)
                v.tensor_scalar(scale[:], scale[:], EXPONENT, None, ALU.bitwise_and).then_inc(done, 1)
                v.wait_ge(done, at + 3)
                v.tensor_scalar(inv, scale[:], -1.0, float(INVERSE), ALU.mult, ALU.add).then_inc(done, 1)
                v.wait_ge(done, at + 4)

            def in_scales(u, j):
                w_ = 4 * j + TILES.index(u)
                v.wait_ge(in_sum_mm, w_ + 1)
                scale_of(ps[:, 7, 0:1], SCALE_TOP, in_scale, in_inv_w[:], in_scale_step, 5 * w_)

            def in_undo(u):
                v.tensor_scalar(in_inv[:, TILES.index(u), :], h_inv[:].bitcast(F32), in_inv_w[:].bitcast(F32), None,
                                ALU.mult).then_inc(in_scale_step, 1)

            def mod_bounds(cc):
                v.wait_ge(mod_sum_mm, cc + 1)
                v.tensor_scalar(mod_bound[:, 0:1], ps[:, 4, 0:1], 1.0, None, ALU.mult).then_inc(mod_bound_step, 1)
                v.tensor_scalar(mod_bound[:, 1:2], ps[:, 4, 1:2], float(D), None, ALU.mult).then_inc(mod_bound_step, 1)
                v.wait_ge(mod_bound_step, 2 * cc + 2)

            def h_scales(n):
                v.wait_ge(x_sum_mm, n + 1)
                v.tensor_scalar(h_bound[:], ps[:, 5 + n % 2, 0:1], mod_bound[:, 1:2], mod_bound[:, 0:1],
                                ALU.mult, ALU.add).then_inc(h_scale_step, 1)
                v.wait_ge(h_scale_step, 6 * n + 1)
                scale_of(h_bound[:], SCALE_TOP_DOUBLE, h_pow, h_inv[:, n:n + 1], h_scale_step, 6 * n + 1)
                v.tensor_scalar(mod_of[:, n], mod0[:, :, :, n // NC], h_pow[:].bitcast(F32), None, ALU.mult)\
                 .then_inc(h_scale_step, 1)
                v.wait_ge(h_scale_step, 6 * (n + 1))

            def h_split(n):
                f = CH if n < NC else TC
                for k in range(KT + 2):
                    if k < KT:
                        if KT * n + k > 3:
                            v.wait_ge(h_lo, KT * n + k - 3)
                        src = streamc[:, k, n, :] if n < NC else h_ctx[:, k, :]
                        v.tensor_scalar(h_tmp[k % 4][:, 0:f], src, mod_of[:, n, 1, k:k + 1], mod_of[:, n, 0, k:k + 1],
                                        ALU.mult, ALU.add).then_inc(h_tmp_ready, 1)
                    if k > 1:
                        dst = stream16[:, k - 2, n] if n < NC else ctx16[:, k - 2]
                        v.wait_ge(h_hi, KT * n + k - 1)
                        v.tensor_tensor(dst[:, 1], h_tmp[(k - 2) % 4][:, 0:f], dst[:, 0], ALU.subtract)\
                         .then_inc(h_lo, 1)

            v.wait_ge(par_loaded, 16)
            lam = pj[:, :, PJ_TH:PJ_TH + 2]
            v.tensor_scalar(sp[:, 4], lam, -1.0, None, ALU.mult).then_inc(prep_step, 1)
            v.wait_ge(prep_step, 1)
            v.tensor_tensor(sp[:, 0], sp[:, 4], lam, ALU.max).then_inc(prep, 1)
            v.tensor_scalar(pj[:, :, PJ_GB:PJ_GB + 4], pj[:, :, PJ_GB:PJ_GB + 4], 0.5, None, ALU.mult)\
             .then_inc(prep_step, 1)
            v.memset(eps_now[:, 0:1], EPS).then_inc(prep_step, 1)
            v.memset(eps_now[:, 1:2], EPS / (ALPHA * ALPHA)).then_inc(prep_step, 1)
            c = 4

            def link(i):
                nonlocal c
                c += 1
                i.then_inc(prep_step, 1)
                v.wait_ge(prep_step, c)

            v.wait_ge(prep, 2)
            e, r, r2, acc, neg = (sp[:, i] for i in (1, 0, 2, 3, 4))
            link(v.tensor_scalar(r2, e, 2.0, None, ALU.add))
            link(v.reciprocal(acc, r2))
            link(v.tensor_tensor(r, e, acc, ALU.mult))
            link(v.tensor_tensor(r2, r, r, ALU.mult))
            link(v.tensor_scalar(acc, r2, 1.0 / 17, 1.0 / 15, ALU.mult, ALU.add))
            for odd in (13, 11, 9, 7, 5, 3, 1):
                link(v.tensor_tensor(acc, acc, r2, ALU.mult))
                link(v.tensor_scalar(acc, acc, 1.0 / odd, None, ALU.add))
            link(v.tensor_tensor(acc, acc, r, ALU.mult))
            link(v.tensor_scalar(neg, neg, 0.0, 0.5, ALU.max, ALU.mult))
            link(v.tensor_tensor(acc, acc, neg, ALU.add))
            link(v.tensor_scalar(pj[:, :, PJ_EX:PJ_EX + 2], acc, -8.0, None, ALU.mult))
            link(v.tensor_scalar(pj[:, :, PJ_TH:PJ_TH + 2], acc, 4.0, None, ALU.mult))

            raw = mod_raw[:].rearrange("p (g k) c -> p g k c", k=KT)
            v.wait_ge(silu_done, 1)
            for t in range(2 * KT):
                if t % 4 == 0:
                    v.wait_ge(ada_loaded[t // 4], 16)
                if t > 3:
                    v.wait_ge(ada_c, t - 3)
                v.scalar_tensor_tensor(out=ada_junk[t % 4], in0=ada_w[:, t, :], scalar=1.0, in1=silu_rows[:, 0, :],
                                       op0=ALU.mult, op1=ALU.mult, accum_out=mod_raw[:, t, 0:1]).then_inc(ada_c, 1)
            v.wait_ge(ada_c, 2 * KT)
            link(v.tensor_tensor(mod0[:, :, :, 0], raw[:, :, :, 0], b_ada[:, 0:2, :], ALU.add))
            v.tensor_scalar(mod0[:, 1, :, 0], mod0[:, 1, :, 0], 1.0, None, ALU.add).then_inc(mod_done, 1)
            v.wait_ge(mod_done, 1)
            mod_bounds(0)
            in_scales("cg", 0)
            for n in range(NC):
                h_scales(n)
                h_split(n)
                if n == NC - 2:
                    v.wait_ge(ada_ctx_sum, 2 * KT)
                    link(v.tensor_tensor(mod0[:, :, :, 1], raw[:, :, :, 1], b_ada[:, 0:2, :], ALU.add))
                    v.tensor_scalar(mod0[:, 1, :, 1], mod0[:, 1, :, 1], 1.0, None, ALU.add).then_inc(ctx_mod_done, 1)
                    v.wait_ge(ctx_mod_done, 1)
            mod_bounds(1)
            h_scales(NC)
            in_undo("cg")
            in_scales("cv", 0)
            in_undo("cv")
            h_split(NC)

            def conv_taps(j, lo, hi, pj_now=pj_now):
                for k in range(lo, hi):
                    if k == 0:
                        v.wait_ge(jp_ready, j + 1)
                        v.wait_ge(cv_evac, NC * (j + 1))
                        i = v.tensor_scalar(side[:, j, :], upad[:, 0:T], pj_now[:, 0:1],
                                            pj_now[:, PJ_CONVB:PJ_CONVB + 1], ALU.mult, ALU.add)
                    else:
                        v.wait_ge(conv_tap, CONV_K * j + k)
                        i = v.scalar_tensor_tensor(out=side[:, j, :], in0=upad[:, k:k + T], scalar=pj_now[:, k:k + 1],
                                                   in1=side[:, j, :], op0=ALU.mult, op1=ALU.add)
                    i.then_inc(conv_tap, 1)

            def rg_conv(j):
                for k in range(1, RG_K):
                    w = pj_now[:, PJ_RG + k:PJ_RG + k + 1]
                    for half, (dst, src) in enumerate(((xr[:, TC:TC + T], rxp[:, LAT0 + k:LAT0 + k + T]),
                                                       (xr[:, 0:TC], rxp[:, k:k + TC]))):
                        if k == 1:
                            v.wait_ge(rg_first, 2 * j + half + 1)
                        else:
                            v.wait_ge(rg_tap, 6 * j + 2 * (k - 2) + half + 1)
                        v.scalar_tensor_tensor(out=dst, in0=src, scalar=w, in1=dst, op0=ALU.mult, op1=ALU.add)\
                         .then_inc(rg_tap, 1)

            def unit(j, d, between=None):
                q = 2 * j + d
                v.wait_ge(rg_act, 3 * (q + 1))
                v.scalar_tensor_tensor(out=sq, in0=tr, scalar=1.0, in1=sq, op0=ALU.add, op1=ALU.mult)\
                 .then_inc(unit_step, 1)
                v.wait_ge(unit_step, 3 * q + 1)
                v.wait_ge(ti_step, 2 * (q + 1))
                v.tensor_tensor(sq, sq, ti, ALU.mult).then_inc(unit_step, 1)
                v.wait_ge(unit_step, 3 * q + 2)
                back = slice(None, None, -1)
                if d == 0:
                    v.tensor_tensor_scan(out=ti[:, 0:TC], data0=tr[:, 0:TC], data1=sq[:, 0:TC], initial=0.0,
                                         op0=ALU.mult, op1=ALU.add).then_inc(unit_step, 1)
                    v.wait_ge(unit_step, 3 * q + 3)
                    v.tensor_tensor_scan(out=side[:, GT + j, :], data0=tr[:, TC:], data1=sq[:, TC:],
                                         initial=ti[:, TC - 1:TC], op0=ALU.mult, op1=ALU.add).then_inc(unit_done, 1)
                else:
                    v.tensor_tensor_scan(out=ti[:, 0:TC][:, back], data0=tr[:, 0:TC][:, back],
                                         data1=sq[:, 0:TC][:, back], initial=0.0,
                                         op0=ALU.mult, op1=ALU.add).then_inc(unit_step, 1)
                    v.wait_ge(unit_step, 3 * q + 3)
                    v.tensor_tensor_scan(out=ti[:, TC:][:, back], data0=tr[:, TC:][:, back],
                                         data1=sq[:, TC:][:, back], initial=ti[:, 0:1],
                                         op0=ALU.mult, op1=ALU.add).then_inc(scan_step, 1)
                    if between is not None:
                        between()
                    v.wait_ge(scan_step, j + 1)
                    v.wait_ge(unit_done, 2 * j + 1)
                    v.tensor_tensor(side[:, GT + j, :], side[:, GT + j, :], ti[:, TC:], ALU.add)\
                     .then_inc(mix_step, 1)
                    v.wait_ge(rg_evac, NC * (j + 1))
                    v.wait_ge(mix_step, j + 1)
                    v.tensor_tensor(side[:, GT + j, :], side[:, GT + j, :], gelu_rg, ALU.mult)\
                     .then_inc(unit_done, 1)

            def leftover(j, scales):
                if scales:
                    conv_taps(j, TAPS_END, TAPS_UNIT)
                    in_scales("cv", j + 1)
                    in_undo("cv")
                unit(j, 0)
                v.tensor_copy(pj_prev[:], pj_now[:]).then_inc(jp_kept, 1)
                v.wait_ge(ada_sum_done, KT * (j + 1))
                v.tensor_tensor(mods[:, j, :], ada_sum[:], b_ada[:, 2 + j, :], ALU.add).then_inc(mod_done, 1)
                v.wait_ge(jp_kept, j + 1)
                if scales:
                    conv_taps(j, TAPS_UNIT, TAPS_RX, pj_prev)
                    in_scales("rx", j + 1)
                    in_undo("rx")
                    conv_taps(j, TAPS_RX, CONV_K, pj_prev)
                else:
                    conv_taps(j, TAPS_END, CONV_K - TAPS_SHARED, pj_prev)

            def mixer(j, first, last):
                if not first:
                    leftover(j - 1, True)
                    v.wait_ge(conv_tap, CONV_K * j)
                v.tensor_copy(pj_now[:], pj[:, j, :]).then_inc(jp_ready, 1)
                for n in range(NC):
                    v.wait_ge(cg_evac, NC * j + n + 1)
                    v.wait_ge(cv_mm, NC * j + n + 1)
                    if n == 0:
                        v.wait_ge(in_scale_step, 5 * (4 * j + 1) + 5)
                    v.scalar_tensor_tensor(out=upad[:, PAD + n * CH:PAD + (n + 1) * CH], in0=ps[:, n, :],
                                           scalar=in_inv[:, 1, n:n + 1], in1=rx_lat[:, n * CH:(n + 1) * CH],
                                           op0=ALU.mult, op1=ALU.mult).then_inc(cv_evac, 1)
                    if first and n == 1:
                        in_scales("rx", j)
                        in_undo("rx")
                conv_taps(j, 0, TAPS_RG)
                in_scales("rg", j)
                in_undo("rg")
                if not first:
                    unit(j - 1, 1)
                conv_taps(j, TAPS_RG, TAPS_CONV)
                rg_conv(j)
                if not last:
                    in_scales("cg", j + 1)
                    in_undo("cg")
                conv_taps(j, TAPS_CONV, TAPS_END)

            v.wait_ge(pads, 5)
            mixer(0, True, False)
            with v.Fori(1, GT - 1) as j:
                mixer(j, False, False)
            mixer(GT - 1, False, True)
            leftover(GT - 1, False)

            def add_shared_taps():
                v.wait_ge(shared_tap_added, TAPS_SHARED - 1)
                v.wait_ge(conv_tap, CONV_TAPS_ALL - 1)
                v.tensor_tensor(side[:, GT - 1, :], side[:, GT - 1, :], shared_sum, ALU.add).then_inc(conv_tap, 1)

            unit(GT - 1, 1, between=add_shared_taps)

            v.wait_ge(mod_done, GT + 1)
            link(v.tensor_scalar(g1s[:], mods[:, 0, :], 1.0 / ALPHA, None, ALU.mult))
            link(v.tensor_scalar(g2s[:], mods[:, 3, :], 1.0 / ALPHA, None, ALU.mult))
            link(v.tensor_scalar(mods[:, 2, :], mods[:, 2, :], 1.0, None, ALU.add))
            link(v.tensor_tensor(h2_scale[:], ln_g[1], mods[:, 2, :], ALU.mult))
            link(v.tensor_tensor(h2_bias[:], ln_b[1], mods[:, 2, :], ALU.mult))
            link(v.tensor_tensor(h2_bias[:], h2_bias[:], mods[:, 1, :], ALU.add))
            assert c == AFFINE_STEP, c

            def up_scales(half, nth_, p, col=0):
                v.wait_ge(w_sum_mm, p + 1)
                inv = up_inv[:, half:half + 1]
                scale_of(ps[:, 7, col:col + 1], SCALE_TOP, up_scale, inv, up_scale_step, 5 * nth_)
                v.tensor_scalar(inv.bitcast(F32), inv.bitcast(F32), h2_inv[:].bitcast(F32), None, ALU.mult)\
                 .then_inc(up_scale_step, 1)


            def newton(var, eps, r0, r, done, base, nth_guess, guess):
                v.wait_ge(guess, nth_guess)
                v.scalar_tensor_tensor(out=r, in0=var, scalar=eps, in1=r0, op0=ALU.add, op1=ALU.mult).then_inc(done, 1)
                v.wait_ge(done, base + 1)
                v.tensor_tensor(r, r, r0, ALU.mult).then_inc(done, 1)
                v.wait_ge(done, base + 2)
                v.tensor_scalar(r, r, -0.5, 1.5, ALU.mult, ALU.add).then_inc(done, 1)
                v.wait_ge(done, base + 3)
                v.tensor_tensor(r, r, r0, ALU.mult).then_inc(done, 1)
                v.wait_ge(done, base + 4)

            def ln_sub(q, n, bank):
                v.wait_ge(mean_mm, q + 1)
                for m in range(KT):
                    v.tensor_tensor(streamc[:, m, n, :], streamc[:, m, n, :], ps[:, bank, :], ALU.subtract)\
                     .then_inc(lsub, 1)

            def ln_mul(q, n, bank, lr0=lr0, lr=lr):
                newton(ps[:, bank, :], eps_now[:, 1:2], lr0, lr, lnewton, 4 * q, q + 1, lexp)
                for m in range(KT):
                    v.tensor_tensor(streamc[:, m, n, :], streamc[:, m, n, :], lr, ALU.mult).then_inc(lnorm, 1)

            def h2_low(n):
                for m in range(KT + 1):
                    if m < KT:
                        v.wait_ge(lnorm, KT * n + m + 1)
                        if m > 1:
                            v.wait_ge(h2_lo, KT * n + m - 1)
                        v.tensor_scalar(h2_f32[m % 2], streamc[:, m, n, :], h2_scale[:, m:m + 1], h2_bias[:, m:m + 1],
                                        ALU.mult, ALU.add).then_inc(h2_ready, 1)
                    if m > 0:
                        v.wait_ge(h2_ready, KT * n + m)
                        v.wait_ge(h2_hi, KT * n + m)
                        v.tensor_tensor(side16[:, m - 1, n, 1], h2_f32[(m - 1) % 2], side16[:, m - 1, n, 0],
                                        ALU.subtract).then_inc(h2_lo, 1)
                v.wait_ge(h2_lo, KT * (n + 1))

            def chunk(n, conv, out, norm, first=False, between=None):
                for m in range(KT):
                    if out:
                        if m == 0 and first:
                            for i in range(NC):
                                v.wait_ge(xr_loaded[i], 16)
                        v.wait_ge(out_mm, KT * n + m + 1)
                        v.scalar_tensor_tensor(out=streamc[:, m, n, :], in0=ps[:, m % 4, :], scalar=g1s[:, m:m + 1],
                                               in1=streamc[:, m, n, :], op0=ALU.mult, op1=ALU.add)\
                         .then_inc(out_evac, 1)
                    if m == 0 and conv:
                        v.wait_ge(cmean_mm, n + 2)
                        for c_ in range(GT):
                            v.tensor_tensor(sidec[:, c_, n + 1, :], sidec[:, c_, n + 1, :], ps[:, 4, :], ALU.subtract)\
                             .then_inc(csub, 1)
                    if m == 1 and norm:
                        ln_sub(n - 1, n - 1, 6)
                    if m == 3 and conv:
                        if between is not None:
                            between()
                        newton(ps[:, 5, :], eps_now[:, 0:1], cr0, cr, cnewton, 4 * (n + 1), n + 2, cexp)
                        for c_ in range(GT):
                            v.tensor_tensor(sidec[:, c_, n + 1, :], sidec[:, c_, n + 1, :], cr, ALU.mult)\
                             .then_inc(cnorm, 1)
                    if m == 5 and norm:
                        ln_mul(n - 1, n - 1, 7)
                if norm:
                    h2_low(n - 1)

            def ffn_scales():
                v.wait_ge(bound_mm, 1)
                scale_of(ps[:, 7, 0:1], SCALE_TOP_DOUBLE, h2_pow, h2_inv[:], h2_scaled, 0)
                for affine in (h2_scale, h2_bias):
                    v.tensor_scalar(affine[:], affine[:], h2_pow[:].bitcast(F32), None, ALU.mult).then_inc(h2_scaled, 1)
                up_scales(0, 0, 0, col=1)

            chunk(-1, True, False, False, between=ffn_scales)
            chunk(0, True, True, False, first=True)
            with v.Fori(1, NC - 1) as n:
                chunk(n, True, True, True)
            chunk(NC - 1, False, True, True)
            chunk(NC, False, False, True)

            def tap3(i, q, k):
                y, z, first_done, done = ((yu[q // 2], zu, first_u, conv_u), (yg, zg, first_g, conv_g))[q % 2]
                tile = 2 * i + q // 2
                dr, dc = k // 3, k % 3
                c_ = 10 * (q % 2) + k
                y3 = y.rearrange("p (r c) -> p r c", c=GRID_W)
                if k == 1:
                    v.wait_ge(first_done, tile + 1)
                else:
                    v.wait_ge(done, 8 * tile + k - 1)
                v.scalar_tensor_tensor(out=y3, in0=z[:, dr:dr + ROWS, dc:dc + GRID_W],
                                       scalar=tap_now[:, q // 2, c_:c_ + 1],
                                       in1=y3, op0=ALU.mult, op1=ALU.add).then_inc(done, 1)

            def gate(i, t):
                v.wait_ge(gelu_done, 2 * i + t + 1)
                v.wait_ge(conv_u, 8 * (2 * i + t + 1))
                v.tensor_tensor(act[t], yu[t], yg, ALU.mult).then_inc((act_a_done, act_b_done)[t], 1)

            def act_scales(i):
                v.wait_ge(act_sum_mm, i + 1)
                scale_of(ps[:, 7, 2:3], SCALE_TOP, act_scale, act_inv[:], act_scale_step, 5 * i)
                v.tensor_scalar(g2_now[:], g2s[:], act_inv[:].bitcast(F32), down_inv[:].bitcast(F32),
                                ALU.mult, ALU.mult).then_inc(act_scale_step, 1)

            def act_low(i, t):
                v.wait_ge(act_hi, 2 * i + t + 1)
                v.scalar_tensor_tensor(out=act16[:, t, 1], in0=act[t], scalar=act_scale[:].bitcast(F32),
                                       in1=act16[:, t, 0], op0=ALU.mult, op1=ALU.subtract).then_inc(act_lo, 1)

            def add_down(i, g):
                n, m = g // KT, g % KT
                if g == 0:
                    v.wait_ge(down_bank_free, NG * i + DB)
                    v.wait_ge(act_scale_step, 5 * (i + 1))
                v.wait_ge(down_mm, NG * i + g + 1)
                v.scalar_tensor_tensor(out=streamc[:, m, n, :], in0=ps[:, 4 + g % DB, :], scalar=g2_now[:, m:m + 1],
                                       in1=streamc[:, m, n, :], op0=ALU.mult, op1=ALU.add)\
                 .then_inc(down_bank_free, 1)

            def down_scales(i):
                v.wait_ge(w_sum_mm, 3 * i + 3)
                scale_of(ps[:, 7, 1:2], SCALE_TOP, down_scale, down_inv[:], down_scale_step, 4 * i)

            def ffn(i, first, last):
                if not first:
                    for k in range(1, 9):
                        tap3(i - 1, 3, k)
                    gate(i - 1, 1)
                for k in range(1, 6):
                    tap3(i, 0, k)
                    if k == 2 and not first:
                        act_scales(i - 1)
                    if k == 3 and not first:
                        act_low(i - 1, 0)
                        act_low(i - 1, 1)
                up_scales(1, 2 * i + 1, 3 * i + 1)
                rest = [(0, k) for k in range(6, 9)] + [(1, k) for k in range(1, 9)]
                if not (first or last):
                    for g in range(NG):
                        add_down(i - 1, g)
                        if g % 4 == 1:
                            tap3(i, *rest.pop(0))
                for q, k in rest:
                    tap3(i, q, k)
                if first:
                    v.wait_ge(x1_ready, KT * NC)
                    v.tensor_copy(g2_now[:], g2s[:]).then_inc(down_bank_free, DB)
                if not last:
                    down_scales(i)
                gate(i, 0)
                for k in range(1, 9):
                    tap3(i, 2, k)
                    if k == 2 and not last:
                        up_scales(0, 2 * i + 2, 3 * i + 3)
                if last:
                    for g in range(NG):
                        add_down(i - 1, g)
                        if g % 4 == 1:
                            tap3(i, 3, g // 4 + 1)
                    down_scales(i)

            ffn(0, True, False)
            with v.Fori(1, NI - 1) as i:
                ffn(i, False, False)
            ffn(NI - 1, False, True)
            gate(NI - 1, 1)
            act_scales(NI - 1)
            act_low(NI - 1, 0)
            act_low(NI - 1, 1)
            for n in range(NC + 1):
                if n < NC:
                    for m in range(KT):
                        add_down(NI - 1, n * KT + m)
                if n > 0:
                    ln_mul(NC + n - 1, n - 1, 2 * ((n - 1) % 2) + 1, *ln2_scratch[3:])
                if n < NC:
                    ln_sub(NC + n, n, 2 * (n % 2))

        @block.gpsimd
        def _(g):
            g.memset(mean_of_group[:], 1.0 / CW).then_inc(consts, 1)
            g.memset(mean_of_model[:], 1.0 / D).then_inc(consts, 1)
            g.memset(upad[:, 0:PAD], 0.0).then_inc(pads, 1)
            g.memset(upad[:, PAD + T:], 0.0).then_inc(pads, 1)
            g.memset(rxp[:, 0:RG_L], 0.0).then_inc(pads, 1)
            g.memset(rxp[:, RG_L + TC:LAT0 + RG_L], 0.0).then_inc(pads, 1)
            g.memset(rxp[:, LAT0 + RG_L + T:], 0.0).then_inc(pads, 1)

            def in_low(u, j):
                w_ = TILES.index(u)
                g.wait_ge(in_hi, 4 * j + w_ + 1)
                g.tensor_tensor(in16[w_ % 2][:, 1], slot[SLOT[u]], in16[w_ % 2][:, 0], ALU.subtract).then_inc(in_lo, 1)

            g.wait_ge(silu_done, 1)
            for t in range(2 * KT):
                if t % 4 == 0:
                    g.wait_ge(ada_loaded[t // 4], 16)
                if t > 1:
                    g.wait_ge(ada_ctx_sum, t - 1)
                if t == KT + 3:
                    in_low("cg", 0)
                g.tensor_tensor(ada_prod[t % 2], ada_w[:, t, :], silu_rows[:, 1, :], ALU.mult).then_inc(ada_ctx_prod, 1)

            def ada_products(j, lo, hi):
                for t in range(lo, hi):
                    u = f"ada{t}"
                    g.wait_ge(*landed(u, j))
                    g.tensor_tensor(slot[SLOT[u]], slot[SLOT[u]], silu_rows[:, 0, :], ALU.mult).then_inc(ada_prod_done, 1)

            def input_gate(j, d):
                q = 2 * j + d
                g.wait_ge(gate_evac, 20 * j + 10 * d + 10)
                g.tensor_tensor(ti, ti, xr, ALU.mult).then_inc(ti_step, 1)
                g.wait_ge(ti_step, 2 * q + 1)
                g.tensor_tensor(ti, ti, xr, ALU.add).then_inc(ti_step, 1)

            def mixer(j, last, first=False):
                if not first:
                    input_gate(j - 1, 0)
                in_low("cv", j)
                if not first:
                    input_gate(j - 1, 1)
                in_low("rx", j)
                ada_products(j, 0, 3)
                in_low("rg", j)
                ada_products(j, 3, 6)
                if not last:
                    in_low("cg", j + 1)
                ada_products(j, 6, KT)

            mixer(0, False, True)
            with g.Fori(1, GT - 1) as j:
                mixer(j, False)
            mixer(GT - 1, True)

            def shared_adds(lo, hi):
                for i in range(lo, hi):
                    g.wait_ge(shared_tap_made, i + 1)
                    if i > 1:
                        g.wait_ge(shared_tap_added, i - 1)
                    g.tensor_tensor(shared_sum, shared_sum, shared_tap[i % 2], ALU.add).then_inc(shared_tap_added, 1)

            input_gate(GT - 1, 0)
            shared_adds(1, 4)
            input_gate(GT - 1, 1)
            shared_adds(4, TAPS_SHARED)

            def sums(q, n, src_ready, base, first=False, scratch=ln1_scratch, squares=True):
                lsq, lsum, lsqs = scratch[:3]
                if not first:
                    g.wait_ge(mean_mm, q)
                for m in range(1, KT):
                    g.wait_ge(src_ready, base + KT * n + m + 1)
                    if m > 1:
                        g.wait_ge(psum_step, (KT - 1) * q + m - 1)
                    a = streamc[:, 0, n, :] if m == 1 else lsum
                    i = g.tensor_tensor(lsum, a, streamc[:, m, n, :], ALU.add)
                    i.then_inc(psum_step, 1)
                if not squares:
                    return
                if not first:
                    g.wait_ge(var_mm, q)
                for m in range(1, KT):
                    g.wait_ge(lsquare, KT * q + m + 1)
                    if m > 1:
                        g.wait_ge(qsum_step, (KT - 1) * q + m - 1)
                    a = lsq[:, 0, :] if m == 1 else lsqs
                    i = g.tensor_tensor(lsqs, a, lsq[:, m, :], ALU.add)
                    i.then_inc(qsum_step, 1)

            def low_part(x16, q, nth_):
                g.wait_ge(w_hi, nth_ + 1)
                g.tensor_tensor(x16[:, q, 1], land[q], x16[:, q, 0], ALU.subtract).then_inc(w_lo, 1)

            g.wait_ge(unit_done, 2 * GT)
            sums(0, 0, out_evac, 0, first=True)
            low_part(up16, 0, 0)
            with g.Fori(1, NC - 1) as n:
                sums(n, n, out_evac, 0)
            sums(NC - 1, NC - 1, out_evac, 0, squares=False)
            g.wait_ge(out_mm, KT * NC)
            for z in (zu, zg):
                g.memset(z[:, 0, :], 0.0)
                g.memset(z[:, ZR - 1, :], 0.0)
                g.memset(z[:, 1:ZR - 1, 0:1], 0.0)
                i = g.memset(z[:, 1:ZR - 1, ZC - 1:ZC], 0.0)
            i.then_inc(zpads, 1)

            def ffn(i, first, last):
                low_part(up16, 1, 6 * i + 1)
                low_part(up16, 0, 6 * i + 2)
                low_part(up16, 1, 6 * i + 3)
                low_part(down16, 0, 6 * i + 4)
                low_part(down16, 1, 6 * i + 5)
                if not last:
                    low_part(up16, 0, 6 * i + 6)

            ffn(0, True, False)
            with g.Fori(1, NI - 1) as i:
                ffn(i, False, False)
            ffn(NI - 1, False, True)
            g.wait_ge(conv_g, 8 * 2 * NI)
            for n in range(NC):
                sums(NC + n, n, down_bank_free, NG * (NI - 1) + DB, scratch=ln2_scratch, squares=False)


def _tiles(w, rows, cols):
    return w.reshape(rows, P, cols, P).transpose(2, 1, 0, 3).reshape(cols, P, rows * P)


def _col(v):
    return v.reshape(-1, P).T


def kernel(x, c, ctx, c_ctx, w_ada, b_ada, w_in, conv_w, conv_b, conv_ln_g, conv_ln_b, rg_conv_w, rg_conv_b,
           rg_wa, rg_ba, rg_wx, rg_bx, rg_lambda, w_out, ln1_g, ln1_b, ffn_up, ffn_dw, ffn_dw_b, ffn_down,
           ln2_g, ln2_b):
    import concourse.bacc as bacc
    import numpy as np
    from concourse.bass_utils import run_bass_kernel_spmd

    A = np.asarray
    x, c, ctx, c_ctx = A(x), A(c), A(ctx), A(c_ctx)
    par = np.zeros((P, NPAR), x.dtype)

    def put(name, a):
        at, n = COLS[name]
        par[:, at:at + n] = np.ascontiguousarray(a).reshape(P, n)

    put("b_ada", _col(A(b_ada)[0]))
    pj = np.zeros((P, GT, PJ_N), x.dtype)
    pj[:, :, PJ_CONV:PJ_CONVB] = A(conv_w)[0].reshape(CONV_K, GT, P).transpose(2, 1, 0)
    pj[:, :, PJ_CONVB] = _col(A(conv_b)[0])
    pj[:, :, PJ_RG:PJ_RGB] = A(rg_conv_w)[0].reshape(RG_K, GT, P).transpose(2, 1, 0)
    pj[:, :, PJ_RGB] = _col(A(rg_conv_b)[0])
    for d in range(2):
        pj[:, :, PJ_GB + 2 * d] = _col(A(rg_ba)[0, d])
        pj[:, :, PJ_GB + 2 * d + 1] = _col(A(rg_bx)[0, d])
        pj[:, :, PJ_TH + d] = _col(A(rg_lambda)[0, d])
    put("pj", pj)
    for name, a in (("cln_g", conv_ln_g), ("cln_b", conv_ln_b), ("ln1_g", ln1_g), ("ln1_b", ln1_b),
                    ("ln2_g", ln2_g), ("ln2_b", ln2_b)):
        put(name, _col(A(a)[0]))
    taps = np.zeros((P, NP, 2, 10), x.dtype)
    taps[:, :, :, 0:9] = A(ffn_dw)[0].reshape(9, 2, NP, P).transpose(3, 2, 1, 0)
    taps[:, :, :, 9] = A(ffn_dw_b)[0].reshape(2, NP, P).transpose(2, 1, 0)

    gate = np.zeros((GT, P, 4, P), x.dtype)
    for d in range(2):
        for g, w in enumerate((A(rg_wa), A(rg_wx))):
            w2 = w[0, d].reshape(GT, 2, 64, 64)
            for h in range(2):
                gate[:, 64 * h:64 * h + 64, 2 * d + g, 64 * h:64 * h + 64] = w2[:, h]

    arrays = {
        "xT": x[0].T.reshape(KT, P, T),
        "ctxT": ctx[0].T.reshape(KT, P, TC).transpose(1, 0, 2),
        "par": par,
        "w_ada": A(w_ada)[0].T.reshape(ADA_G * KT, P, D),
        "w_in": _tiles(A(w_in)[0], KT, 4 * GT),
        "w_gate": gate,
        "w_out": _tiles(A(w_out)[0], KT, KT),
        "w_up": _tiles(A(ffn_up)[0], KT, 2 * NP),
        "w_down": A(ffn_down)[0].reshape(NP, P, D),
        "ffn_taps": taps.transpose(1, 0, 2, 3).reshape(NP, P, TAP_N),
        "c_rows": np.broadcast_to(np.stack([c[0], c_ctx]), (P, 2, D)),
    }
    nc = bacc.Bacc("TRN2", target_bir_lowering=False, num_devices=1, dynamic_dma_scratch_size=64)
    feeds, args = {}, []
    for name, a in arrays.items():
        feeds[name] = np.ascontiguousarray(a)
        args.append(nc.dram_tensor(name, a.shape, F32, kind="ExternalInput").ap())
    args.append(nc.dram_tensor("outT", (KT, P, T), F32, kind="ExternalOutput").ap())
    hybrid_layer(nc, *args)
    r = run_bass_kernel_spmd(nc, [feeds], core_ids=[0])
    out = np.asarray(r.results[0]["outT"]).reshape(D, T).T
    return np.ascontiguousarray(out).reshape(1, T, D)
```
